# Optimizing a Trainium2 kernel written in Bass

```python
import math
import jax, jax.numpy as jnp
from jax import lax
import numpy as np

D_MODEL = 1024
BATCH = 1
SEQ = 512
DEPTH = 2

CHUNK = 64
N_META = 16
N_A_LAYERS = DEPTH // 2
N_B_LAYERS = DEPTH - N_A_LAYERS
D_RNN = 3 * D_MODEL // 2
N_LRU_BLOCKS = 16
LRU_BLOCK = D_RNN // N_LRU_BLOCKS
LRU_C = 8.0
CONV_A_WIDTH = 4
N_FOX_HEADS = 16
FOX_HEAD_DIM = D_MODEL // N_FOX_HEADS
Q_BLOCK = 128
D_FF = ((8 * D_MODEL // 3 + 255) // 256) * 256
CONV_F_WIDTH = 3
DN_ALPHA = (2 * DEPTH) ** 0.25
DN_BETA = (8 * DEPTH) ** -0.25
LN_EPS = 1e-5


def layer_norm(x, g, b):
    xf = x.astype(jnp.float32)
    mu = jnp.mean(xf, axis=-1, keepdims=True)
    var = jnp.mean(jnp.square(xf - mu), axis=-1, keepdims=True)
    y = (xf - mu) * lax.rsqrt(var + LN_EPS)
    return (y * g.astype(jnp.float32) + b.astype(jnp.float32)).astype(x.dtype)

def causal_dwconv(x, w, b):
    width = w.shape[0]
    length = x.shape[1]
    xp = jnp.pad(x, ((0, 0), (width - 1, 0), (0, 0)))
    y = b
    for k in range(width):
        y = y + xp[:, k:k + length] * w[k]
    return y

def rg_lru(x, w_r, b_r, w_i, b_i, lam):
    bsz, length, width = x.shape
    xb = x.reshape(bsz, length, N_LRU_BLOCKS, LRU_BLOCK)
    r = jax.nn.sigmoid(jnp.einsum('blnc,ncd->blnd', xb, w_r).reshape(bsz, length, width) + b_r)
    i = jax.nn.sigmoid(jnp.einsum('blnc,ncd->blnd', xb, w_i).reshape(bsz, length, width) + b_i)
    log_a = -LRU_C * r.astype(jnp.float32) * jax.nn.softplus(-lam.astype(jnp.float32))
    a = jnp.exp(log_a)
    u = jnp.sqrt(-jnp.expm1(2.0 * log_a)) * (i * x).astype(jnp.float32)

    def combine(left, right):
        a1, b1 = left
        a2, b2 = right
        return a1 * a2, a2 * b1 + b2

    _, h = lax.associative_scan(combine, (a, u), axis=1)
    return h.astype(x.dtype)

def recurrent_mixer(x, w_in, conv_w, conv_b, w_r, b_r, w_i, b_i, lam, w_out):
    gr = x @ w_in
    gate, rec = gr[..., :D_RNN], gr[..., D_RNN:]
    rec = causal_dwconv(rec, conv_w, conv_b)
    h = rg_lru(rec, w_r, b_r, w_i, b_i, lam)
    return (jax.nn.gelu(gate) * h) @ w_out

def conv_ffn(x, w_in, conv_w, conv_b, w_out):
    h = causal_dwconv(x @ w_in, conv_w, conv_b)
    gate, val = h[..., :D_FF], h[..., D_FF:]
    return (jax.nn.gelu(gate) * val) @ w_out

def to_heads_padded(t, lp):
    bsz, length, _ = t.shape
    t = t.reshape(bsz, length, N_FOX_HEADS, FOX_HEAD_DIM).transpose(0, 2, 1, 3)
    return jnp.pad(t, ((0, 0), (0, 0), (0, lp - length), (0, 0)))

def shared_kv(x, kv_w, f_b):
    length = x.shape[1]
    lp = -(-length // Q_BLOCK) * Q_BLOCK
    z = x @ kv_w
    k = to_heads_padded(z[..., :D_MODEL], lp)
    v = to_heads_padded(z[..., D_MODEL:2 * D_MODEL], lp)
    log_f = jax.nn.log_sigmoid(z[..., 2 * D_MODEL:].astype(jnp.float32) + f_b.astype(jnp.float32))
    c = jnp.cumsum(log_f, axis=1).transpose(0, 2, 1)
    c = jnp.pad(c, ((0, 0), (0, 0), (0, lp - length)), mode='edge')
    return k, v, c

def forgetting_attention(q, k, v, c):
    lp = q.shape[2]
    scale = q.shape[-1] ** -0.5
    outs = []
    for q0 in range(0, lp, Q_BLOCK):
        end = q0 + Q_BLOCK
        s = jnp.einsum('bhqd,bhkd->bhqk', q[:, :, q0:end], k[:, :, :end]).astype(jnp.float32) * scale
        s = s + c[:, :, q0:end, None] - c[:, :, None, :end]
        mask = jnp.arange(end)[None, :] <= jnp.arange(q0, end)[:, None]
        s = jnp.where(mask, s, -jnp.inf)
        p = jax.nn.softmax(s, axis=-1).astype(v.dtype)
        outs.append(jnp.einsum('bhqk,bhkd->bhqd', p, v[:, :, :end]))
    return jnp.concatenate(outs, axis=2)

def fox_mixer(x, w_in, w_out, k, v, c):
    bsz, length, _ = x.shape
    qg = x @ w_in
    q = to_heads_padded(qg[..., :D_MODEL], k.shape[2])
    o = forgetting_attention(q, k, v, c)[:, :, :length]
    o = o.transpose(0, 2, 1, 3).reshape(bsz, length, D_MODEL)
    return (o * jax.nn.sigmoid(qg[..., D_MODEL:])) @ w_out

def first_inputs(seed: int = 0) -> dict:
    key = jax.random.key(seed)
    ks = jax.random.split(key, 24)
    f32 = jnp.float32
    d = D_MODEL

    def nrm(k, shape, scale):
        return jax.random.normal(k, shape, f32) * scale

    u = jax.random.uniform(ks[9], (N_A_LAYERS, D_RNN), f32, 0.9, 0.999)
    a0 = u ** (1.0 / LRU_C)
    lam = jnp.log(a0) - jnp.log1p(-a0)

    kv_w = jnp.concatenate([
        nrm(ks[11], (d, d), d ** -0.5),
        nrm(ks[12], (d, d), d ** -0.5 * DN_BETA),
        nrm(ks[13], (d, N_FOX_HEADS), d ** -0.5),
    ], axis=1)

    return {
        "x": nrm(ks[0], (BATCH, SEQ, d), 1.0),
        "meta": nrm(ks[1], (N_META, d), 1.0),
        "a_w_in": nrm(ks[2], (N_A_LAYERS, d, 2 * D_RNN), d ** -0.5),
        "a_conv_w": nrm(ks[3], (N_A_LAYERS, CONV_A_WIDTH, D_RNN), CONV_A_WIDTH ** -0.5),
        "a_conv_b": nrm(ks[4], (N_A_LAYERS, D_RNN), 0.02),
        "a_w_r": nrm(ks[5], (N_A_LAYERS, N_LRU_BLOCKS, LRU_BLOCK, LRU_BLOCK), LRU_BLOCK ** -0.5),
        "a_b_r": nrm(ks[6], (N_A_LAYERS, D_RNN), 0.02),
        "a_w_i": nrm(ks[7], (N_A_LAYERS, N_LRU_BLOCKS, LRU_BLOCK, LRU_BLOCK), LRU_BLOCK ** -0.5),
        "a_b_i": nrm(ks[8], (N_A_LAYERS, D_RNN), 0.02),
        "a_lambda": lam,
        "a_w_out": nrm(ks[10], (N_A_LAYERS, D_RNN, d), D_RNN ** -0.5 * DN_BETA),
        "kv_w": kv_w,
        "kv_f_b": jax.random.uniform(ks[14], (N_FOX_HEADS,), f32, 1.0, 4.0),
        "b_w_in": nrm(ks[15], (N_B_LAYERS, d, 2 * d), d ** -0.5),
        "b_w_out": nrm(ks[16], (N_B_LAYERS, d, d), d ** -0.5 * DN_BETA),
        "f_w_in": nrm(ks[17], (DEPTH, d, 2 * D_FF), d ** -0.5),
        "f_conv_w": nrm(ks[18], (DEPTH, CONV_F_WIDTH, 2 * D_FF), CONV_F_WIDTH ** -0.5),
        "f_conv_b": nrm(ks[19], (DEPTH, 2 * D_FF), 0.02),
        "f_w_out": nrm(ks[20], (DEPTH, D_FF, d), D_FF ** -0.5 * DN_BETA),
        "ln1_g": 1.0 + nrm(ks[21], (DEPTH, d), 0.02),
        "ln1_b": nrm(ks[22], (DEPTH, d), 0.02),
        "ln2_g": 1.0 + nrm(ks[23], (DEPTH, d), 0.02),
        "ln2_b": nrm(jax.random.fold_in(key, 99), (DEPTH, d), 0.02),
    }

def first_block(x, meta, a_w_in, a_conv_w, a_conv_b, a_w_r, a_b_r, a_w_i, a_b_i, a_lambda, a_w_out,
              kv_w, kv_f_b, b_w_in, b_w_out, f_w_in, f_conv_w, f_conv_b, f_w_out,
              ln1_g, ln1_b, ln2_g, ln2_b):
    bsz = x.shape[0]
    h = jnp.concatenate([jnp.broadcast_to(meta.astype(x.dtype), (bsz, N_META, D_MODEL)), x], axis=1)
    k = v = c = None
    for layer in range(DEPTH):
        if layer < N_A_LAYERS:
            mix = recurrent_mixer(h, a_w_in[layer], a_conv_w[layer], a_conv_b[layer],
                                  a_w_r[layer], a_b_r[layer], a_w_i[layer], a_b_i[layer],
                                  a_lambda[layer], a_w_out[layer])
        else:
            if layer == N_A_LAYERS:
                k, v, c = shared_kv(h, kv_w, kv_f_b)
            j = layer - N_A_LAYERS
            mix = fox_mixer(h, b_w_in[j], b_w_out[j], k, v, c)
        h = layer_norm(DN_ALPHA * h + mix, ln1_g[layer], ln1_b[layer])
        ffn = conv_ffn(h, f_w_in[layer], f_conv_w[layer], f_conv_b[layer], f_w_out[layer])
        h = layer_norm(DN_ALPHA * h + ffn, ln2_g[layer], ln2_b[layer])
    return h[:, N_META:]


HEAD_DIM = 64
NORM_EPS = 1e-6
D_FF_2 = 2752
A_HEADS = 6
A_WIDTH = 384
A_DECAY_LORA = 32
A_AAA_LORA = 32
A_GATE_LORA = 64
A_MV_LORA = 16
A_GN_EPS = 64e-5
A_SLAB = (384, 384, 384, 32, 32, 64)
A_IN = 1280
B_HEADS = 6
B_WIDTH = 384
B_KV_LATENT = 128
B_IDX_HEADS = 8
B_IDX_DIM = 64
B_TOPK_MAX = 256
B_QUERY_BLOCK = 128
B_SLAB = (384, 128, 512, 64, 8)
B_IN = 1096
C_HEADS = 4
C_WIDTH = 256
C_CHUNK = 128
C_ROPE_BASE = 10000.0
C_SLAB = (256, 256, 256, 256)
C_IN = 1024
D_MIX = 1024
N_IN = 3400


def _split(p, widths):
    out, start = [], 0
    for w in widths:
        out.append(p[..., start:start + w])
        start += w
    return out

def rmsnorm(x, g, eps=NORM_EPS):
    xf = x.astype(jnp.float32)
    y = xf * lax.rsqrt(jnp.mean(xf * xf, axis=-1, keepdims=True) + eps)
    return y.astype(x.dtype) * g

def swiglu(h, w_gate, w_up, w_down):
    return (jax.nn.silu(h @ w_gate) * (h @ w_up)) @ w_down

def shift_lerp(p, mu):
    prev = jnp.pad(p, ((0, 0), (1, 0), (0, 0)))[:, :-1]
    return p + (prev - p) * mu

def _head_layernorm(y, eps):
    mu = jnp.mean(y, axis=-1, keepdims=True)
    var = jnp.mean(jnp.square(y - mu), axis=-1, keepdims=True)
    return (y - mu) * lax.rsqrt(var + eps)

def _rwkv7_recurrence(r, decay, k, v, a, b):
    Bsz, T, H, N = r.shape

    def step(S, inp):
        r_t, w_t, k_t, v_t, a_t, b_t = inp
        sa = jnp.einsum('bhvk,bhk->bhv', S, a_t)
        S = S * w_t[:, :, None, :] + sa[..., None] * b_t[:, :, None, :] + v_t[..., None] * k_t[:, :, None, :]
        return S, jnp.einsum('bhvk,bhk->bhv', S, r_t)

    xs = tuple(jnp.moveaxis(z, 1, 0) for z in (r, decay, k, v, a, b))
    _, y = lax.scan(step, jnp.zeros((Bsz, H, N, N), jnp.float32), xs)
    return jnp.moveaxis(y, 0, 1)

def rwkv7_mixer(r, k, v, w_lo, a_lo, g_lo, w0, w2, a0, a2, g2, k_k, k_a, r_k, ln_w, ln_b):
    Bsz, T, _ = r.shape
    dt = r.dtype
    heads = lambda z: z.astype(jnp.float32).reshape(Bsz, T, A_HEADS, HEAD_DIM)
    w = -jax.nn.softplus(-(w0 + jnp.tanh(w_lo) @ w2)) - 0.5
    a = jax.nn.sigmoid(a0 + a_lo @ a2)
    g = jax.nn.sigmoid(g_lo) @ g2
    kk = heads(k * k_k)
    kk = kk / jnp.maximum(jnp.linalg.norm(kk, axis=-1, keepdims=True), 1e-12)
    k = k * (1.0 + (a - 1.0) * k_a)
    decay = jnp.exp(-jnp.exp(heads(w)))
    rh, kh, vh, ah = heads(r), heads(k), heads(v), heads(a)
    y = _rwkv7_recurrence(rh, decay, kh, vh, -kk, kk * ah)
    y = _head_layernorm(y, A_GN_EPS) * ln_w.reshape(A_HEADS, HEAD_DIM) + ln_b.reshape(A_HEADS, HEAD_DIM)
    y = y + jnp.sum(rh * kh * r_k, axis=-1, keepdims=True) * vh
    return y.reshape(Bsz, T, A_WIDTH).astype(dt) * g

def dsa_mixer(q, c_kv, iq, ik, iw, kv_norm, w_uk, w_uv):
    Bsz, T, _ = q.shape
    n_keys = T
    topk = min(B_TOPK_MAX, n_keys // 4)
    nb = T // B_QUERY_BLOCK
    c = rmsnorm(c_kv, kv_norm)
    qh = q.reshape(Bsz, T, B_HEADS, HEAD_DIM)
    q_lat = jnp.einsum('bthd,hdc->bthc', qh, w_uk) * HEAD_DIM ** -0.5
    iqh = iq.reshape(Bsz, T, B_IDX_HEADS, B_IDX_DIM) * B_IDX_DIM ** -0.5
    iwh = iw * B_IDX_HEADS ** -0.5
    key_pos = jnp.arange(n_keys)
    blocks = lambda z: jnp.moveaxis(z.reshape((Bsz, nb, B_QUERY_BLOCK) + z.shape[2:]), 1, 0)

    def one_block(args):
        q_lat_b, iq_b, iw_b, blk = args
        q_pos = blk * B_QUERY_BLOCK + jnp.arange(B_QUERY_BLOCK)
        rel = jax.nn.relu(jnp.einsum('bqhd,bsd->bqhs', iq_b, ik))
        score = jnp.einsum('bqh,bqhs->bqs', iw_b, rel).astype(jnp.float32)
        visible = key_pos[None, :] <= q_pos[:, None]
        score = jnp.where(visible[None], score, -jnp.inf)
        _, idx = lax.top_k(score, topk)
        valid = idx <= q_pos[None, :, None]
        c_sel = jax.vmap(lambda cb, ib: cb[ib])(c, idx)
        logits = jnp.einsum('bqhc,bqkc->bqhk', q_lat_b, c_sel).astype(jnp.float32)
        logits = jnp.where(valid[:, :, None, :], logits, -jnp.inf)
        prob = jax.nn.softmax(logits, axis=-1).astype(c.dtype)
        o_lat = jnp.einsum('bqhk,bqkc->bqhc', prob, c_sel)
        return jnp.einsum('bqhc,hcd->bqhd', o_lat, w_uv)

    out = lax.map(one_block, (blocks(q_lat), blocks(iqh), blocks(iwh), jnp.arange(nb)))
    return jnp.moveaxis(out, 0, 1).reshape(Bsz, T, B_WIDTH)

def _retnet_rotate(z):
    T = z.shape[1]
    half = HEAD_DIM // 2
    theta = C_ROPE_BASE ** (-jnp.linspace(0.0, 1.0, half, dtype=jnp.float32))
    ang = jnp.arange(T, dtype=jnp.float32)[:, None] * theta[None, :]
    cos, sin = jnp.cos(ang)[None, :, None, :], jnp.sin(ang)[None, :, None, :]
    z1, z2 = z[..., :half], z[..., half:]
    return jnp.concatenate([z1 * cos - z2 * sin, z1 * sin + z2 * cos], axis=-1)

def retention_mixer(q, k, v, g):
    Bsz, T, _ = q.shape
    nc = T // C_CHUNK
    dt = q.dtype
    f32 = jnp.float32
    heads = lambda z: z.astype(f32).reshape(Bsz, T, C_HEADS, HEAD_DIM)
    qh = _retnet_rotate(heads(q))
    kh = _retnet_rotate(heads(k)) * HEAD_DIM ** -0.5
    vh = heads(v)
    log_gamma = jnp.log(1.0 - 2.0 ** (-5.0 - jnp.arange(C_HEADS, dtype=f32)))
    n = jnp.arange(C_CHUNK, dtype=f32)
    diff = n[:, None] - n[None, :]
    intra = jnp.where(diff[None] >= 0, jnp.exp(jnp.maximum(diff, 0.0)[None] * log_gamma[:, None, None]), 0.0)
    q_decay = jnp.exp((n[:, None] + 1.0) * log_gamma[None, :])
    k_decay = jnp.exp((C_CHUNK - 1.0 - n)[:, None] * log_gamma[None, :])
    chunk_decay = jnp.exp(C_CHUNK * log_gamma)
    chunks = lambda z: jnp.moveaxis(z.reshape(Bsz, nc, C_CHUNK, C_HEADS, HEAD_DIM), 1, 0)

    def step(state, inp):
        qc, kc, vc = inp
        scores = jnp.einsum('bnhd,bmhd->bhnm', qc, kc) * intra[None]
        inner = jnp.einsum('bhnm,bmhe->bnhe', scores, vc)
        cross = jnp.einsum('bnhd,bhde->bnhe', qc, state) * q_decay[None, :, :, None]
        state = state * chunk_decay[None, :, None, None] + jnp.einsum('bmhd,bmhe->bhde', kc * k_decay[None, :, :, None], vc)
        return state, inner + cross

    state0 = jnp.zeros((Bsz, C_HEADS, HEAD_DIM, HEAD_DIM), f32)
    _, y = lax.scan(step, state0, (chunks(qh), chunks(kh), chunks(vh)))
    y = jnp.moveaxis(y, 0, 1).reshape(Bsz, T, C_HEADS, HEAD_DIM)
    y = y * lax.rsqrt(jnp.mean(y * y, axis=-1, keepdims=True) + NORM_EPS)
    return jax.nn.silu(g) * y.reshape(Bsz, T, C_WIDTH).astype(dt)

def second_inputs(seed: int = 0) -> dict:
    key = jax.random.key(seed)
    counter = [0]

    def nk():
        counter[0] += 1
        return jax.random.fold_in(key, counter[0])

    def nrm(shape, scale):
        return jax.random.normal(nk(), shape, jnp.float32) * scale

    def gain(shape):
        return 1.0 + nrm(shape, 0.02)

    L = DEPTH
    return {
        'x': nrm((BATCH, SEQ, D_MODEL), 1.0),
        'ffn1_norm': gain((L, D_MODEL)),
        'ffn1_w_gate': nrm((L, D_MODEL, D_FF_2), D_MODEL ** -0.5),
        'ffn1_w_up': nrm((L, D_MODEL, D_FF_2), D_MODEL ** -0.5),
        'ffn1_w_down': nrm((L, D_FF_2, D_MODEL), D_FF_2 ** -0.5),
        'mix_norm': gain((L, D_MODEL)),
        'w_in': nrm((L, D_MODEL, N_IN), D_MODEL ** -0.5),
        'w_out': nrm((L, D_MIX, D_MODEL), D_MIX ** -0.5),
        'rwkv_mu': jax.random.uniform(nk(), (L, A_IN), jnp.float32),
        'rwkv_w0': jnp.linspace(-6.0, -1.0, A_WIDTH, dtype=jnp.float32)[None, :] + nrm((L, A_WIDTH), 0.1),
        'rwkv_w2': nrm((L, A_DECAY_LORA, A_WIDTH), 0.1),
        'rwkv_a0': nrm((L, A_WIDTH), 0.1),
        'rwkv_a2': nrm((L, A_AAA_LORA, A_WIDTH), 0.1),
        'rwkv_g2': nrm((L, A_GATE_LORA, A_WIDTH), A_GATE_LORA ** -0.5),
        'rwkv_k_k': 0.85 + nrm((L, A_WIDTH), 0.02),
        'rwkv_k_a': 1.0 + nrm((L, A_WIDTH), 0.02),
        'rwkv_r_k': nrm((L, A_HEADS, HEAD_DIM), 0.1),
        'rwkv_ln_w': gain((L, A_WIDTH)),
        'rwkv_ln_b': nrm((L, A_WIDTH), 0.01),
        'rwkv_vres_w_in': nrm((L - 1, D_MODEL, A_MV_LORA), D_MODEL ** -0.5),
        'rwkv_vres_mu': jax.random.uniform(nk(), (L - 1, A_MV_LORA), jnp.float32),
        'rwkv_v0': 0.5 + nrm((L - 1, A_WIDTH), 0.1),
        'rwkv_v2': nrm((L - 1, A_MV_LORA, A_WIDTH), 0.1),
        'dsa_kv_norm': gain((L, B_KV_LATENT)),
        'dsa_w_uk': nrm((L, B_HEADS, HEAD_DIM, B_KV_LATENT), B_KV_LATENT ** -0.5),
        'dsa_w_uv': nrm((L, B_HEADS, B_KV_LATENT, HEAD_DIM), B_KV_LATENT ** -0.5),
        'ffn2_norm': gain((L, D_MODEL)),
        'ffn2_w_gate': nrm((L, D_MODEL, D_FF_2), D_MODEL ** -0.5),
        'ffn2_w_up': nrm((L, D_MODEL, D_FF_2), D_MODEL ** -0.5),
        'ffn2_w_down': nrm((L, D_FF_2, D_MODEL), D_FF_2 ** -0.5),
        'final_norm': gain((D_MODEL,)),
    }

def second_block(x, ffn1_norm, ffn1_w_gate, ffn1_w_up, ffn1_w_down, mix_norm, w_in, w_out,
              rwkv_mu, rwkv_w0, rwkv_w2, rwkv_a0, rwkv_a2, rwkv_g2, rwkv_k_k, rwkv_k_a, rwkv_r_k,
              rwkv_ln_w, rwkv_ln_b, rwkv_vres_w_in, rwkv_vres_mu, rwkv_v0, rwkv_v2,
              dsa_kv_norm, dsa_w_uk, dsa_w_uv,
              ffn2_norm, ffn2_w_gate, ffn2_w_up, ffn2_w_down, final_norm):
    v_first = None
    for l in range(DEPTH):
        x = x + 0.5 * swiglu(rmsnorm(x, ffn1_norm[l]), ffn1_w_gate[l], ffn1_w_up[l], ffn1_w_down[l])
        h = rmsnorm(x, mix_norm[l])
        if l == 0:
            p_a, p_b, p_c = _split(h @ w_in[l], (A_IN, B_IN, C_IN))
        else:
            w_comb = jnp.concatenate([w_in[l], rwkv_vres_w_in[l - 1]], axis=1)
            p_a, p_b, p_c, p_mv = _split(h @ w_comb, (A_IN, B_IN, C_IN, A_MV_LORA))
        r, k, v, w_lo, a_lo, g_lo = _split(shift_lerp(p_a, rwkv_mu[l]), A_SLAB)
        if l == 0:
            v_first = v
        else:
            mv = shift_lerp(p_mv, rwkv_vres_mu[l - 1])
            v = v + (v_first - v) * jax.nn.sigmoid(rwkv_v0[l - 1] + mv @ rwkv_v2[l - 1])
        o_a = rwkv7_mixer(r, k, v, w_lo, a_lo, g_lo, rwkv_w0[l], rwkv_w2[l], rwkv_a0[l], rwkv_a2[l],
                          rwkv_g2[l], rwkv_k_k[l], rwkv_k_a[l], rwkv_r_k[l], rwkv_ln_w[l], rwkv_ln_b[l])
        q_b, c_b, iq_b, ik_b, iw_b = _split(p_b, B_SLAB)
        o_b = dsa_mixer(q_b, c_b, iq_b, ik_b, iw_b, dsa_kv_norm[l], dsa_w_uk[l], dsa_w_uv[l])
        q_c, k_c, v_c, g_c = _split(p_c, C_SLAB)
        o_c = retention_mixer(q_c, k_c, v_c, g_c)
        x = x + jnp.concatenate([o_a, o_b, o_c], axis=-1) @ w_out[l]
        x = x + 0.5 * swiglu(rmsnorm(x, ffn2_norm[l]), ffn2_w_gate[l], ffn2_w_up[l], ffn2_w_down[l])
    return rmsnorm(x, final_norm)


def setup_inputs(seed=0):
    out = dict(first_inputs(seed))
    for name, value in second_inputs(seed + 1).items():
        if name != "x":
            out[name + "_2"] = value
    return out


def reference(
    x, meta, a_w_in, a_conv_w, a_conv_b, a_w_r, a_b_r, a_w_i, a_b_i, a_lambda, a_w_out, kv_w,
    kv_f_b, b_w_in, b_w_out, f_w_in, f_conv_w, f_conv_b, f_w_out, ln1_g, ln1_b, ln2_g, ln2_b,
    ffn1_norm_2, ffn1_w_gate_2, ffn1_w_up_2, ffn1_w_down_2, mix_norm_2, w_in_2, w_out_2,
    rwkv_mu_2, rwkv_w0_2, rwkv_w2_2, rwkv_a0_2, rwkv_a2_2, rwkv_g2_2, rwkv_k_k_2, rwkv_k_a_2,
    rwkv_r_k_2, rwkv_ln_w_2, rwkv_ln_b_2, rwkv_vres_w_in_2, rwkv_vres_mu_2, rwkv_v0_2,
    rwkv_v2_2, dsa_kv_norm_2, dsa_w_uk_2, dsa_w_uv_2, ffn2_norm_2, ffn2_w_gate_2, ffn2_w_up_2,
    ffn2_w_down_2, final_norm_2,
):
    x = first_block(
        x, meta, a_w_in, a_conv_w, a_conv_b, a_w_r, a_b_r, a_w_i, a_b_i, a_lambda, a_w_out,
        kv_w, kv_f_b, b_w_in, b_w_out, f_w_in, f_conv_w, f_conv_b, f_w_out, ln1_g, ln1_b, ln2_g,
        ln2_b,
    )
    return second_block(
        x, ffn1_norm_2, ffn1_w_gate_2, ffn1_w_up_2, ffn1_w_down_2, mix_norm_2, w_in_2, w_out_2,
        rwkv_mu_2, rwkv_w0_2, rwkv_w2_2, rwkv_a0_2, rwkv_a2_2, rwkv_g2_2, rwkv_k_k_2,
        rwkv_k_a_2, rwkv_r_k_2, rwkv_ln_w_2, rwkv_ln_b_2, rwkv_vres_w_in_2, rwkv_vres_mu_2,
        rwkv_v0_2, rwkv_v2_2, dsa_kv_norm_2, dsa_w_uk_2, dsa_w_uv_2, ffn2_norm_2, ffn2_w_gate_2,
        ffn2_w_up_2, ffn2_w_down_2, final_norm_2,
    )


_drawn_inputs = setup_inputs


def setup_inputs(seed=0):
    import zlib

    import numpy as np

    out = dict(_drawn_inputs(seed))
    spreads = {}
    factors = {'a_b_r': 8.0,
     'a_b_i': 8.0,
     'f_conv_b': 3.07,
     'ffn1_norm_2': 3.091,
     'rwkv_w2_2': 2.676,
     'rwkv_a0_2': 2.773,
     'rwkv_k_k_2': 7.607,
     'rwkv_k_a_2': 4.726,
     'rwkv_ln_w_2': 5.591,
     'rwkv_ln_b_2': 8.0,
     'rwkv_vres_mu_2': 11.649,
     'rwkv_v0_2': 17.129,
     'dsa_kv_norm_2': 8.0,
     'ffn2_norm_2': 4.489,
     'final_norm_2': 7.888}
    for name, (base, spread) in spreads.items():
        noise = np.random.default_rng([zlib.crc32(name.encode()), seed]).standard_normal(out[name].shape)
        drawn = base * np.exp(spread * noise) if base else spread * noise
        out[name] = __import__('jax').numpy.asarray(drawn.astype(out[name].dtype))
    for name, factor in factors.items():
        out[name] = (out[name] * factor).astype(out[name].dtype)
    return out
```

```python
import concourse.bass as bass
from concourse import mybir
from contextlib import ExitStack, contextmanager
import math
import numpy as np

FP32 = mybir.dt.float32
FP32R = mybir.dt.float32r
ALU = mybir.AluOpType
ACT = mybir.ActivationFunctionType
AX = mybir.AxisListType

P = 128
D = 1024
KT = D // P
SEQ = 512
META = 16
T1 = SEQ + META
HALF1 = T1 // 2
D_RNN = 1536
N_LRU = 16
LRU = D_RNN // N_LRU
D_FF = 2816
FT = D_FF // P
FT2 = 22
ALPHA = 4.0 ** 0.25
LN_EPS = 1e-5
RMS_EPS = 1e-6
GN_EPS = 64e-5
HEADS1 = 16
HD = 64
QB = 128
NEG = -1.0e30
SCALE = HD ** -0.5


class Span:

    def __init__(self, tokens):
        self.tokens = tokens
        self.banks = -(-tokens // 512)
        self.width = tokens // self.banks

    def psum(self, ps, bank, row=0, rows=P):
        return ps[row:row + rows, bank:bank + self.banks, 0:self.width]

    def sbuf(self, ap):
        return ap.rearrange("p (h t) -> p h t", h=self.banks)


S1 = Span(T1)
S2 = Span(SEQ)


class Own:

    def __init__(self, eng, sem, base=0):
        self.eng, self.sem, self.base, self.n = eng, sem, base, 0

    def then(self, ins):
        ins.then_inc(self.sem, 1)
        self.n += 1
        return ins

    def wait(self):
        self.eng.wait_ge(self.sem, self.base + self.n)



@contextmanager
def stage(nc, name, *signals):
    sems = {s: nc.alloc_semaphore(f"{name}_{s}") for s in signals}
    with nc.Block() as block:
        yield block, sems
    nc.clear_and_free_semaphores(list(sems.values()))
    nc.all_engine_barrier()


def vector_columns():
    cols, at = {}, 0

    def add(name, n):
        nonlocal at
        cols[name] = (at, n)
        at += n

    for k in range(4):
        add(f"a_conv_w{k}", N_LRU)
    for n in ("a_conv_b", "a_b_r", "a_b_i", "a_lambda"):
        add(n, N_LRU)
    for l in range(2):
        for k in range(3):
            add(f"f_conv_w{l}_{k}", 2 * FT)
        add(f"f_conv_b{l}", 2 * FT)
        for n in ("ln1_g", "ln1_b", "ln2_g", "ln2_b"):
            add(f"{n}{l}", KT)
    add("kv_f_b", 1)
    for l in range(2):
        for n in ("ffn1_norm", "mix_norm", "ffn2_norm"):
            add(f"{n}{l}", KT)
        add(f"rwkv_mu{l}", 10)
        for n in ("w0", "a0", "k_k", "k_a", "r_k", "ln_w", "ln_b"):
            add(f"rwkv_{n}{l}", 3)
        add(f"dsa_kv_norm{l}", 1)
    add("rwkv_v0", 3)
    add("rwkv_vres_mu", 1)
    add("final_norm", KT)
    return cols, at


COLS, NCOLS = vector_columns()


class Mem:

    def __init__(self, nc, ctx):
        def sb(name, shape):
            return ctx.enter_context(nc.sbuf_tensor(name, shape, FP32))

        self.x = sb("x_tokens", [P, KT, T1])
        self.vec = sb("vectors", [P, NCOLS])
        self.ones = sb("ones", [P, P])
        self.ident = sb("identity", [P, P])
        self.causal = sb("causal", [P, P])
        self.stat = sb("stat", [P, 64])
        self.eps = sb("eps", [P, 3])
        self.c_dram = nc.dram_tensor("forget_scratch", (HEADS1, T1), FP32).ap()
        self.ps = ctx.enter_context(nc.psum_tensor("psum", [P, 8, 512], FP32))

    def add_part_two(self, nc, ctx):
        self.masks = ctx.enter_context(nc.sbuf_tensor("masks", [P, 7 * P], FP32))
        (self.head_ones, self.low16, self.edge16, self.edge32, self.up16, self.strict64,
         self.upto64) = [self.masks[:, i * P:(i + 1) * P] for i in range(7)]
        self.v_first = ctx.enter_context(nc.sbuf_tensor("v_first", [P, 3, SEQ], FP32))

    def col(self, name, i=0, rows=P):
        at, _ = COLS[name]
        if isinstance(i, int):
            return self.vec[0:rows, at + i:at + i + 1]
        return self.vec[0:rows, bass.ds(i + at, 1)]


def mixer_memory(nc, ctx, m, name, part_two):
    def sb(what, shape):
        return ctx.enter_context(nc.sbuf_tensor(f"{name}_{what}", shape, FP32))

    m.y = sb("y", [P, KT, T1])
    m.big = sb("big", [P, 24 * T1])
    m.ring = sb("ring", [P, 2, 4 * KT * P])
    m.work = sb("work", [P, 8, 532])
    m.wide = sb("wide", [P, 8 * SEQ])
    misc = sb("misc", [P, 4 * T1])
    m.crow = misc[0:1, :]
    m.ret_v = misc[:, 0:1024].rearrange("p (n f) -> p n f", f=256)
    m.reset = misc[:, 1024:1536]
    if part_two:
        m.other = sb("other", [P, 16, SEQ])


def load_tiles(sp, nc, ring, dram, n, loaded, finished):
    for j in range(2):
        sp.dma_start(ring[j], dram[j]).then_inc(loaded[j], 16)
    with sp.Fori(1, n // 2) as i:
        for j in range(2):
            sp.wait_ge(finished, 2 * i + j - 1)
            sp.dma_start(ring[j], dram[2 * i + j]).then_inc(loaded[j], 16)


def project(nc, ps, bank, w, x, k_tiles, span, rows=P, row=0):
    last = None
    for h in range(span.banks):
        for k in range(k_tiles):
            last = nc.tensor.matmul(ps[row:row + rows, bank + h, 0:span.width], w[:, k * rows:(k + 1) * rows],
                                    x(k)[:, h * span.width:(h + 1) * span.width],
                                    start=(k == 0), stop=(k == k_tiles - 1))
    return last


def setup_stage(nc, m, d):
    with stage(nc, "setup", "loaded", "const") as (block, s):
        @block.sync
        def _(sp):
            sp.dma_start(m.x[:, :, :], d["x"]).then_inc(s["loaded"], 16)
            sp.dma_start(m.vec[:, :], d["vectors"]).then_inc(s["loaded"], 16)
            sp.wait_ge(s["loaded"], 32)

        @block.gpsimd
        def _(pool):
            nc.gpsimd.memset(m.ones[:, :], 1.0).then_inc(s["const"], 1)
            nc.gpsimd.memset(m.ident[:, :], 0.0).then_inc(s["const"], 1)
            nc.gpsimd.memset(m.causal[:, :], 0.0).then_inc(s["const"], 1)
            pool.wait_ge(s["const"], 3)
            nc.gpsimd.affine_select(out=m.causal[:, :], in_=m.causal[:, :], compare_op=ALU.is_ge, fill=NEG,
                                    base=0, pattern=[[-1, P]], channel_multiplier=1)
            nc.gpsimd.memset(m.eps[:, 0:1], LN_EPS)
            nc.gpsimd.memset(m.eps[:, 1:2], RMS_EPS)
            nc.gpsimd.memset(m.eps[:, 2:3], GN_EPS)
            pool.wait_ge(s["const"], 2)
            nc.gpsimd.affine_select(out=m.ident[:, :], in_=m.ident[:, :], compare_op=ALU.not_equal, fill=1.0,
                                    base=0, pattern=[[-1, P]], channel_multiplier=1).then_inc(s["const"], 1)
            pool.wait_ge(s["const"], 4)


def load_masks_stage(nc, m, d):
    with stage(nc, "load_masks", "loaded") as (block, s):
        @block.sync
        def _(sp):
            sp.dma_start(m.masks[:, :], d["masks"]).then_inc(s["loaded"], 16)
            sp.wait_ge(s["loaded"], 16)


def lru_stage(nc, m, d):
    R = LRU
    hid = m.big[:, 0:N_LRU * T1].rearrange("p (n t) -> p n t", t=T1)
    width = 2 * KT * R + 2 * R
    ring = [m.ring[:, j, 0:width] for j in range(2)]
    gate, pad, conv, rr, ii, th, q, u = [m.work[0:R, k, 0:T1 + 3] for k in range(8)]
    decay = m.stat[0:R, 0:N_LRU]
    with stage(nc, "lru", "loaded0", "loaded1", "projected", "tile_done", "evacuated", "convolved", "gates_in_psum",
               "gated", "tanh_ready", "q_ready", "root_ready", "h_ready", "vec_own", "act_own", "lam_ready") as (block, s):
        @block.sync
        def _(sp):
            load_tiles(sp, nc, ring, d["lru_w"], N_LRU, (s["loaded0"], s["loaded1"]), s["tile_done"])

        @block.tensor
        def _(pe):
            with pe.Fori(0, N_LRU // 2) as i:
                for j in range(2):
                    t = 2 * i + j
                    pe.wait_ge((s["loaded0"], s["loaded1"])[j], 16 * i + 16)
                    pe.wait_ge(s["evacuated"], t + 1)
                    project(nc, m.ps, 0, ring[j], lambda k: m.x[:, k, :], KT, S1, rows=R)
                    project(nc, m.ps, 2, ring[j][:, KT * R:2 * KT * R], lambda k: m.x[:, k, :], KT, S1,
                            rows=R).then_inc(s["projected"], 1)
                    pe.wait_ge(s["convolved"], t + 1)
                    pe.wait_ge(s["gated"], t + 1)
                    for g in range(2):
                        w = ring[j][0:R, 2 * KT * R + g * R:2 * KT * R + (g + 1) * R]
                        last = project(nc, m.ps, 4 + 2 * g, w, lambda k: conv[:, 0:T1], 1, S1, rows=R)
                    last.then_inc(s["tile_done"], 1)

        @block.scalar
        def _(act):
            nc.scalar.activation(m.stat[0:R, 16:32], m.vec[0:R, COLS["a_lambda"][0]:COLS["a_lambda"][0] + N_LRU],
                                 ACT.Abs).then_inc(s["act_own"], 1)
            act.wait_ge(s["act_own"], 1)
            nc.scalar.activation(m.stat[0:R, 16:32], m.stat[0:R, 16:32], ACT.Exp, scale=-1.0).then_inc(s["act_own"], 1)
            act.wait_ge(s["act_own"], 2)
            nc.scalar.activation(m.stat[0:R, 16:32], m.stat[0:R, 16:32], ACT.Ln, bias=1.0).then_inc(s["lam_ready"], 1)
            act.sem_inc(s["evacuated"], 1)
            act.sem_inc(s["gated"], 1)
            with act.Fori(0, N_LRU // 2) as i:
                for j in range(2):
                    t = 2 * i + j
                    act.wait_ge(s["projected"], t + 1)
                    act.wait_ge(s["h_ready"], t + 1)
                    nc.scalar.copy(S1.sbuf(pad[:, 3:3 + T1]), S1.psum(m.ps, 2, rows=R)).then_inc(s["act_own"], 1)
                    nc.scalar.activation(S1.sbuf(gate[:, 0:T1]), S1.psum(m.ps, 0, rows=R),
                                         ACT.Gelu_apprx_tanh).then_inc(s["evacuated"], 1)
                    act.wait_ge(s["tile_done"], t + 1)
                    nc.scalar.activation(S1.sbuf(rr[:, 0:T1]), S1.psum(m.ps, 4, rows=R), ACT.Sigmoid,
                                         bias=m.col("a_b_r", t, R)).then_inc(s["act_own"], 1)
                    nc.scalar.activation(S1.sbuf(ii[:, 0:T1]), S1.psum(m.ps, 6, rows=R), ACT.Sigmoid,
                                         bias=m.col("a_b_i", t, R)).then_inc(s["gated"], 1)
                    act.wait_ge(s["act_own"], 2 * t + 4)
                    act.wait_ge(s["lam_ready"], 2)
                    nc.scalar.activation(th[:, 0:T1], rr[:, 0:T1], ACT.Tanh,
                                         scale=m.stat[0:R, bass.ds(t, 1)]).then_inc(s["tanh_ready"], 1)
                    act.wait_ge(s["tanh_ready"], t + 1)
                    nc.scalar.activation(rr[:, 0:T1], th[:, 0:T1], ACT.Sqrt, scale=-4.0).then_inc(s["root_ready"], 1)

        @block.vector
        def _(dve):
            nc.vector.memset(pad[:, 0:3], 0.0).then_inc(s["vec_own"], 1)
            nc.vector.tensor_scalar(decay, m.vec[0:R, COLS["a_lambda"][0]:COLS["a_lambda"][0] + N_LRU], -1.0, 0.0,
                                    ALU.mult, ALU.max).then_inc(s["vec_own"], 1)
            dve.wait_ge(s["vec_own"], 2)
            dve.wait_ge(s["lam_ready"], 1)
            nc.vector.tensor_tensor(decay, decay, m.stat[0:R, 16:32], ALU.add).then_inc(s["vec_own"], 1)
            dve.wait_ge(s["vec_own"], 3)
            nc.vector.tensor_scalar(decay, decay, -4.0, None, ALU.mult).then_inc(s["lam_ready"], 1)
            dve.sem_inc(s["h_ready"], 1)
            with dve.Fori(0, N_LRU // 2) as i:
                for j in range(2):
                    t = 2 * i + j
                    own = Own(dve, s["vec_own"], 9 * t + 3)
                    dve.wait_ge(s["evacuated"], t + 2)
                    dve.wait_ge(s["act_own"], 2 * t + 3)
                    own.then(nc.vector.tensor_scalar(conv[:, 0:T1], pad[:, 0:T1], m.col("a_conv_w0", t, R),
                                                     m.col("a_conv_b", t, R), ALU.mult, ALU.add))
                    for k in (1, 2):
                        own.wait()
                        own.then(nc.vector.scalar_tensor_tensor(conv[:, 0:T1], pad[:, k:k + T1],
                                                                m.col(f"a_conv_w{k}", t, R), conv[:, 0:T1],
                                                                ALU.mult, ALU.add))
                    own.wait()
                    nc.vector.scalar_tensor_tensor(conv[:, 0:T1], pad[:, 3:3 + T1], m.col("a_conv_w3", t, R),
                                                   conv[:, 0:T1], ALU.mult, ALU.add).then_inc(s["convolved"], 1)
                    dve.wait_ge(s["tanh_ready"], t + 1)
                    own.then(nc.vector.tensor_scalar(q[:, 0:T1], th[:, 0:T1], -1.0, 1.0, ALU.mult, ALU.add))
                    own.wait()
                    own.then(nc.vector.reciprocal(q[:, 0:T1], q[:, 0:T1]))
                    dve.wait_ge(s["gated"], t + 2)
                    dve.wait_ge(s["convolved"], t + 1)
                    own.then(nc.vector.tensor_tensor(ii[:, 0:T1], ii[:, 0:T1], conv[:, 0:T1], ALU.mult))
                    own.wait()
                    own.then(nc.vector.tensor_tensor(u[:, 0:T1], ii[:, 0:T1], q[:, 0:T1], ALU.mult))
                    own.wait()
                    dve.wait_ge(s["root_ready"], t + 1)
                    own.then(nc.vector.tensor_tensor(u[:, 0:T1], u[:, 0:T1], rr[:, 0:T1], ALU.mult))
                    nc.vector.scalar_tensor_tensor(q[:, 0:T1], th[:, 0:T1], 1.0, q[:, 0:T1], ALU.add,
                                                   ALU.mult).then_inc(s["q_ready"], 1)
                    own.wait()
                    dve.wait_ge(s["q_ready"], t + 1)
                    own.then(nc.vector.tensor_tensor_scan(conv[:, 0:T1], q[:, 0:T1], u[:, 0:T1], 0.0, ALU.mult,
                                                          ALU.add))
                    own.wait()
                    nc.vector.tensor_tensor(hid[0:R, bass.ds(t, 1), :].rearrange("p a t -> p (a t)"), conv[:, 0:T1],
                                            gate[:, 0:T1], ALU.mult).then_inc(s["h_ready"], 1)
                    assert own.n == 9


def out_stage(nc, m, name, weights, k_tiles, rows, hidden, span, skip, y_scale, x_scale, dst=None):
    ring = [m.ring[0:rows, j, 0:k_tiles * P] for j in range(2)]
    tok = span.tokens
    dst = m.y if dst is None else dst
    with stage(nc, name, "loaded0", "loaded1", "projected", "emptied") as (block, s):
        @block.sync
        def _(sp):
            load_tiles(sp, nc, ring, weights, KT, (s["loaded0"], s["loaded1"]), s["projected"])

        @block.tensor
        def _(pe):
            with pe.Fori(0, KT // 2) as i:
                for j in range(2):
                    pe.wait_ge((s["loaded0"], s["loaded1"])[j], 16 * i + 16)
                    pe.wait_ge(s["emptied"], 2 * i + j + 1)
                    project(nc, m.ps, 4 * j, ring[j], hidden, k_tiles, span).then_inc(s["projected"], 1)

        @block.vector
        def _(dve):
            dve.sem_inc(s["emptied"], 2)
            with dve.Fori(0, KT // 2) as i:
                for j in range(2):
                    t = 2 * i + j
                    xt = skip[:, bass.ds(t, 1), :].rearrange("p a t -> p (a t)")
                    dve.wait_ge(s["projected"], t + 1)
                    if y_scale != 1.0:
                        assert x_scale == 1.0
                        nc.vector.scalar_tensor_tensor(span.sbuf(dst[:, bass.ds(t, 1), 0:tok].rearrange("p a t -> p (a t)")),
                                                       span.psum(m.ps, 4 * j), y_scale, span.sbuf(xt), ALU.mult,
                                                       ALU.add).then_inc(s["emptied"], 1)
                    else:
                        nc.vector.scalar_tensor_tensor(span.sbuf(dst[:, bass.ds(t, 1), 0:tok].rearrange("p a t -> p (a t)")),
                                                       span.sbuf(xt), x_scale, span.psum(m.ps, 4 * j), ALU.mult,
                                                       ALU.add).then_inc(s["emptied"], 1)


def norm_stage(nc, m, name, src, dst, gain, bias, eps, span, centre, split=None):
    tok = span.tokens
    acc, mean, rstd = [m.work[:, k, 0:tok] for k in range(3)]
    sq = [m.work[:, 3 + k, 0:tok] for k in range(2)]
    inv = 1.0 / D
    with stage(nc, name, "summed", "mean_psum", "mean_ready", "centred", "squared", "sq_used", "sq_summed", "var_psum",
               "std_ready", "own", "scaled", "done", "hi_ready", "lo_ready") as (block, s):
        @block.vector
        def _(dve):
            own = Own(dve, s["own"])
            if centre:
                own.then(nc.vector.tensor_tensor(acc, src(0), src(1), ALU.add))
                for k in range(2, KT):
                    own.wait()
                    ins = nc.vector.tensor_tensor(acc, acc, src(k), ALU.add)
                    if k < KT - 1:
                        own.then(ins)
                ins.then_inc(s["summed"], 1)
                dve.wait_ge(s["mean_psum"], 1)
                own.then(nc.vector.tensor_scalar(span.sbuf(mean), span.psum(m.ps, 0), inv, None, ALU.mult))
                own.wait()
                for k in range(KT):
                    nc.vector.tensor_tensor(src(k), src(k), mean, ALU.subtract).then_inc(s["centred"], 1)
            for k in range(KT):
                dve.wait_ge(s["squared"], k + 1)
                if k == 0:
                    nc.vector.tensor_copy(acc, sq[0]).then_inc(s["sq_used"], 1)
                else:
                    dve.wait_ge(s["sq_used"], k)
                    nc.vector.tensor_tensor(acc, acc, sq[k % 2], ALU.add).then_inc(s["sq_used"], 1)
            dve.wait_ge(s["std_ready"], 1)
            own.then(nc.vector.reciprocal(rstd, rstd))
            own.wait()

            def scale(k):
                if split and k >= 2:
                    dve.wait_ge(s["lo_ready"], k - 1)
                nc.vector.tensor_tensor(dst(k), src(k), rstd, ALU.mult).then_inc(s["scaled"], 1)

            scale(0)
            for k in range(KT):
                if k + 1 < KT:
                    scale(k + 1)
                if split:
                    dve.wait_ge(s["hi_ready"], k + 1)
                    nc.vector.tensor_tensor(split.lo[:, k, :], dst(k), split.hi[:, k, :].bitcast(FP32),
                                            ALU.subtract).then_inc(s["lo_ready"], 1)

        @block.tensor
        def _(pe):
            if centre:
                pe.wait_ge(s["summed"], 1)
                project(nc, m.ps, 0, m.ones, lambda k: acc, 1, span).then_inc(s["mean_psum"], 1)
            pe.wait_ge(s["sq_used"], KT)
            project(nc, m.ps, 2, m.ones, lambda k: acc, 1, span).then_inc(s["var_psum"], 1)

        @block.scalar
        def _(act):
            for k in range(KT):
                if centre:
                    act.wait_ge(s["centred"], k + 1)
                if k >= 2:
                    act.wait_ge(s["sq_used"], k - 1)
                nc.scalar.activation(sq[k % 2], src(k), ACT.Square).then_inc(s["squared"], 1)
            act.wait_ge(s["var_psum"], 1)
            nc.scalar.activation(span.sbuf(rstd), span.psum(m.ps, 2), ACT.Sqrt, scale=inv,
                                 bias=m.eps[:, 0:1] if eps == LN_EPS else m.eps[:, 1:2]).then_inc(s["std_ready"], 1)
            for k in range(KT):
                act.wait_ge(s["scaled"], k + 1)
                if bias is None:
                    nc.scalar.activation(dst(k), dst(k), ACT.Copy, scale=m.col(gain, k)).then_inc(s["done"], 1)
                else:
                    nc.scalar.activation(dst(k), dst(k), ACT.Identity, scale=m.col(gain, k),
                                         bias=m.col(bias, k)).then_inc(s["done"], 1)
                if split:
                    act.wait_ge(s["done"], k + 1)
                    nc.scalar.copy(split.hi[:, k, :], dst(k)).then_inc(s["hi_ready"], 1)


class Split:

    def __init__(self, nc, ctx, name, shape):
        self.hi = ctx.enter_context(nc.sbuf_tensor(f"{name}_hi", shape, FP32R))
        self.lo = ctx.enter_context(nc.sbuf_tensor(f"{name}_lo", shape, FP32R))


def ffn_memory(nc, ctx, m, name, span):
    tok = span.tokens
    m.xs = Split(nc, ctx, f"{name}_x", [P, KT, tok])
    m.hs = Split(nc, ctx, f"{name}_h", [P, FT, tok])
    m.ws = Split(nc, ctx, f"{name}_w", [P, 2, 11 * P])
    m.raw = ctx.enter_context(nc.sbuf_tensor(f"{name}_raw", [P, 4, 11 * P], FP32))
    m.work = ctx.enter_context(nc.sbuf_tensor(f"{name}_work", [P, 8 if tok > SEQ else 5, tok + 4], FP32))


class Units:

    def __init__(self, nc, m, s, weights, n, k_tiles):
        self.nc, self.m, self.s, self.weights, self.n = nc, m, s, weights, n
        self.k_tiles, self.cols = k_tiles, k_tiles * P

    SIGNALS = ("loaded0", "loaded1", "loaded2", "loaded3", "hi_ready", "lo_ready", "unit_done")

    def source(self, t, g):
        return self.weights[t][:, g * self.cols:(g + 1) * self.cols]

    def load_all(self, sp):
        for j in range(2):
            for g in range(2):
                sp.dma_start(self.m.raw[:, 2 * j + g, 0:self.cols], self.source(j, g)).then_inc(
                    self.s[f"loaded{2 * j + g}"], 16)
        with sp.Fori(1, self.n // 2) as i:
            for j in range(2):
                for g in range(2):
                    sp.wait_ge(self.s["lo_ready"], 4 * i + 2 * j + g - 3)
                    sp.dma_start(self.m.raw[:, 2 * j + g, 0:self.cols], self.source(2 * i + j, g)).then_inc(
                        self.s[f"loaded{2 * j + g}"], 16)

    def split_hi(self, act, i, j, g):
        u = 4 * i + 2 * j + g
        act.wait_ge(self.s[f"loaded{2 * j + g}"], 16 * i + 16)
        act.wait_ge(self.s["unit_done"], u + 1)
        self.nc.scalar.copy(self.m.ws.hi[:, g, 0:self.cols], self.m.raw[:, 2 * j + g, 0:self.cols]).then_inc(
            self.s["hi_ready"], 1)

    def split_lo(self, dve, i, j, g):
        dve.wait_ge(self.s["hi_ready"], 4 * i + 2 * j + g + 1)
        self.nc.vector.tensor_tensor(self.m.ws.lo[:, g, 0:self.cols], self.m.raw[:, 2 * j + g, 0:self.cols],
                                     self.m.ws.hi[:, g, 0:self.cols].bitcast(FP32), ALU.subtract).then_inc(
            self.s["lo_ready"], 1)

    def multiply(self, pe, i, j, g, bank, x, k0, span, start, stop):
        pe.wait_ge(self.s["lo_ready"], 4 * i + 2 * j + g + 1)
        hi, lo, last = self.m.ws.hi, self.m.ws.lo, None
        for h in range(span.banks):
            cols = slice(h * span.width, (h + 1) * span.width)
            for k in range(self.k_tiles):
                w = slice(k * P, (k + 1) * P)
                for n, (a, b) in enumerate(((hi, x.hi), (hi, x.lo), (lo, x.hi))):
                    last = self.nc.tensor.matmul(self.m.ps[:, bank + h, 0:span.width], a[:, g, w], b[:, k0 + k, cols],
                                                 start=(start and k == 0 and n == 0),
                                                 stop=(stop and k == self.k_tiles - 1 and n == 2))
        last.then_inc(self.s["unit_done"], 1)

    def rounds(self, eng, body):
        with eng.Fori(0, self.n // 2 - 1) as i:
            for j in range(2):
                body(i, j, True)
        for j in range(2):
            body(self.n // 2 - 1, j, j == 0)

    def ahead(self, i, j):
        return (i, 1) if j == 0 else (i + 1, 0)


def conv_ffn_stage(nc, m, layer, weights):
    pads = [[m.work[:, 4 * j + g, 0:T1 + 2] for g in range(2)] for j in range(2)]
    convs = [[m.work[:, 4 * j + 2 + g, 0:T1] for g in range(2)] for j in range(2)]
    flat = lambda ap: ap.rearrange("p a t -> p (a t)")
    with stage(nc, f"ffn_in{layer}", *Units.SIGNALS, "emptied", "evacuated", "convolved", "gelu",
               "pads_free", "own", "product", "hidden_hi", "hidden_lo") as (block, s):
        un = Units(nc, m, s, weights, FT, KT)

        @block.sync
        def _(sp):
            un.load_all(sp)

        @block.tensor
        def _(pe):
            pe.sem_inc(s["unit_done"], 2)
            with pe.Fori(0, FT // 2) as i:
                for j in range(2):
                    pe.wait_ge(s["emptied"], 2 * i + j + 1)
                    for g in range(2):
                        un.multiply(pe, i, j, g, 4 * j + 2 * g, m.xs, 0, S1, True, True)

        @block.scalar
        def _(act):
            act.sem_inc(s["emptied"], 2)
            un.split_hi(act, 0, 0, 0)
            un.split_hi(act, 0, 0, 1)

            def body(i, j, more):
                t = 2 * i + j
                if more:
                    for g in range(2):
                        un.split_hi(act, *un.ahead(i, j), g)
                act.wait_ge(s["unit_done"], 2 * t + 4)
                act.wait_ge(s["pads_free"], t + 1)
                act.wait_ge(s["hidden_lo"], t + 1)
                nc.scalar.copy(S1.sbuf(pads[j][0][:, 2:2 + T1]), S1.psum(m.ps, 4 * j)).then_inc(s["evacuated"], 1)
                nc.scalar.copy(S1.sbuf(pads[j][1][:, 2:2 + T1]), S1.psum(m.ps, 4 * j + 2)).then_inc(s["emptied"], 1)
                act.wait_ge(s["convolved"], t + 1)
                nc.scalar.activation(convs[j][0], convs[j][0], ACT.Gelu_apprx_tanh).then_inc(s["gelu"], 1)
                act.wait_ge(s["product"], t + 1)
                nc.scalar.copy(flat(m.hs.hi[:, bass.ds(t, 1), :]), convs[j][1]).then_inc(s["hidden_hi"], 1)

            un.rounds(act, body)

        @block.vector
        def _(dve):
            for j in range(2):
                for g in range(2):
                    nc.vector.memset(pads[j][g][:, 0:2], 0.0).then_inc(s["own"], 1)
            dve.wait_ge(s["own"], 4)
            dve.sem_inc(s["pads_free"], 2)
            dve.sem_inc(s["hidden_lo"], 2)
            un.split_lo(dve, 0, 0, 0)
            un.split_lo(dve, 0, 0, 1)

            def body(i, j, more):
                t = 2 * i + j
                own = Own(dve, s["own"], 4 * t + 4)
                if more:
                    for g in range(2):
                        un.split_lo(dve, *un.ahead(i, j), g)
                for g in range(2):
                    if g == 0:
                        dve.wait_ge(s["evacuated"], t + 1)
                    else:
                        dve.wait_ge(s["emptied"], t + 3)
                    c, x = convs[j][g], pads[j][g]
                    own.then(nc.vector.tensor_scalar(c, x[:, 0:T1], m.col(f"f_conv_w{layer}_0", t + g * FT),
                                                     m.col(f"f_conv_b{layer}", t + g * FT), ALU.mult, ALU.add))
                    own.wait()
                    own.then(nc.vector.scalar_tensor_tensor(c, x[:, 1:1 + T1], m.col(f"f_conv_w{layer}_1", t + g * FT),
                                                            c, ALU.mult, ALU.add))
                    own.wait()
                    nc.vector.scalar_tensor_tensor(c, x[:, 2:2 + T1], m.col(f"f_conv_w{layer}_2", t + g * FT),
                                                   c, ALU.mult, ALU.add).then_inc((s["convolved"], s["pads_free"])[g], 1)
                dve.wait_ge(s["gelu"], t + 1)
                dve.wait_ge(s["pads_free"], t + 3)
                nc.vector.tensor_tensor(convs[j][1], convs[j][0], convs[j][1], ALU.mult).then_inc(s["product"], 1)
                dve.wait_ge(s["hidden_hi"], t + 1)
                nc.vector.tensor_tensor(flat(m.hs.lo[:, bass.ds(t, 1), :]), convs[j][1],
                                        flat(m.hs.hi[:, bass.ds(t, 1), :]).bitcast(FP32), ALU.subtract).then_inc(
                    s["hidden_lo"], 1)
                assert own.n == 4

            un.rounds(dve, body)


def swiglu_stage(nc, m, name, weights):
    silu = [m.work[:, j, 0:SEQ] for j in range(2)]
    prod = [m.work[:, 2 + j, 0:SEQ] for j in range(2)]
    flat = lambda ap: ap.rearrange("p a t -> p (a t)")
    with stage(nc, name, *Units.SIGNALS, "silu_ready", "product", "hidden_hi", "hidden_lo") as (block, s):
        un = Units(nc, m, s, weights, FT2, KT)

        @block.sync
        def _(sp):
            un.load_all(sp)

        @block.tensor
        def _(pe):
            pe.sem_inc(s["unit_done"], 2)
            with pe.Fori(0, FT2 // 2) as i:
                for j in range(2):
                    pe.wait_ge(s["product"], 2 * i + j + 1)
                    for g in range(2):
                        un.multiply(pe, i, j, g, 2 * j + g, m.xs, 0, S2, True, True)

        @block.scalar
        def _(act):
            un.split_hi(act, 0, 0, 0)
            un.split_hi(act, 0, 0, 1)

            def body(i, j, more):
                t = 2 * i + j
                if more:
                    for g in range(2):
                        un.split_hi(act, *un.ahead(i, j), g)
                act.wait_ge(s["unit_done"], 2 * t + 4)
                nc.scalar.activation(silu[j], m.ps[:, 2 * j, :], ACT.Silu).then_inc(s["silu_ready"], 1)
                act.wait_ge(s["product"], t + 3)
                nc.scalar.copy(flat(m.hs.hi[:, bass.ds(t, 1), :]), prod[j]).then_inc(s["hidden_hi"], 1)

            un.rounds(act, body)

        @block.vector
        def _(dve):
            dve.sem_inc(s["product"], 2)
            un.split_lo(dve, 0, 0, 0)
            un.split_lo(dve, 0, 0, 1)

            def body(i, j, more):
                t = 2 * i + j
                if more:
                    for g in range(2):
                        un.split_lo(dve, *un.ahead(i, j), g)
                dve.wait_ge(s["silu_ready"], t + 1)
                nc.vector.tensor_tensor(prod[j], silu[j], m.ps[:, 2 * j + 1, :], ALU.mult).then_inc(s["product"], 1)
                dve.wait_ge(s["hidden_hi"], t + 1)
                nc.vector.tensor_tensor(flat(m.hs.lo[:, bass.ds(t, 1), :]), prod[j],
                                        flat(m.hs.hi[:, bass.ds(t, 1), :]).bitcast(FP32), ALU.subtract).then_inc(
                    s["hidden_lo"], 1)

            un.rounds(dve, body)


def split_out_stage(nc, m, name, weights, k_tiles, hidden, span, x, y_scale, x_scale):
    half = k_tiles // 2
    with stage(nc, name, *Units.SIGNALS, "emptied") as (block, s):
        un = Units(nc, m, s, weights, KT, half)

        @block.sync
        def _(sp):
            un.load_all(sp)

        @block.tensor
        def _(pe):
            pe.sem_inc(s["unit_done"], 2)
            with pe.Fori(0, KT // 2) as i:
                for j in range(2):
                    pe.wait_ge(s["emptied"], 2 * i + j + 1)
                    if span.banks == 1:
                        for g in range(2):
                            un.multiply(pe, i, j, g, 4 * j, hidden, g * half, span, g == 0, g == 1)
                    else:
                        for g in range(2):
                            un.multiply(pe, i, j, g, 4 * j, hidden, g * half, span, g == 0, g == 1)

        @block.scalar
        def _(act):
            un.split_hi(act, 0, 0, 0)
            un.split_hi(act, 0, 0, 1)

            def body(i, j, more):
                if more:
                    for g in range(2):
                        un.split_hi(act, *un.ahead(i, j), g)

            un.rounds(act, body)

        @block.vector
        def _(dve):
            dve.sem_inc(s["emptied"], 2)
            un.split_lo(dve, 0, 0, 0)
            un.split_lo(dve, 0, 0, 1)

            def body(i, j, more):
                t = 2 * i + j
                if more:
                    for g in range(2):
                        un.split_lo(dve, *un.ahead(i, j), g)
                xt = span.sbuf(x[:, bass.ds(t, 1), :].rearrange("p a t -> p (a t)"))
                dve.wait_ge(s["unit_done"], 2 * t + 4)
                if y_scale != 1.0:
                    assert x_scale == 1.0
                    nc.vector.scalar_tensor_tensor(xt, span.psum(m.ps, 4 * j), y_scale, xt, ALU.mult, ALU.add).then_inc(
                        s["emptied"], 1)
                else:
                    nc.vector.scalar_tensor_tensor(xt, xt, x_scale, span.psum(m.ps, 4 * j), ALU.mult, ALU.add).then_inc(
                        s["emptied"], 1)

            un.rounds(dve, body)


def forget_stage(nc, m, d):
    w = m.ring[:, 0, 0:KT * HEADS1]
    soft, low, c = [m.work[0:HEADS1, k, 0:T1] for k in range(3)]
    logits = S1.psum(m.ps, 0, rows=HEADS1)
    bias = m.col("kv_f_b", 0, HEADS1)
    with stage(nc, "forget", "loaded", "projected", "soft_own", "soft_ready", "own", "c_ready", "stored") as (block, s):
        @block.sync
        def _(sp):
            sp.dma_start(w, d["forget_w"]).then_inc(s["loaded"], 16)
            sp.wait_ge(s["c_ready"], 1)
            sp.dma_start(m.c_dram, c).then_inc(s["stored"], 16)
            sp.wait_ge(s["stored"], 16)

        @block.tensor
        def _(pe):
            pe.wait_ge(s["loaded"], 16)
            project(nc, m.ps, 0, w, lambda k: m.x[:, k, :], KT, S1, rows=HEADS1).then_inc(s["projected"], 1)

        @block.scalar
        def _(act):
            own = Own(act, s["soft_own"])
            act.wait_ge(s["projected"], 1)
            own.then(nc.scalar.activation(S1.sbuf(soft), logits, ACT.Abs, bias=bias))
            own.wait()
            own.then(nc.scalar.activation(soft, soft, ACT.Exp, scale=-1.0))
            own.wait()
            nc.scalar.activation(soft, soft, ACT.Ln, bias=1.0).then_inc(s["soft_ready"], 1)

        @block.vector
        def _(dve):
            own = Own(dve, s["own"])
            dve.wait_ge(s["soft_own"], 1)
            own.then(nc.vector.tensor_scalar(S1.sbuf(low), logits, bias, 0.0, ALU.add, ALU.min))
            own.wait()
            dve.wait_ge(s["soft_ready"], 1)
            own.then(nc.vector.tensor_tensor(low, low, soft, ALU.subtract))
            own.wait()
            own.then(nc.vector.tensor_scalar(low, low, -1.0 / SCALE, None, ALU.mult))
            own.then(nc.vector.memset(soft, 1.0))
            own.wait()
            nc.vector.tensor_tensor_scan(c, soft, low, 0.0, ALU.mult, ALU.add).then_inc(s["c_ready"], 1)


def attention_stage(nc, m, d):
    PAIRS = HEADS1 // 2
    NQ = -(-T1 // QB)
    rows_of = lambda i: min(QB, T1 - i * QB)
    units = [(hh, i) for hh in range(2) for i in range(NQ)]
    NU = len(units)
    ring = [m.ring[:, j, :] for j in range(2)]
    qT, kT, vT, gate = [m.work[:, k, 0:T1] for k in range(4)]
    v = m.wide[:, 0:NQ * P].rearrange("p (n f) -> p n f", f=P)
    prob = [m.wide[:, 640 + 528 * b:640 + 528 * b + T1] for b in range(2)]
    probT = [m.wide[:, 1696 + 640 * b:1696 + 640 * (b + 1)] for b in range(2)]
    crow = [m.crow[0:1, 2 * T1 * b:2 * T1 * (b + 1)].rearrange("p (h t) -> p h t", t=T1) for b in range(2)]
    out = m.big[:, 0:KT * T1].rearrange("p (n t) -> p n t", t=T1)
    peak = [m.stat[:, b:b + 1] for b in range(2)]
    shift = [m.stat[:, 2 + b:3 + b] for b in range(2)]
    total = [m.stat[:, 4 + b:5 + b] for b in range(2)]
    scores = [m.ps[:, 2 + 2 * b:4 + 2 * b, :].rearrange("p b t -> p (b t)") for b in range(2)]
    with stage(nc, "attend", "loaded0", "loaded1", "projected", "evacuated", "v_psum", "v_ready", "scored",
               "shift_ready", "exp_done", "prob_ready", "probT_psum", "probT_ready", "out_psum", "out_done",
               "own") as (block, s):
        loaded = (s["loaded0"], s["loaded1"])

        @block.sync
        def _(sp):
            for j in range(2):
                sp.dma_start(ring[j], d["attn_w"][j]).then_inc(loaded[j], 16)
                sp.dma_start(crow[j], m.c_dram[2 * j:2 * j + 2, :].rearrange("(a h) t -> a h t", a=1)).then_inc(loaded[j], 16)
            with sp.Fori(1, PAIRS // 2) as i:
                for j in range(2):
                    sp.wait_ge(s["out_done"], NU * (2 * i + j - 1) + 1)
                    sp.dma_start(ring[j], d["attn_w"][2 * i + j]).then_inc(loaded[j], 16)
                    sp.dma_start(crow[j], m.c_dram.rearrange("(n h) t -> n h t", h=2)[bass.ds(2 * i + j, 1)]).then_inc(
                        loaded[j], 16)

        @block.tensor
        def _(pe):
            def score(j, u):
                hh, i = units[u]
                n, nk = rows_of(i), min((i + 1) * QB, T1)
                lo = 64 * hh
                for a, b in ((0, min(nk, 512)), (512, nk)):
                    if b <= a:
                        continue
                    dst = scores[u % 2][0:n, a:b]
                    diag = b > i * QB >= a
                    nc.tensor.matmul(dst, qT[lo:lo + HD, i * QB:i * QB + n], kT[lo:lo + HD, a:b], start=True, stop=False)
                    last = nc.tensor.matmul(dst, m.ones[0:1, 0:n], crow[j][0:1, hh, a:b], start=False, stop=not diag)
                    if diag:
                        last = nc.tensor.matmul(scores[u % 2][0:n, i * QB:nk], m.ident[0:n, 0:n],
                                                m.causal[0:n, 0:n], start=False, stop=True)
                last.then_inc(s["scored"], 1)

            with pe.Fori(0, PAIRS // 2) as it:
                for j in range(2):
                    t = 2 * it + j
                    pe.wait_ge(loaded[j], 32 * it + 32)
                    for g in range(4):
                        if g == 3:
                            pe.wait_ge(s["out_done"], NU * t + 1)
                        project(nc, m.ps, 2 * g, ring[j][:, g * KT * P:(g + 1) * KT * P], lambda k: m.x[:, k, :], KT,
                                S1).then_inc(s["projected"], 1)
                    pe.wait_ge(s["evacuated"], 4 * t + 3)
                    for n in range(NQ):
                        r = rows_of(n)
                        dst = m.ps[0:r, 0, n * P:(n + 1) * P] if n < 4 else m.ps[0:r, 1, 0:P]
                        last = nc.tensor.transpose(dst, vT[:, n * QB:n * QB + r], m.ident[:, :])
                    last.then_inc(s["v_psum"], 1)
                    score(j, 0)
                    for u, (hh, i) in enumerate(units):
                        n = rows_of(i)
                        if u + 1 < NU:
                            score(j, u + 1)
                        if u == 0:
                            pe.wait_ge(s["v_ready"], t + 1)
                            pe.wait_ge(s["evacuated"], 4 * t + 4)
                        pe.wait_ge(s["prob_ready"], NU * t + u + 1)
                        for b in range(i + 1):
                            r = rows_of(b)
                            dst, src, one = (m.ps[0:r, u % 2, b * n:(b + 1) * n],
                                             prob[u % 2][0:n, b * QB:b * QB + r], m.ident[0:n, 0:n])
                            last = nc.tensor.transpose(dst, src, one) if n == QB else nc.tensor.matmul(
                                dst, src, one, start=True, stop=True)
                        last.then_inc(s["probT_psum"], 1)
                        pe.wait_ge(s["probT_ready"], NU * t + u + 1)
                        if u >= 2:
                            pe.wait_ge(s["out_done"], NU * t + u)
                        for b in range(i + 1):
                            r = rows_of(b)
                            last = nc.tensor.matmul(m.ps[64 * hh:64 * hh + HD, 6 + u % 2, 0:n],
                                                    v[0:r, b, 64 * hh:64 * hh + HD], probT[u % 2][0:r, b * n:(b + 1) * n],
                                                    start=(b == 0), stop=(b == i))
                        last.then_inc(s["out_psum"], 1)

        @block.scalar
        def _(act):
            def exponentiate(t, u):
                hh, i = units[u]
                n, nk = rows_of(i), min((i + 1) * QB, T1)
                act.wait_ge(s["shift_ready"], NU * t + u + 1)
                nc.scalar.activation(prob[u % 2][0:n, 0:nk], scores[u % 2][0:n, 0:nk], ACT.Exp, scale=SCALE,
                                     bias=shift[u % 2][0:n], accum_out=total[u % 2][0:n]).then_inc(s["exp_done"], 1)

            with act.Fori(0, PAIRS // 2) as it:
                for j in range(2):
                    t = 2 * it + j
                    for g, dst in enumerate((qT, kT, vT)):
                        act.wait_ge(s["projected"], 4 * t + g + 1)
                        nc.scalar.copy(S1.sbuf(dst), S1.psum(m.ps, 2 * g)).then_inc(s["evacuated"], 1)
                    act.wait_ge(s["projected"], 4 * t + 4)
                    nc.scalar.activation(S1.sbuf(gate), S1.psum(m.ps, 6), ACT.Sigmoid).then_inc(s["evacuated"], 1)
                    exponentiate(t, 0)
                    for u, (hh, i) in enumerate(units):
                        if u + 1 < NU:
                            exponentiate(t, u + 1)
                        n = rows_of(i)
                        act.wait_ge(s["probT_psum"], NU * t + u + 1)
                        full = n * (i + 1) if n == QB else n * i
                        ins = nc.scalar.copy(probT[u % 2][:, 0:full], m.ps[:, u % 2, 0:full])
                        if n < QB:
                            ins = nc.scalar.copy(probT[u % 2][0:n, full:full + n], m.ps[0:n, u % 2, full:full + n])
                        ins.then_inc(s["probT_ready"], 1)

        @block.vector
        def _(dve):
            OWN = 2 * NU

            def stabilise(t, u):
                hh, i = units[u]
                n, nk = rows_of(i), min((i + 1) * QB, T1)
                dve.wait_ge(s["scored"], NU * t + u + 1)
                nc.vector.reduce_max(peak[u % 2][0:n], scores[u % 2][0:n, 0:nk], AX.X).then_inc(s["own"], 1)
                dve.wait_ge(s["own"], OWN * t + (1 if u == 0 else 2 * u))
                nc.vector.tensor_scalar(shift[u % 2][0:n], peak[u % 2][0:n], -SCALE, None, ALU.mult).then_inc(
                    s["shift_ready"], 1)

            dve.sem_inc(s["out_done"], 1)
            with dve.Fori(0, PAIRS // 2) as it:
                for j in range(2):
                    t = 2 * it + j
                    dve.wait_ge(s["v_psum"], t + 1)
                    nc.vector.tensor_copy(v[:, 0:4, :], m.ps[:, 0, :].rearrange("p (n f) -> p n f", f=P))
                    nc.vector.tensor_copy(v[0:T1 - 4 * QB, 4, :], m.ps[0:T1 - 4 * QB, 1, 0:P]).then_inc(s["v_ready"], 1)
                    stabilise(t, 0)
                    for u, (hh, i) in enumerate(units):
                        n, nk = rows_of(i), min((i + 1) * QB, T1)
                        if u + 1 < NU:
                            stabilise(t, u + 1)
                        dve.wait_ge(s["exp_done"], NU * t + u + 1)
                        nc.vector.reciprocal(total[u % 2][0:n], total[u % 2][0:n]).then_inc(s["own"], 1)
                        dve.wait_ge(s["own"], OWN * t + min(2 * u + 3, 2 * NU))
                        nc.vector.tensor_scalar(prob[u % 2][0:n, 0:nk], prob[u % 2][0:n, 0:nk], total[u % 2][0:n], None,
                                                ALU.mult).then_inc(s["prob_ready"], 1)
                        dve.wait_ge(s["out_psum"], NU * t + u + 1)
                        dve.wait_ge(s["evacuated"], 4 * t + 4)
                        rows = slice(64 * hh, 64 * hh + HD)
                        nc.vector.tensor_tensor(out[rows, bass.ds(t, 1), i * QB:i * QB + n].rearrange("p a t -> p (a t)"),
                                                m.ps[rows, 6 + u % 2, 0:n], gate[rows, i * QB:i * QB + n],
                                                ALU.mult).then_inc(s["out_done"], 1)


def part_one(nc, m, d):
    x_tile = lambda k: m.x[:, k, :]
    y_tile = lambda k: m.y[:, k, :]
    for l in range(2):
        with ExitStack() as ctx:
            mixer_memory(nc, ctx, m, f"m{l}", False)
            h_lru = m.big[0:LRU, 0:N_LRU * T1].rearrange("p (n t) -> p n t", t=T1)
            h_att = m.big[:, 0:KT * T1].rearrange("p (n t) -> p n t", t=T1)
            if l == 0:
                lru_stage(nc, m, d)
                out_stage(nc, m, "lru_out", d["lru_out"], N_LRU, LRU, lambda k: h_lru[:, k, :], S1, m.x, 1.0, ALPHA, m.x)
            else:
                forget_stage(nc, m, d)
                attention_stage(nc, m, d)
                out_stage(nc, m, "attn_out", d["attn_out"], KT, P, lambda k: h_att[:, k, :], S1, m.x, 1.0, ALPHA, m.x)
        with ExitStack() as ctx:
            ffn_memory(nc, ctx, m, f"f{l}", S1)
            norm_stage(nc, m, f"ln1_{l}", x_tile, x_tile, f"ln1_g{l}", f"ln1_b{l}", LN_EPS, S1, True, m.xs)
            conv_ffn_stage(nc, m, l, d["ffn_in"][l])
            split_out_stage(nc, m, f"ffn_out{l}", d["ffn_out"][l], FT, m.hs, S1, m.x, 1.0, ALPHA)
            norm_stage(nc, m, f"ln2_{l}", x_tile, x_tile, f"ln2_g{l}", f"ln2_b{l}", LN_EPS, S1, True)


class Signals:

    def __init__(self, sem, names):
        self.sem, self.names, self.given = sem, names, 0

    def start(self, eng):
        eng.sem_inc(self.sem, 1)

    def give(self, ins, name):
        assert self.names[self.given % len(self.names)] == name, (name, self.names[self.given % len(self.names)])
        self.given += 1
        ins.then_inc(self.sem, 1)

    def wait(self, eng, rnd, name):
        eng.wait_ge(self.sem, len(self.names) * rnd + self.names.index(name) + 2)

    def wait_round(self, eng, rnd):
        eng.wait_ge(self.sem, len(self.names) * rnd + 1)


def mix_in_stage(nc, m, layer, d):
    ring = [m.ring[:, j, 0:KT * P] for j in range(2)]
    ring2 = [m.ring[:, j, KT * P:2 * KT * P] for j in range(2)]
    wv = m.ring[:, 0, 2 * KT * P:4 * KT * P]
    NR, NO = 10, 16
    rwkv = m.big[:, 0:NR * SEQ].rearrange("p (n t) -> p n t", t=SEQ)
    pads = [m.work[:, j, 0:SEQ + 1] for j in range(2)]
    diff = [m.work[:, 2 + j, 0:SEQ] for j in range(2)]
    y = lambda k: m.y[:, k, 0:SEQ]
    flat = lambda ap: ap.rearrange("p a t -> p (a t)")
    with stage(nc, f"mix_in{layer}", "loaded0", "loaded1", "projected", "pad_ready", "shifted", "own",
               "loaded2", "loaded3", "projected2", "emptied2", "loaded_v", "v_psum", "v_ready") as (block, s):
        @block.sync
        def _(sp):
            sp.dma_start(wv, d["ret_v"][layer]).then_inc(s["loaded_v"], 16)
            load_tiles(sp, nc, ring, d["rwkv_in"][layer], NR, (s["loaded0"], s["loaded1"]), s["projected"])
            load_tiles(sp, nc, ring2, d["other_in"][layer], NO, (s["loaded2"], s["loaded3"]), s["projected2"])

        @block.tensor
        def _(pe):
            with pe.Fori(0, NR // 2) as i:
                for j in range(2):
                    pe.wait_ge((s["loaded0"], s["loaded1"])[j], 16 * i + 16)
                    pe.wait_ge(s["pad_ready"], 2 * i + j + 1)
                    project(nc, m.ps, j, ring[j], y, KT, S2).then_inc(s["projected"], 1)
            with pe.Fori(0, NO // 2) as i:
                for j in range(2):
                    pe.wait_ge((s["loaded2"], s["loaded3"])[j], 16 * i + 16)
                    pe.wait_ge(s["emptied2"], 2 * i + j + 1)
                    project(nc, m.ps, 2 + j, ring2[j], y, KT, S2).then_inc(s["projected2"], 1)
            pe.wait_ge(s["loaded_v"], 16)
            for n in range(4):
                for k in range(KT):
                    last = nc.tensor.matmul(m.ps[:, 4 + n, 0:256], m.y[:, k, n * P:(n + 1) * P],
                                            wv[:, k * 256:(k + 1) * 256], start=(k == 0), stop=(k == KT - 1))
            last.then_inc(s["v_psum"], 1)

        @block.scalar
        def _(act):
            act.sem_inc(s["pad_ready"], 2)
            act.sem_inc(s["emptied2"], 2)
            with act.Fori(0, NR // 2) as i:
                for j in range(2):
                    t = 2 * i + j
                    act.wait_ge(s["projected"], t + 1)
                    act.wait_ge(s["shifted"], t + 1)
                    nc.scalar.copy(pads[j][:, 1:1 + SEQ], m.ps[:, j, :]).then_inc(s["pad_ready"], 1)
            with act.Fori(0, NO // 2) as i:
                for j in range(2):
                    t = 2 * i + j
                    act.wait_ge(s["projected2"], t + 1)
                    nc.scalar.copy(flat(m.other[:, bass.ds(t, 1), :]), m.ps[:, 2 + j, :]).then_inc(s["emptied2"], 1)

        @block.vector
        def _(dve):
            for j in range(2):
                nc.vector.memset(pads[j][:, 0:1], 0.0).then_inc(s["own"], 1)
            dve.wait_ge(s["own"], 2)
            dve.sem_inc(s["shifted"], 2)
            with dve.Fori(0, NR // 2) as i:
                for j in range(2):
                    t = 2 * i + j
                    dve.wait_ge(s["pad_ready"], t + 3)
                    nc.vector.tensor_tensor(diff[j], pads[j][:, 0:SEQ], pads[j][:, 1:1 + SEQ],
                                            ALU.subtract).then_inc(s["own"], 1)
                    dve.wait_ge(s["own"], t + 3)
                    nc.vector.scalar_tensor_tensor(flat(rwkv[:, bass.ds(t, 1), :]), diff[j], m.col(f"rwkv_mu{layer}", t),
                                                   pads[j][:, 1:1 + SEQ], ALU.mult, ALU.add).then_inc(s["shifted"], 1)
            dve.wait_ge(s["v_psum"], 1)
            nc.vector.tensor_copy(m.ret_v[:, :, :], m.ps[:, 4:8, 0:256]).then_inc(s["v_ready"], 1)


class Rwkv:

    def __init__(self, m):
        three = lambda ap: ap.rearrange("p (n t) -> p n t", t=SEQ)
        big, ring, wide, work = m.big, m.ring[:, :, :].rearrange("p a b -> p (a b)"), m.wide, m.work[:, :, :].rearrange("p a b -> p (a b)")
        N = 3 * SEQ
        at = lambda t, i: three(t[:, i:i + N])
        self.r, self.k, self.v = at(big, 0), at(big, N), at(big, 2 * N)
        self.lo = big[:, 3 * N:3 * N + SEQ]
        self.el = at(big, 5120)
        self.logw, self.cum, self.prev = at(big, 5120 + N), at(big, 5120 + 2 * N), at(big, 5120 + 3 * N)
        self.a, self.g, self.kk, self.neg = at(ring, 0), at(ring, N), at(ring, 2 * N), at(ring, 3 * N)
        self.square = [ring[:, 4 * N + j * SEQ:4 * N + (j + 1) * SEQ] for j in range(2)]
        self.prod = [ring[:, 4 * N + (2 + j) * SEQ:4 * N + (3 + j) * SEQ] for j in range(2)]
        self.bonus = at(wide, 0)
        self.lo_w = wide[:, N:N + 768]
        self.mv = wide[:, N + 768:N + 768 + SEQ]
        self.mv_pad = wide[:, N + 768 + SEQ:N + 768 + 2 * SEQ]
        S = 3 * P
        sl = lambda t, i: t[:, i:i + S].rearrange("p (n t) -> p n t", t=P)
        spare = m.y[:, :, :].rearrange("p a b -> p (a b)")[:, 3 * T1:8 * T1]
        self.st_a, self.st_b, self.st_k, self.st_r, self.st_v = [sl(spare, i * S) for i in range(5)]
        self.tok_b, self.tok_v, self.x = [work[:, i * S:(i + 1) * S] for i in range(3)]
        self.tok_k = [work[:, (3 + i) * S:(4 + i) * S] for i in range(2)]
        self.u = [work[:, (5 + i) * S:(6 + i) * S] for i in range(2)]
        self.state = sl(work, 7 * S)
        self.end = [sl(work, (8 + i) * S) for i in range(2)]
        M = 6 * P
        free = [big[:, 5120 + N + i * M:5120 + N + (i + 1) * M] for i in range(7)]
        free += [ring[:, 3 * N + i * M:3 * N + (i + 1) * M] for i in range(4)]
        free += [wide[:, N:N + M]]
        (self.E1, self.E2, self.GA, self.GB, self.HA, self.HB, self.ZA, self.ZB, self.Z, self.MAK, self.MRB,
         self.MRK) = free
        assert 5120 + N + 7 * M <= 24 * T1 and 3 * N + 4 * M <= 8192 and 10 * S <= 8 * 532


def rwkv_prepare_stage(nc, m, layer, d):
    w = Rwkv(m)
    C, LW = 3, layer == 1
    col = lambda n, c: m.col(f"rwkv_{n}{layer}", c)
    with stage(nc, f"rwkv_prep{layer}", "loaded", "lo_ready", "mv_ready", "z_psum", "z_out", "cum_ready", "exp_out", "sq_ready",
               "ss_psum", "ss_ready", "root_ready", "prod_ready", "bonus_psum", "bonus_out", "v_saved", "own",
               "scaled") as (block, s):
        @block.sync
        def _(sp):
            sp.dma_start(w.lo_w, d["rwkv_lo"][layer]).then_inc(s["loaded"], 16)
            sp.wait_ge(s["loaded"], 16)

        @block.tensor
        def _(pe):
            pe.wait_ge(s["loaded"], 16)
            pe.wait_ge(s["lo_ready"], 2)
            if LW:
                pe.wait_ge(s["mv_ready"], 1)
            for c in range(C):
                b = 4 * (c % 2)
                if c == 2:
                    pe.wait_ge(s["z_out"], 1)
                for q, (lo, n) in enumerate(((0, 32), (32, 32), (64, 64))):
                    last = nc.tensor.matmul(m.ps[:, b + q, :], w.lo_w[lo:lo + n, c * P:(c + 1) * P], w.lo[lo:lo + n, :],
                                            start=True, stop=True)
                if LW:
                    last = nc.tensor.matmul(m.ps[:, b + 3, :], w.lo_w[32:48, 384 + c * P:384 + (c + 1) * P],
                                            w.mv[32:48, :], start=True, stop=True)
                last.then_inc(s["z_psum"], 1)
            pe.wait_ge(s["z_out"], C)
            for c in range(C):
                pe.wait_ge(s["sq_ready"], c + 1)
                nc.tensor.matmul(m.ps[:, c, :], m.head_ones, w.square[c % 2], start=True, stop=True).then_inc(s["ss_psum"], 1)
                pe.wait_ge(s["prod_ready"], c + 1)
                nc.tensor.matmul(m.ps[:, 4 + c, :], m.head_ones, w.prod[c % 2], start=True, stop=True).then_inc(s["bonus_psum"], 1)

        @block.scalar
        def _(act):
            nc.scalar.activation(w.lo[0:32, :], w.lo[0:32, :], ACT.Tanh).then_inc(s["lo_ready"], 1)
            nc.scalar.activation(w.lo[64:128, :], w.lo[64:128, :], ACT.Sigmoid).then_inc(s["lo_ready"], 1)
            for c in range(C):
                b = 4 * (c % 2)
                act.wait_ge(s["z_psum"], c + 1)
                nc.scalar.activation(w.logw[:, c, :], m.ps[:, b, :], ACT.Sigmoid, bias=col("w0", c))
                nc.scalar.activation(w.a[:, c, :], m.ps[:, b + 1, :], ACT.Sigmoid, bias=col("a0", c))
                if LW:
                    nc.scalar.activation(w.neg[:, c, :], m.ps[:, b + 3, :], ACT.Sigmoid, bias=m.col("rwkv_v0", c))
                nc.scalar.copy(w.g[:, c, :], m.ps[:, b + 2, :]).then_inc(s["z_out"], 1)
            for c in range(C):
                act.wait_ge(s["cum_ready"], c + 1)
                nc.scalar.activation(w.prev[:, c, :], w.prev[:, c, :], ACT.Exp)
                nc.scalar.activation(w.el[:, c, :], w.cum[:, c, :], ACT.Exp)
                nc.scalar.activation(w.neg[:, c, :], w.cum[:, c, :], ACT.Exp, scale=-1.0).then_inc(s["exp_out"], 1)
            for c in range(C):
                act.wait_ge(s["ss_ready"], c + 1)
                nc.scalar.activation(w.logw[:, c, :], w.logw[:, c, :], ACT.Sqrt).then_inc(s["root_ready"], 1)

        @block.gpsimd
        def _(pool):
            if not LW:
                nc.gpsimd.tensor_copy(m.v_first[:, :, :], w.v).then_inc(s["v_saved"], 1)
                pool.wait_ge(s["v_saved"], 1)

        @block.vector
        def _(dve):
            own = Own(dve, s["own"])
            if LW:
                src = m.other[32:48, 15, :]
                own.then(nc.vector.memset(w.mv_pad[32:48, 0:1], 0.0))
                own.then(nc.vector.tensor_copy(w.mv_pad[32:48, 1:SEQ], src[:, 0:SEQ - 1]))
                own.wait()
                own.then(nc.vector.tensor_tensor(w.mv[32:48, :], w.mv_pad[32:48, 0:SEQ], src, ALU.subtract))
                own.wait()
                nc.vector.scalar_tensor_tensor(w.mv[32:48, :], w.mv[32:48, :],
                                               m.vec[32:48, COLS["rwkv_vres_mu"][0]:COLS["rwkv_vres_mu"][0] + 1], src,
                                               ALU.mult, ALU.add).then_inc(s["mv_ready"], 1)
            own.then(nc.vector.memset(m.reset, 1.0))
            own.wait()
            own.then(nc.vector.memset(m.reset.rearrange("p (n c) -> p n c", c=HD)[:, :, 0:1], 0.0))
            for c in range(C):
                dve.wait_ge(s["z_out"], c + 1)
                L, cum, k, v, r, a = (x[:, c, :] for x in (w.logw, w.cum, w.k, w.v, w.r, w.a))
                own.then(nc.vector.tensor_scalar(L, L, -math.exp(-0.5), None, ALU.mult))
                own.wait()
                own.then(nc.vector.tensor_tensor_scan(cum, m.reset, L, 0.0, ALU.mult, ALU.add))
                if LW:
                    sv = w.neg[:, c, :]
                    own.then(nc.vector.tensor_tensor(w.prev[:, c, :], m.v_first[:, c, :], v, ALU.subtract))
                    own.wait()
                    own.then(nc.vector.tensor_tensor(w.prev[:, c, :], w.prev[:, c, :], sv, ALU.mult))
                    own.wait()
                    own.then(nc.vector.tensor_tensor(v, v, w.prev[:, c, :], ALU.add))
                own.wait()
                nc.vector.tensor_tensor(w.prev[:, c, :], cum, L, ALU.subtract).then_inc(s["cum_ready"], 1)
                own.then(nc.vector.tensor_scalar(w.kk[:, c, :], k, col("k_k", c), None, ALU.mult))
                own.wait()
                if c >= 2:
                    dve.wait_ge(s["ss_psum"], c - 1)
                nc.vector.tensor_tensor(w.square[c % 2], w.kk[:, c, :], w.kk[:, c, :], ALU.mult).then_inc(s["sq_ready"], 1)
                if c >= 2:
                    dve.wait_ge(s["bonus_psum"], c - 1)
                own.then(nc.vector.tensor_scalar(w.prod[c % 2], a, -1.0, col("k_a", c), ALU.add, ALU.mult))
                own.wait()
                own.then(nc.vector.scalar_tensor_tensor(k, w.prod[c % 2], 1.0, k, ALU.add, ALU.mult))
                own.wait()
                nc.vector.scalar_tensor_tensor(w.prod[c % 2], r, col("r_k", c), k, ALU.mult, ALU.mult).then_inc(
                    s["prod_ready"], 1)
            for c in range(C):
                dve.wait_ge(s["ss_psum"], c + 1)
                nc.vector.tensor_scalar(w.logw[:, c, :], m.ps[:, c, :], 1e-24, None, ALU.max).then_inc(s["ss_ready"], 1)
                dve.wait_ge(s["bonus_psum"], c + 1)
                own.then(nc.vector.tensor_tensor(w.bonus[:, c, :], m.ps[:, 4 + c, :], w.v[:, c, :], ALU.mult))
            for c in range(C):
                kk, a, k, r, neg, n = (x[:, c, :] for x in (w.kk, w.a, w.k, w.r, w.neg, w.logw))
                dve.wait_ge(s["root_ready"], c + 1)
                own.then(nc.vector.reciprocal(n, n))
                own.wait()
                own.then(nc.vector.tensor_tensor(kk, kk, n, ALU.mult))
                own.wait()
                own.then(nc.vector.tensor_tensor(a, kk, a, ALU.mult))
                own.wait()
                dve.wait_ge(s["exp_out"], c + 1)
                nc.vector.tensor_tensor(a, a, neg, ALU.mult).then_inc(s["scaled"], 1)
                nc.vector.scalar_tensor_tensor(kk, kk, -1.0, w.prev[:, c, :], ALU.mult, ALU.mult).then_inc(s["scaled"], 1)
                nc.vector.tensor_tensor(k, k, neg, ALU.mult).then_inc(s["scaled"], 1)
                nc.vector.tensor_tensor(r, r, w.el[:, c, :], ALU.mult).then_inc(s["scaled"], 1)


def rwkv_recurrence_stage(nc, m, layer):
    w = Rwkv(m)
    H = 6
    half = lambda h: slice(64 * (h % 2), 64 * (h % 2) + 64)
    pair = lambda q: m.ps[:, 2 * q:2 * q + 2, 0:3 * P]
    set_psum = lambda q, h: m.ps[:, 2 * q + h % 2, (h // 2) * P:(h // 2 + 1) * P]
    block_of = lambda M, h: M[:, (h % 2 * 3 + h // 2) * P:(h % 2 * 3 + h // 2 + 1) * P]
    shaped = lambda M: M.rearrange("p (a b) -> p a b", a=2)
    four = lambda M: M.rearrange("p (a b c) -> p a b c", a=2, b=3)
    spread = lambda mask: mask.unsqueeze(1).unsqueeze(1).broadcast_to([P, 2, 3, P])
    with stage(nc, f"rwkv_rec{layer}", "made", "vec_out", "act_out", "staged", "ones_added") as (block, s):
        made = Signals(s["made"], ["tok", "ab", "ba", "ak", "g1", "h1", "z1", "rb", "g2", "h2", "z2", "rk", "g3", "z3", "t3",
                                "q3", "z4", "t4", "q4", "z5", "x0", "u0", "y0", "s0", "x1", "u1", "y1", "s1"])
        vec = Signals(s["vec_out"], ["tok_v", "GA", "E1", "E2", "HA", "MAK", "z1", "MRB", "z2", "MRK", "z3", "z4", "z5",
                                  "u0", "s0", "u1", "s1"])
        act_ = Signals(s["act_out"], ["tok_bk", "g1", "h1", "g2", "h2", "g3", "t3", "q3", "t4", "q4", "x0", "y0", "x1", "y1"])

        @block.gpsimd
        def _(pool):
            nc.gpsimd.memset(w.state, 0.0)
            nc.gpsimd.memset(w.x, 0.0)
            for c in range(2):
                nc.gpsimd.memset(w.u[c], 0.0)
                nc.gpsimd.memset(w.tok_k[c], 0.0)
            nc.gpsimd.memset(m.ident[0:1, 0:1], 1.0).then_inc(s["staged"], 1)
            with pool.Fori(0, 4) as t:
                made.wait_round(pool, t)
                for dst, src in ((w.st_a, w.kk), (w.st_b, w.a), (w.st_k, w.k), (w.st_r, w.r), (w.st_v, w.v)):
                    nc.gpsimd.tensor_copy(dst, src[:, :, bass.ds(t * P, P)]).then_inc(s["staged"], 1)
                vec.wait_round(pool, t)
                for c in range(2):
                    at_end = w.el.rearrange("p n (c s) -> p n c s", s=HD)[:, :, bass.ds(2 * t + c, 1), HD - 1]
                    nc.gpsimd.tensor_tensor(w.end[c], at_end.broadcast_to([P, 3, P]),
                                            m.head_ones.unsqueeze(1).broadcast_to([P, 3, P]), ALU.mult).then_inc(
                        s["staged"], 1)
                vec.wait(pool, t, "HA")
                nc.gpsimd.tensor_tensor(four(w.ZA), four(w.HA), spread(m.ident[:, :]), ALU.add).then_inc(s["ones_added"], 1)

        @block.tensor
        def _(pe):
            def batch(name, q, left, right):
                for h in range(H):
                    last = nc.tensor.matmul(set_psum(q, h), left(h), right(h), start=True, stop=True)
                made.give(last, name)

            feat = lambda x: (lambda h: x[half(h), h // 2, :])
            mat = lambda M: (lambda h: block_of(M, h))

            made.start(pe)
            with pe.Fori(0, 4) as t:
                pe.wait_ge(s["staged"], 7 * t + 8)
                act_.wait_round(pe, t)
                for b, src in enumerate((w.st_b, w.st_k, w.st_v)):
                    for c in range(3):
                        last = nc.tensor.transpose(m.ps[:, b, c * P:(c + 1) * P], src[:, c, :], m.ident[:, :])
                made.give(last, "tok")
                batch("ab", 2, feat(w.st_a), feat(w.st_b))
                batch("ba", 3, feat(w.st_b), feat(w.st_a))
                act_.wait(pe, t, "tok_bk")
                batch("ak", 0, feat(w.st_k), feat(w.st_a))
                vec.wait(pe, t, "tok_v")
                vec.wait(pe, t, "HA")
                batch("g1", 1, mat(w.HA), mat(w.GA))
                batch("h1", 2, mat(w.GA), mat(w.HA))
                act_.wait(pe, t, "g1")
                pe.wait_ge(s["ones_added"], t + 1)
                batch("z1", 3, mat(w.GB), mat(w.ZA))
                vec.wait(pe, t, "MAK")
                batch("rb", 0, feat(w.st_b), feat(w.st_r))
                act_.wait(pe, t, "h1")
                batch("g2", 1, mat(w.HB), mat(w.GB))
                batch("h2", 2, mat(w.GB), mat(w.HB))
                act_.wait(pe, t, "g2")
                vec.wait(pe, t, "z1")
                batch("z2", 3, mat(w.GA), mat(w.ZB))
                vec.wait(pe, t, "MRB")
                batch("rk", 0, feat(w.st_k), feat(w.st_r))
                act_.wait(pe, t, "h2")
                batch("g3", 1, mat(w.HA), mat(w.GA))
                act_.wait(pe, t, "g3")
                vec.wait(pe, t, "z2")
                batch("z3", 3, mat(w.GB), mat(w.ZA))
                vec.wait(pe, t, "z3")
                for h in range(H):
                    last = nc.tensor.transpose(set_psum(1, h), block_of(w.ZB, h), m.ident[:, :])
                made.give(last, "t3")
                batch("q3", 2, mat(w.E1), mat(w.ZB))
                act_.wait(pe, t, "q3")
                batch("z4", 3, mat(w.HA), mat(w.HB))
                vec.wait(pe, t, "z4")
                for h in range(H):
                    last = nc.tensor.transpose(set_psum(1, h), block_of(w.ZA, h), m.ident[:, :])
                made.give(last, "t4")
                batch("q4", 2, mat(w.E2), mat(w.ZA))
                act_.wait(pe, t, "q4")
                batch("z5", 3, mat(w.HA), mat(w.HB))
                vec.wait(pe, t, "z5")
                for c in range(2):
                    rows = slice(64 * c, 64 * c + 64)
                    if c == 1:
                        vec.wait(pe, t, "s0")
                    for n in range(3):
                        dst = m.ps[rows, 0, n * P:(n + 1) * P]
                        nc.tensor.matmul(dst, w.st_a[:, n, rows], w.state[:, n, :], start=True, stop=False)
                        for h in (2 * n, 2 * n + 1):
                            last = nc.tensor.matmul(m.ps[rows, 0, h * HD:(h + 1) * HD], block_of(w.MAK, h)[:, rows],
                                                    w.tok_v[:, h * HD:(h + 1) * HD], start=False, stop=(h % 2 == 1))
                    made.give(last, f"x{c}")
                    act_.wait(pe, t, f"x{c}")
                    for h in range(H):
                        last = nc.tensor.matmul(m.ps[rows, 1, h * HD:(h + 1) * HD], block_of(w.Z, h)[:, rows],
                                                w.x[:, h * HD:(h + 1) * HD], start=True, stop=True)
                    made.give(last, f"u{c}")
                    vec.wait(pe, t, f"u{c}")
                    if c == 1:
                        act_.wait(pe, t, "y0")
                    for n in range(3):
                        dst = m.ps[:, 2, n * HD:(n + 1) * HD]
                        nc.tensor.matmul(dst, w.state[:, n, :], w.st_r[:, n, rows], start=True, stop=False)
                        for h in (2 * n, 2 * n + 1):
                            dst, cols = m.ps[half(h), 2, n * HD:(n + 1) * HD], slice(h * HD, (h + 1) * HD)
                            nc.tensor.matmul(dst, w.u[c][:, cols], block_of(w.MRB, h)[:, rows], start=False, stop=False)
                            last = nc.tensor.matmul(dst, w.tok_v[:, cols], block_of(w.MRK, h)[:, rows], start=False, stop=True)
                    made.give(last, f"y{c}")
                    for n in range(3):
                        dst, cols = m.ps[:, 3, n * P:(n + 1) * P], slice(n * P, (n + 1) * P)
                        nc.tensor.matmul(dst, m.ident[:, :], w.state[:, n, :], start=True, stop=False)
                        nc.tensor.matmul(dst, w.tok_b[:, cols], w.u[c][:, cols], start=False, stop=False)
                        last = nc.tensor.matmul(dst, w.tok_k[c][:, cols], w.tok_v[:, cols], start=False, stop=True)
                    made.give(last, f"s{c}")

        @block.scalar
        def _(act):
            def take(t, name, src, dst, given=None):
                made.wait(act, t, name)
                act_.give(nc.scalar.copy(dst, src), given or name)

            act_.start(act)
            with act.Fori(0, 4) as t:
                made.wait(act, t, "tok")
                nc.scalar.copy(w.tok_b, m.ps[:, 0, 0:3 * P])
                nc.scalar.copy(w.tok_k[0][0:64, :], m.ps[0:64, 1, 0:3 * P])
                act_.give(nc.scalar.copy(w.tok_k[1][64:128, :], m.ps[64:128, 1, 0:3 * P]), "tok_bk")
                take(t, "g1", pair(1), shaped(w.GB))
                take(t, "h1", pair(2), shaped(w.HB))
                take(t, "g2", pair(1), shaped(w.GA))
                act.wait_ge(s["ones_added"], t + 1)
                take(t, "h2", pair(2), shaped(w.HA))
                take(t, "g3", pair(1), shaped(w.GB))
                take(t, "t3", pair(1), shaped(w.HA))
                take(t, "q3", pair(2), shaped(w.HB))
                take(t, "t4", pair(1), shaped(w.HA))
                take(t, "q4", pair(2), shaped(w.HB))
                for c in range(2):
                    rows = slice(64 * c, 64 * c + 64)
                    take(t, f"x{c}", m.ps[rows, 0, 0:3 * P], w.x[rows, :])
                    take(t, f"y{c}", m.ps[:, 2, 0:192].rearrange("p (n t) -> p n t", t=HD),
                         w.v[:, :, bass.ds(t * P + 64 * c, HD)])

        @block.vector
        def _(dve):
            def masked(t, name, q, mask, dst, given):
                made.wait(dve, t, name)
                vec.give(nc.vector.tensor_tensor(four(dst), m.ps[:, 2 * q:2 * q + 2, 0:3 * P].rearrange(
                    "p a (b c) -> p a b c", c=P), spread(mask), ALU.mult), given)

            def added(t, name, old, dst):
                made.wait(dve, t, name)
                vec.give(nc.vector.tensor_tensor(shaped(dst), pair(3), shaped(old), ALU.add), name)

            vec.start(dve)
            with dve.Fori(0, 4) as t:
                made.wait(dve, t, "tok")
                vec.give(nc.vector.tensor_copy(w.tok_v, m.ps[:, 2, 0:3 * P]), "tok_v")
                masked(t, "ab", 2, m.low16, w.GA, "GA")
                masked(t, "ab", 2, m.edge16, w.E1, "E1")
                masked(t, "ab", 2, m.edge32, w.E2, "E2")
                masked(t, "ba", 3, m.up16, w.HA, "HA")
                masked(t, "ak", 0, m.strict64, w.MAK, "MAK")
                dve.wait_ge(s["ones_added"], t + 1)
                added(t, "z1", w.ZA, w.ZB)
                masked(t, "rb", 0, m.upto64, w.MRB, "MRB")
                vec.wait(dve, t, "z1")
                added(t, "z2", w.ZB, w.ZA)
                masked(t, "rk", 0, m.upto64, w.MRK, "MRK")
                vec.wait(dve, t, "z2")
                added(t, "z3", w.ZA, w.ZB)
                vec.wait(dve, t, "z3")
                added(t, "z4", w.ZB, w.ZA)
                vec.wait(dve, t, "z4")
                added(t, "z5", w.ZA, w.Z)
                for c in range(2):
                    rows = slice(64 * c, 64 * c + 64)
                    made.wait(dve, t, f"u{c}")
                    vec.give(nc.vector.tensor_copy(w.u[c][rows, :], m.ps[rows, 1, 0:3 * P]), f"u{c}")
                    made.wait(dve, t, f"s{c}")
                    vec.give(nc.vector.tensor_tensor(w.state, m.ps[:, 3, 0:3 * P].rearrange("p (n t) -> p n t", t=P),
                                                     w.end[c], ALU.mult), f"s{c}")


def rwkv_finish_stage(nc, m, layer):
    w = Rwkv(m)
    C, col = 3, lambda n, c: m.col(f"rwkv_{n}{layer}", c)
    with stage(nc, f"rwkv_fin{layer}", "mean_psum", "centred", "squared", "var_psum", "root_ready", "own", "done") as (block, s):
        @block.tensor
        def _(pe):
            for c in range(C):
                nc.tensor.matmul(m.ps[:, c, :], m.head_ones, w.v[:, c, :], start=True, stop=True).then_inc(s["mean_psum"], 1)
            for c in range(C):
                pe.wait_ge(s["squared"], c + 1)
                nc.tensor.matmul(m.ps[:, 4 + c, :], m.head_ones, w.cum[:, c, :], start=True, stop=True).then_inc(s["var_psum"], 1)

        @block.scalar
        def _(act):
            for c in range(C):
                act.wait_ge(s["centred"], c + 1)
                nc.scalar.activation(w.cum[:, c, :], w.logw[:, c, :], ACT.Square).then_inc(s["squared"], 1)
            for c in range(C):
                act.wait_ge(s["var_psum"], c + 1)
                nc.scalar.activation(w.prev[:, c, :], m.ps[:, 4 + c, :], ACT.Sqrt, scale=1.0 / HD,
                                     bias=m.eps[:, 2:3]).then_inc(s["root_ready"], 1)

        @block.vector
        def _(dve):
            own = Own(dve, s["own"])
            for c in range(C):
                dve.wait_ge(s["mean_psum"], c + 1)
                nc.vector.scalar_tensor_tensor(w.logw[:, c, :], m.ps[:, c, :], -1.0 / HD, w.v[:, c, :], ALU.mult,
                                               ALU.add).then_inc(s["centred"], 1)
            for c in range(C):
                y, r = w.logw[:, c, :], w.prev[:, c, :]
                dve.wait_ge(s["root_ready"], c + 1)
                own.then(nc.vector.reciprocal(r, r))
                own.wait()
                own.then(nc.vector.tensor_tensor(y, y, r, ALU.mult))
                own.wait()
                own.then(nc.vector.tensor_scalar(y, y, col("ln_w", c), col("ln_b", c), ALU.mult, ALU.add))
                own.wait()
                own.then(nc.vector.tensor_tensor(y, y, w.bonus[:, c, :], ALU.add))
                own.wait()
                nc.vector.tensor_tensor(m.y[:, c, 0:SEQ], y, w.g[:, c, :], ALU.mult).then_inc(s["done"], 1)


TOPK = 128
HIDDEN = -3.0e38
TAKEN = -3.4e38


class Dsa:

    def __init__(self, m):
        big, wide = m.big, m.wide
        self.qlat = big[:, 0:6 * SEQ].rearrange("p (n t) -> p n t", t=SEQ)
        self.olat = big[:, 6 * SEQ:12 * SEQ].rearrange("p (n t) -> p n t", t=SEQ)
        self.mask = [m.causal[:, :]] + [big[:, 12 * SEQ + b * SEQ:12 * SEQ + b * SEQ + (b + 2) * QB] for b in range(3)]
        self.logits = [big[:, (15 + j) * SEQ:(16 + j) * SEQ] for j in range(2)]
        self.probT = [big[:, (17 + j) * SEQ:(18 + j) * SEQ] for j in range(2)]
        self.relu = [big[:, (19 + j) * SEQ:(20 + j) * SEQ] for j in range(4)]
        self.root, self.square = wide[:, 0:SEQ], wide[:, SEQ:2 * SEQ]
        self.c_tok = wide[:, 2 * SEQ:3 * SEQ].rearrange("p (n f) -> p n f", f=P)
        self.score = wide[:, 3 * SEQ:4 * SEQ]
        self.both = wide[:, 4 * SEQ:4 * SEQ + 768]
        self.up = wide[:, 4 * SEQ:4 * SEQ + 384]
        self.down = wide[:, 4 * SEQ + 384:4 * SEQ + 768]
        self.iw = wide[:, 6 * SEQ:6 * SEQ + 32]
        self.top = wide[:, 6 * SEQ + 32:6 * SEQ + 40]


def dsa_stage(nc, m, layer, d):
    w = Dsa(m)
    half = lambda h: slice(64 * (h % 2), 64 * (h % 2) + 64)
    c = m.other[:, 3, :]
    NB, IH, H = SEQ // QB, 8, 6
    with stage(nc, f"dsa_in{layer}", "loaded", "squared", "ss_psum", "root_ready", "own", "c_scaled", "c_ready", "iw_psum", "c_psum",
               "q_psum", "q_out", "tok_ready") as (block, s):
        @block.sync
        def _(sp):
            sp.dma_start(w.both, d["dsa_w"][layer]).then_inc(s["loaded"], 16)
            sp.wait_ge(s["loaded"], 16)

        @block.tensor
        def _(pe):
            pe.wait_ge(s["loaded"], 16)
            for n in range(NB):
                last = nc.tensor.transpose(m.ps[:, 7, n * 8:(n + 1) * 8], m.other[0:8, 15, n * P:(n + 1) * P],
                                           m.ident[0:8, 0:8])
            last.then_inc(s["iw_psum"], 1)
            for h in range(H):
                nc.tensor.matmul(m.ps[:, h, :], w.up[half(h), (h // 2) * P:(h // 2 + 1) * P], m.other[half(h), h // 2, :],
                                 start=True, stop=True).then_inc(s["q_psum"], 1)
            pe.wait_ge(s["squared"], 1)
            nc.tensor.matmul(m.ps[:, 6, :], m.ones[:, :], w.square, start=True, stop=True).then_inc(s["ss_psum"], 1)
            pe.wait_ge(s["c_ready"], 1)
            pe.wait_ge(s["q_out"], 1)
            for n in range(NB):
                last = nc.tensor.transpose(m.ps[:, 0, n * P:(n + 1) * P], c[:, n * P:(n + 1) * P], m.ident[:, :])
            last.then_inc(s["c_psum"], 1)

        @block.scalar
        def _(act):
            nc.scalar.activation(w.square, c, ACT.Square).then_inc(s["squared"], 1)
            for h in range(H):
                act.wait_ge(s["q_psum"], h + 1)
                nc.scalar.mul(w.qlat[:, h, :], m.ps[:, h, :], SCALE).then_inc(s["q_out"], 1)
            act.wait_ge(s["ss_psum"], 1)
            nc.scalar.activation(w.root, m.ps[:, 6, :], ACT.Sqrt, scale=1.0 / P, bias=m.eps[:, 1:2]).then_inc(s["root_ready"], 1)
            act.wait_ge(s["c_scaled"], 1)
            nc.scalar.activation(c, c, ACT.Copy, scale=m.col(f"dsa_kv_norm{layer}")).then_inc(s["c_ready"], 1)

        @block.vector
        def _(dve):
            own = Own(dve, s["own"])
            dve.wait_ge(s["iw_psum"], 1)
            own.then(nc.vector.tensor_scalar(w.iw, m.ps[:, 7, 0:32], SCALE * IH ** -0.5, None, ALU.mult))
            dve.wait_ge(s["root_ready"], 1)
            own.then(nc.vector.reciprocal(w.root, w.root))
            own.wait()
            nc.vector.tensor_tensor(c, c, w.root, ALU.mult).then_inc(s["c_scaled"], 1)
            dve.wait_ge(s["c_psum"], 1)
            nc.vector.tensor_copy(w.c_tok, m.ps[:, 0, :].rearrange("p (n f) -> p n f", f=P)).then_inc(s["tok_ready"], 1)

    with stage(nc, f"dsa_index{layer}", "rel_psum", "relu_ready", "relu_used", "scored", "hidden", "own", "mask_ready") as (block, s):
        blocks = (3, 2, 1)

        @block.tensor
        def _(pe):
            for i, b in enumerate(blocks):
                for h in range(IH):
                    if i:
                        pe.wait_ge(s["relu_ready"], IH * (i - 1) + h + 1)
                    nc.tensor.matmul(m.ps[:, h, 0:(b + 1) * QB], m.other[half(h), 4 + h // 2, b * QB:(b + 1) * QB],
                                     m.other[half(h), 8, 0:(b + 1) * QB], start=True, stop=True).then_inc(s["rel_psum"], 1)

        @block.scalar
        def _(act):
            for i, b in enumerate(blocks):
                for h in range(IH):
                    u = IH * i + h
                    act.wait_ge(s["rel_psum"], u + 1)
                    if u >= 4:
                        act.wait_ge(s["relu_used"], u - 3)
                    nc.scalar.activation(w.relu[h % 4][:, 0:(b + 1) * QB], m.ps[:, h, 0:(b + 1) * QB],
                                         ACT.Relu).then_inc(s["relu_ready"], 1)

        @block.gpsimd
        def _(pool):
            for i, b in enumerate(blocks):
                pool.wait_ge(s["relu_used"], IH * (i + 1))
                diag = w.score[:, b * QB:(b + 1) * QB]
                nc.gpsimd.affine_select(out=diag, in_=diag, compare_op=ALU.is_ge, fill=HIDDEN, base=0,
                                        pattern=[[-1, QB]], channel_multiplier=1).then_inc(s["hidden"], 1)

        @block.vector
        def _(dve):
            own = Own(dve, s["own"])
            for i, b in enumerate(blocks):
                n = (b + 1) * QB
                score = w.score[:, 0:n]
                for h in range(IH):
                    u = IH * i + h
                    dve.wait_ge(s["relu_ready"], u + 1)
                    iw = w.iw[:, b * IH + h:b * IH + h + 1]
                    if h == 0:
                        if i:
                            dve.wait_ge(s["mask_ready"], i)
                        nc.vector.tensor_scalar(score, w.relu[0][:, 0:n], iw, None, ALU.mult).then_inc(s["relu_used"], 1)
                    else:
                        dve.wait_ge(s["relu_used"], u)
                        nc.vector.scalar_tensor_tensor(score, w.relu[h % 4][:, 0:n], iw, score, ALU.mult,
                                                       ALU.add).then_inc(s["relu_used"], 1)
                dve.wait_ge(s["hidden"], i + 1)
                for _ in range(TOPK // 8):
                    own.then(nc.vector.max(w.top, score))
                    own.wait()
                    own.then(nc.vector.match_replace(score, w.top, score, TAKEN))
                    own.wait()
                nc.vector.tensor_scalar(w.mask[b], score, 0.5 * (HIDDEN + TAKEN), NEG, ALU.is_gt, ALU.mult).then_inc(
                    s["mask_ready"], 1)

    units = [(b, h) for b in range(NB) for h in range(H)]
    NU = len(units)
    peak, shift, total = ([m.stat[:, 2 * i + j:2 * i + j + 1] for j in range(2)] for i in range(3))
    with stage(nc, f"dsa_att{layer}", "scored", "masked", "shift_ready", "exp_done", "own", "prob_ready", "probT_psum",
               "probT_ready", "out_psum", "out_ready", "final_psum", "final_ready") as (block, s):
        @block.tensor
        def _(pe):
            def score(u):
                b, h = units[u]
                if u >= 2:
                    pe.wait_ge(s["masked"], u - 1)
                nc.tensor.matmul(m.ps[:, u % 2, 0:(b + 1) * QB], w.qlat[:, h, b * QB:(b + 1) * QB], c[:, 0:(b + 1) * QB],
                                 start=True, stop=True).then_inc(s["scored"], 1)

            score(0)
            for u, (b, h) in enumerate(units):
                if u + 1 < NU:
                    score(u + 1)
                pe.wait_ge(s["prob_ready"], u + 1)
                for k in range(b + 1):
                    last = nc.tensor.transpose(m.ps[:, 2 + u % 2, k * QB:(k + 1) * QB], w.logits[u % 2][:, k * QB:(k + 1) * QB],
                                               m.ident[:, :])
                last.then_inc(s["probT_psum"], 1)
                pe.wait_ge(s["probT_ready"], u + 1)
                if u >= 2:
                    pe.wait_ge(s["out_ready"], u - 1)
                for k in range(b + 1):
                    last = nc.tensor.matmul(m.ps[:, 4 + u % 2, 0:QB], w.c_tok[:, k, :],
                                            w.probT[u % 2][:, k * QB:(k + 1) * QB], start=(k == 0), stop=(k == b))
                last.then_inc(s["out_psum"], 1)
            pe.wait_ge(s["out_ready"], NU)
            for h in range(H):
                last = nc.tensor.matmul(m.ps[half(h), h // 2, :], w.down[:, h * HD:(h + 1) * HD], w.olat[:, h, :],
                                        start=True, stop=True)
                if h % 2:
                    last.then_inc(s["final_psum"], 1)

        @block.scalar
        def _(act):
            def exponentiate(u):
                b, h = units[u]
                act.wait_ge(s["shift_ready"], u + 1)
                x = w.logits[u % 2][:, 0:(b + 1) * QB]
                nc.scalar.activation(x, x, ACT.Exp, bias=shift[u % 2], accum_out=total[u % 2]).then_inc(s["exp_done"], 1)

            exponentiate(0)
            for u, (b, h) in enumerate(units):
                if u + 1 < NU:
                    exponentiate(u + 1)
                act.wait_ge(s["probT_psum"], u + 1)
                nc.scalar.copy(w.probT[u % 2][:, 0:(b + 1) * QB], m.ps[:, 2 + u % 2, 0:(b + 1) * QB]).then_inc(s["probT_ready"], 1)

        @block.vector
        def _(dve):
            own = Own(dve, s["own"])

            def stabilise(u):
                b, h = units[u]
                n = (b + 1) * QB
                dve.wait_ge(s["scored"], u + 1)
                if u >= 2:
                    dve.wait_ge(s["probT_psum"], u - 1)
                nc.vector.tensor_tensor_reduce(out=w.logits[u % 2][:, 0:n], in0=m.ps[:, u % 2, 0:n], in1=w.mask[b],
                                               scale=1.0, scalar=4.0 * NEG, op0=ALU.add, op1=ALU.max,
                                               accum_out=peak[u % 2]).then_inc(s["masked"], 1)
                dve.wait_ge(s["masked"], u + 1)
                nc.vector.tensor_scalar(shift[u % 2], peak[u % 2], -1.0, None, ALU.mult).then_inc(s["shift_ready"], 1)

            stabilise(0)
            for u, (b, h) in enumerate(units):
                if u + 1 < NU:
                    stabilise(u + 1)
                dve.wait_ge(s["exp_done"], u + 1)
                own.then(nc.vector.reciprocal(total[u % 2], total[u % 2]))
                own.wait()
                x = w.logits[u % 2][:, 0:(b + 1) * QB]
                nc.vector.tensor_scalar(x, x, total[u % 2], None, ALU.mult).then_inc(s["prob_ready"], 1)
                dve.wait_ge(s["out_psum"], u + 1)
                nc.vector.tensor_copy(w.olat[:, h, b * QB:(b + 1) * QB], m.ps[:, 4 + u % 2, 0:QB]).then_inc(s["out_ready"], 1)
            for n in range(H // 2):
                dve.wait_ge(s["final_psum"], n + 1)
                nc.vector.tensor_copy(m.y[:, 3 + n, 0:SEQ], m.ps[:, n, :]).then_inc(s["final_ready"], 1)


def retention_stage(nc, m, layer, d):
    ring = m.ring[:, :, :].rearrange("p a b -> p (a b)")
    cos, sin, turn = ring[:, 0:SEQ], ring[:, SEQ:2 * SEQ], ring[:, 2 * SEQ:2 * SEQ + P]
    decay = [ring[:, 2 * SEQ + P + h * SEQ:2 * SEQ + P + (h + 1) * SEQ] for h in range(4)]
    z = [m.other[:, 9 + i, :] for i in range(4)]
    q, k = z[0:2], z[2:4]
    g = [m.other[:, 13 + i, :] for i in range(2)]
    half = lambda h: slice(64 * (h % 2), 64 * (h % 2) + 64)
    st = [m.wide[:, i * SEQ:(i + 1) * SEQ] for i in range(4)]
    tmp = [m.wide[:, (4 + i) * SEQ:(5 + i) * SEQ] for i in range(4)]
    yf, sq, root, sg = ([m.work[:, 2 * j + i, 0:SEQ] for i in range(2)] for j in range(4))
    NK = SEQ // P
    units = [(h, j) for h in range(4) for j in range(NK)]
    with stage(nc, f"retain{layer}", "loaded", "turned_psum", "cosine", "own", "rotated", "scored", "decayed", "y_psum",
               "y_ready", "squared", "ss_psum", "root_ready", "gate_ready", "done") as (block, s):
        @block.sync
        def _(sp):
            sp.dma_start(ring[:, 0:2 * SEQ + P + 4 * SEQ], d["ret_const"]).then_inc(s["loaded"], 16)
            sp.wait_ge(s["loaded"], 16)

        @block.gpsimd
        def _(pool):
            pool.wait_ge(s["loaded"], 16)
            pool.wait_ge(s["turned_psum"], 4)
            for i in range(4):
                nc.gpsimd.tensor_tensor(z[i], z[i], cos, ALU.mult).then_inc(s["cosine"], 1)

        @block.tensor
        def _(pe):
            pe.wait_ge(s["loaded"], 16)
            for i in range(4):
                nc.tensor.matmul(m.ps[:, i, :], turn, z[i], start=True, stop=True).then_inc(s["turned_psum"], 1)
            pe.wait_ge(s["rotated"], 4)

            def score(u):
                h, j = units[u]
                if u >= 4:
                    pe.wait_ge(s["decayed"], u - 3)
                n = SEQ - j * P
                nc.tensor.matmul(m.ps[:, u % 4, 0:n], k[h // 2][half(h), j * P:(j + 1) * P], q[h // 2][half(h), j * P:SEQ],
                                 start=True, stop=True).then_inc(s["scored"], 1)

            for u in range(3):
                score(u)
            for u, (h, j) in enumerate(units):
                if u + 3 < len(units):
                    score(u + 3)
                pe.wait_ge(s["decayed"], u + 1)
                n = SEQ - j * P
                last = nc.tensor.matmul(m.ps[half(h), 4 + h // 2, j * P:SEQ], m.ret_v[:, j, h * HD:(h + 1) * HD],
                                        st[u % 4][:, 0:n], start=(j == 0), stop=(j == NK - 1))
                if j == NK - 1 and h % 2:
                    last.then_inc(s["y_psum"], 1)
                else:
                    last.then_inc(s["own"], 1)
            for i in range(2):
                pe.wait_ge(s["squared"], i + 1)
                nc.tensor.matmul(m.ps[:, 6 + i, :], m.head_ones, sq[i], start=True, stop=True).then_inc(s["ss_psum"], 1)

        @block.scalar
        def _(act):
            for i in range(2):
                nc.scalar.activation(sg[i], g[i], ACT.Silu).then_inc(s["gate_ready"], 1)
            for i in range(2):
                act.wait_ge(s["y_psum"], i + 1)
                nc.scalar.copy(yf[i], m.ps[:, 4 + i, :]).then_inc(s["y_ready"], 1)
                act.wait_ge(s["y_ready"], i + 1)
                nc.scalar.activation(sq[i], yf[i], ACT.Square).then_inc(s["squared"], 1)
            for i in range(2):
                act.wait_ge(s["ss_psum"], i + 1)
                nc.scalar.activation(root[i], m.ps[:, 6 + i, :], ACT.Sqrt, scale=1.0 / HD,
                                     bias=m.eps[:, 1:2]).then_inc(s["root_ready"], 1)

        @block.vector
        def _(dve):
            dve.wait_ge(s["loaded"], 16)
            for i in range(4):
                dve.wait_ge(s["turned_psum"], i + 1)
                nc.vector.tensor_tensor(tmp[i], m.ps[:, i, :], sin, ALU.mult).then_inc(s["done"], 1)
                dve.wait_ge(s["cosine"], i + 1)
                dve.wait_ge(s["done"], i + 1)
                nc.vector.tensor_tensor(z[i], z[i], tmp[i], ALU.add).then_inc(s["rotated"], 1)
            for u, (h, j) in enumerate(units):
                n = SEQ - j * P
                dve.wait_ge(s["scored"], u + 1)
                if u >= 4:
                    before = sum(1 for hh, jj in units[:u - 3] if jj == NK - 1 and hh % 2)
                    dve.wait_ge(s["own"], u - 3 - before)
                    if before:
                        dve.wait_ge(s["y_psum"], before)
                nc.vector.tensor_tensor(st[u % 4][:, 0:n], m.ps[:, u % 4, 0:n], decay[h][:, 0:n], ALU.mult).then_inc(
                    s["decayed"], 1)
            n_done = 4
            for i in range(2):
                dve.wait_ge(s["root_ready"], i + 1)
                nc.vector.reciprocal(root[i], root[i]).then_inc(s["done"], 1)
                n_done += 1
                dve.wait_ge(s["done"], n_done)
                nc.vector.tensor_tensor(yf[i], yf[i], root[i], ALU.mult).then_inc(s["done"], 1)
                n_done += 1
                dve.wait_ge(s["done"], n_done)
                dve.wait_ge(s["gate_ready"], i + 1)
                nc.vector.tensor_tensor(m.y[:, 6 + i, 0:SEQ], yf[i], sg[i], ALU.mult).then_inc(s["done"], 1)
                n_done += 1


def part_two(nc, m, d):
    x2 = m.x[:, :, META:T1]
    x_tile = lambda k: m.x[:, k, META:T1]
    y_tile = lambda k: m.y[:, k, 0:SEQ]

    def feed_forward(l, f, w_in, w_out):
        with ExitStack() as ctx:
            ffn_memory(nc, ctx, m, f"s{f}_{l}", S2)
            norm_stage(nc, m, f"norm{f}_{l}", x_tile, lambda k: m.work[:, 3 + k % 2, 0:SEQ], f"ffn{f}_norm{l}", None,
                       RMS_EPS, S2, False, m.xs)
            swiglu_stage(nc, m, f"swiglu{f}_{l}", w_in)
            split_out_stage(nc, m, f"swi_out{f}_{l}", w_out, FT2, m.hs, S2, x2, 0.5, 1.0)

    for l in range(2):
        feed_forward(l, 1, d["swi1_in"][l], d["swi1_out"][l])
        with ExitStack() as ctx:
            mixer_memory(nc, ctx, m, f"mix{l}", True)
            norm_stage(nc, m, f"mix_norm_{l}", x_tile, y_tile, f"mix_norm{l}", None, RMS_EPS, S2, False)
            mix_in_stage(nc, m, l, d)
            rwkv_prepare_stage(nc, m, l, d)
            rwkv_recurrence_stage(nc, m, l)
            rwkv_finish_stage(nc, m, l)
            dsa_stage(nc, m, l, d)
            retention_stage(nc, m, l, d)
            out_stage(nc, m, f"mix_out{l}", d["mix_out"][l], KT, P, y_tile, S2, x2, 1.0, 1.0, x2)
        feed_forward(l, 2, d["swi2_in"][l], d["swi2_out"][l])
    with ExitStack() as ctx:
        ffn_memory(nc, ctx, m, "last", S2)
        norm_stage(nc, m, "final", x_tile, x_tile, "final_norm", None, RMS_EPS, S2, False)


def build(nc, d):
    with ExitStack() as ctx:
        m = Mem(nc, ctx)
        setup_stage(nc, m, d)
        part_one(nc, m, d)
        m.add_part_two(nc, ctx)
        load_masks_stage(nc, m, d)
        part_two(nc, m, d)
        with stage(nc, "store", "stored") as (block, s):
            @block.sync
            def _(sp):
                sp.dma_start(d["out"], m.x[:, :, META:T1]).then_inc(s["stored"], 16)
                sp.wait_ge(s["stored"], 16)


def weight_tiles(w, cols, rows=P):
    k, n = w.shape
    return np.ascontiguousarray(w.reshape(k // rows, rows, n // cols, cols).transpose(2, 1, 0, 3)).reshape(
        n // cols, rows, (k // rows) * cols)


def columns(v, size=P):
    v = np.asarray(v).reshape(-1, size).T
    out = np.zeros((P, v.shape[1]), v.dtype)
    out[:size] = v
    return out


def masks():
    p, f = np.meshgrid(np.arange(P), np.arange(P), indexing="ij")
    same = lambda n: p // n == f // n
    out = [same(64), same(16) & (f < p), same(32) & (p % 32 >= 16) & (f % 32 < 16), same(64) & (p % 64 >= 32) & (f % 64 < 32),
           same(16) & (p < f), same(64) & (p < f), same(64) & (p <= f)]
    return np.concatenate([x.astype(np.float32) for x in out], axis=1)


def retention_constants():
    f32 = np.float32
    theta = f32(10000.0) ** -np.linspace(0.0, 1.0, HD // 2, dtype=f32)
    ang = (np.arange(SEQ, dtype=f32)[None, :] * theta[:, None]).astype(f32)
    ang = np.tile(ang, (4, 1)).astype(np.float64)
    turn = np.zeros((P, P), f32)
    for r in range(P):
        turn[(r + 32 if r % 64 < 32 else r - 32), r] = -1.0 if r % 64 < 32 else 1.0
    key, query = np.meshgrid(np.arange(P), np.arange(SEQ), indexing="ij")
    decay = [np.where(query >= key, np.exp((query - key) * np.log(1.0 - 2.0 ** (-5.0 - h))), 0.0) * SCALE for h in range(4)]
    return np.concatenate([np.cos(ang), np.sin(ang), turn] + decay, axis=1).astype(f32)


def layout(a):
    A = {}
    x = np.concatenate([a["meta"], a["x"][0]], axis=0).T
    A["x"] = np.ascontiguousarray(x.reshape(KT, P, T1).transpose(1, 0, 2))
    vec = np.zeros((P, NCOLS), np.float32)

    def put(name, v, size=P):
        at, n = COLS[name]
        c = columns(v, size)
        assert c.shape[1] == n, name
        vec[:, at:at + n] = c

    for k in range(4):
        put(f"a_conv_w{k}", a["a_conv_w"][0, k], LRU)
    for n in ("a_conv_b", "a_b_r", "a_b_i", "a_lambda"):
        put(n, a[n][0], LRU)
    for l in range(2):
        for k in range(3):
            put(f"f_conv_w{l}_{k}", a["f_conv_w"][l, k])
        put(f"f_conv_b{l}", a["f_conv_b"][l])
        for n in ("ln1_g", "ln1_b", "ln2_g", "ln2_b"):
            put(f"{n}{l}", a[n][l])
    put("kv_f_b", a["kv_f_b"], HEADS1)
    for l in range(2):
        for n in ("ffn1_norm", "mix_norm", "ffn2_norm"):
            put(f"{n}{l}", a[f"{n}_2"][l])
        put(f"rwkv_mu{l}", a["rwkv_mu_2"][l])
        for n in ("w0", "a0", "k_k", "k_a", "r_k", "ln_w", "ln_b"):
            put(f"rwkv_{n}{l}", a[f"rwkv_{n}_2"][l].reshape(-1))
        put(f"dsa_kv_norm{l}", a["dsa_kv_norm_2"][l])
    put("rwkv_v0", a["rwkv_v0_2"][0])
    vec[32:48, COLS["rwkv_vres_mu"][0]] = a["rwkv_vres_mu_2"][0]
    put("final_norm", a["final_norm_2"])
    A["vectors"] = vec
    A["masks"] = masks()
    A["ret_const"] = retention_constants()
    for l in range(2):
        for f in (1, 2):
            pad = lambda w: np.concatenate([w, np.zeros((w.shape[0], FT2 * P - w.shape[1]), w.dtype)], axis=1)
            g, u = a[f"ffn{f}_w_gate_2"][l], a[f"ffn{f}_w_up_2"][l]
            A[f"swi{f}_in{l}"] = np.concatenate([weight_tiles(pad(g), P), weight_tiles(pad(u), P)], axis=2)
            A[f"swi{f}_out{l}"] = weight_tiles(pad(a[f"ffn{f}_w_down_2"][l].T).T, P)
        w = a["w_in_2"][l]
        A[f"rwkv_in{l}"] = weight_tiles(w[:, :1280], P)
        q, c, iq, ik, iw = np.split(w[:, 1280:2376], np.cumsum([384, 128, 512, 64]), axis=1)
        rq, rk, rv, rg = np.split(w[:, 2376:], 4, axis=1)
        last = np.zeros((D, P), w.dtype)
        last[:, 0:8] = iw
        if l == 1:
            last[:, 32:48] = a["rwkv_vres_w_in_2"][0]
        A[f"other_in{l}"] = weight_tiles(np.concatenate([q, c, iq, ik, ik, rq, rk, rg, last], axis=1), P)
        A[f"ret_v{l}"] = weight_tiles(rv, 256)[0]
        lo = np.zeros((P, 768), w.dtype)
        lo[0:32, 0:384], lo[32:64, 0:384], lo[64:128, 0:384] = a["rwkv_w2_2"][l], a["rwkv_a2_2"][l], a["rwkv_g2_2"][l]
        lo[32:48, 384:768] = a["rwkv_v2_2"][0]
        A[f"rwkv_lo{l}"] = lo
        A[f"dsa_w{l}"] = np.concatenate([a["dsa_w_uk_2"][l].reshape(3, P, P).transpose(1, 0, 2).reshape(P, 384),
                                         a["dsa_w_uv_2"][l].transpose(1, 0, 2).reshape(P, 384)], axis=1)
        A[f"mix_out{l}"] = weight_tiles(a["w_out_2"][l], P)
    win = a["a_w_in"][0]
    g, r = weight_tiles(win[:, :D_RNN], LRU), weight_tiles(win[:, D_RNN:], LRU)
    small = np.zeros((N_LRU, P, 2 * LRU), np.float32)
    small[:, :LRU, :LRU] = a["a_w_r"][0]
    small[:, :LRU, LRU:] = a["a_w_i"][0]
    kv, qg = a["kv_w"], a["b_w_in"][0]
    A["attn_w"] = np.concatenate([weight_tiles(qg[:, :D], P), weight_tiles(kv[:, :D], P),
                                  weight_tiles(kv[:, D:2 * D], P), weight_tiles(qg[:, D:], P)], axis=2)
    A["forget_w"] = weight_tiles(kv[:, 2 * D:], HEADS1)[0]
    A["attn_out"] = weight_tiles(a["b_w_out"][0], P)
    A["lru_w"] = np.concatenate([g, r, small], axis=2)
    A["lru_out"] = weight_tiles(a["a_w_out"][0], P, LRU)
    for l in range(2):
        w = a["f_w_in"][l]
        A[f"ffn_in{l}"] = np.concatenate([weight_tiles(w[:, :D_FF], P), weight_tiles(w[:, D_FF:], P)], axis=2)
        A[f"ffn_out{l}"] = weight_tiles(a["f_w_out"][l], P)
    return A


def program(nc, shapes):
    aps, groups = {}, {}
    for name, shape in shapes.items():
        ap = nc.dram_tensor(f"in_{name}", shape, FP32, kind="ExternalInput").ap()
        if name[-1] in "01":
            groups.setdefault(name[:-1], {})[int(name[-1])] = ap
        else:
            aps[name] = ap
    out = nc.dram_tensor("out_tokens", (P, KT, SEQ), FP32, kind="ExternalOutput").ap()
    d = {"out": out, **aps, **groups}
    build(nc, d)


def kernel(**inputs):
    import concourse.bacc as bacc
    from concourse.bass_utils import run_bass_kernel_spmd

    a = {k: np.asarray(v) for k, v in inputs.items()}
    arrays = layout(a)
    nc = bacc.Bacc("TRN2", target_bir_lowering=False, num_devices=1)
    program(nc, {k: v.shape for k, v in arrays.items()})
    r = run_bass_kernel_spmd(nc, [{f"in_{k}": v for k, v in arrays.items()}], core_ids=[0])
    out = r.results[0]["out_tokens"]
    return np.ascontiguousarray(out.transpose(2, 1, 0)).reshape(1, SEQ, D)
```

```python
import concourse.bass as bass
from concourse import mybir
from contextlib import ExitStack, contextmanager
import math
import numpy as np

FP32 = mybir.dt.float32
FP32R = mybir.dt.float32r
ALU = mybir.AluOpType
ACT = mybir.ActivationFunctionType
AX = mybir.AxisListType

P = 128
D = 1024
KT = D // P
SEQ = 512
META = 16
T1 = SEQ + META
HALF1 = T1 // 2
D_RNN = 1536
N_LRU = 16
LRU = D_RNN // N_LRU
D_FF = 2816
FT = D_FF // P
FT2 = 22
ALPHA = 4.0 ** 0.25
LN_EPS = 1e-5
RMS_EPS = 1e-6
GN_EPS = 64e-5
HEADS1 = 16
HD = 64
QB = 128
NEG = -1.0e30
SCALE = HD ** -0.5


class Span:

    def __init__(self, tokens):
        self.tokens = tokens
        self.banks = -(-tokens // 512)
        self.width = tokens // self.banks

    def psum(self, ps, bank, row=0, rows=P):
        return ps[row:row + rows, bank:bank + self.banks, 0:self.width]

    def sbuf(self, ap):
        return ap.rearrange("p (h t) -> p h t", h=self.banks)


S1 = Span(T1)
S2 = Span(SEQ)


class Own:

    def __init__(self, eng, sem, base=0):
        self.eng, self.sem, self.base, self.n = eng, sem, base, 0

    def then(self, ins):
        ins.then_inc(self.sem, 1)
        self.n += 1
        return ins

    def wait(self):
        self.eng.wait_ge(self.sem, self.base + self.n)



@contextmanager
def stage(nc, name, *signals):
    sems = {s: nc.alloc_semaphore(f"{name}_{s}") for s in signals}
    with nc.Block() as block:
        yield block, sems
    nc.clear_and_free_semaphores(list(sems.values()))
    nc.all_engine_barrier()


def vector_columns():
    cols, at = {}, 0

    def add(name, n):
        nonlocal at
        cols[name] = (at, n)
        at += n

    for k in range(4):
        add(f"a_conv_w{k}", N_LRU)
    for n in ("a_conv_b", "a_b_r", "a_b_i", "a_lambda"):
        add(n, N_LRU)
    for l in range(2):
        for k in range(3):
            add(f"f_conv_w{l}_{k}", 2 * FT)
        add(f"f_conv_b{l}", 2 * FT)
        for n in ("ln1_g", "ln1_b", "ln2_g", "ln2_b"):
            add(f"{n}{l}", KT)
    add("kv_f_b", 1)
    for l in range(2):
        for n in ("ffn1_norm", "mix_norm", "ffn2_norm"):
            add(f"{n}{l}", KT)
        add(f"rwkv_mu{l}", 10)
        for n in ("w0", "a0", "k_k", "k_a", "r_k", "ln_w", "ln_b"):
            add(f"rwkv_{n}{l}", 3)
        add(f"dsa_kv_norm{l}", 1)
    add("rwkv_v0", 3)
    add("rwkv_vres_mu", 1)
    add("final_norm", KT)
    return cols, at


COLS, NCOLS = vector_columns()


class Mem:

    def __init__(self, nc, ctx):
        def sb(name, shape):
            return ctx.enter_context(nc.sbuf_tensor(name, shape, FP32))

        self.x = sb("x_tokens", [P, KT, T1])
        self.vec = sb("vectors", [P, NCOLS])
        self.ones = sb("ones", [P, P])
        self.ident = sb("identity", [P, P])
        self.causal = sb("causal", [P, P])
        self.stat = sb("stat", [P, 64])
        self.eps = sb("eps", [P, 3])
        self.c_dram = nc.dram_tensor("forget_scratch", (HEADS1, T1), FP32).ap()
        self.ps = ctx.enter_context(nc.psum_tensor("psum", [P, 8, 512], FP32))

    def add_part_two(self, nc, ctx):
        self.masks = ctx.enter_context(nc.sbuf_tensor("masks", [P, 7 * P], FP32))
        (self.head_ones, self.low16, self.edge16, self.edge32, self.up16, self.strict64,
         self.upto64) = [self.masks[:, i * P:(i + 1) * P] for i in range(7)]
        self.v_first = ctx.enter_context(nc.sbuf_tensor("v_first", [P, 3, SEQ], FP32))

    def col(self, name, i=0, rows=P):
        at, _ = COLS[name]
        if isinstance(i, int):
            return self.vec[0:rows, at + i:at + i + 1]
        return self.vec[0:rows, bass.ds(i + at, 1)]


def mixer_memory(nc, ctx, m, name):
    def sb(what, shape):
        return ctx.enter_context(nc.sbuf_tensor(f"{name}_{what}", shape, FP32))

    m.y = sb("y", [P, KT, T1])
    m.big = sb("big", [P, 24 * T1])
    m.ring = sb("ring", [P, 2, 4 * KT * P])
    m.work = sb("work", [P, 8, 532])
    m.wide = sb("wide", [P, 8 * SEQ])
    m.crow = sb("crow", [1, 4 * T1])


def projected_memory(nc, ctx, m, name):
    def sb(what, shape):
        return ctx.enter_context(nc.sbuf_tensor(f"{name}_{what}", shape, FP32))

    m.work = sb("work", [P, 8, 532])
    m.low = sb("low", [P, 10 * SEQ])
    m.other = sb("other", [P, 16, SEQ])
    misc = sb("misc", [P, 4 * SEQ])
    m.ret_v = misc[:, 0:2 * SEQ].rearrange("p (n f) -> p n f", f=256)
    m.values = [misc[:, (2 + f) * SEQ:(3 + f) * SEQ] for f in range(2)]
    m.reset = misc[:, 2 * SEQ:3 * SEQ]


def split_memory(nc, ctx, m, name):
    m.xs = Split(nc, ctx, f"{name}_x", [P, KT, SEQ])
    m.ws = Split(nc, ctx, f"{name}_w", [P, 2, KT * P])
    m.raw = ctx.enter_context(nc.sbuf_tensor(f"{name}_raw", [P, 4, KT * P], FP32))


def mixed_memory(nc, ctx, m, name):
    def sb(what, shape):
        return ctx.enter_context(nc.sbuf_tensor(f"{name}_{what}", shape, FP32))

    m.y = sb("y", [P, KT, T1])
    m.high = sb("high", [P, 14 * SEQ + 384])
    m.ring = sb("ring", [P, 2, 4 * KT * P])
    m.wide = sb("wide", [P, 8 * SEQ])


def load_tiles(sp, nc, ring, dram, n, loaded, finished, preloaded=False):
    for j in range(2):
        if preloaded:
            sp.sem_inc(loaded[j], 16)
        else:
            sp.dma_start(ring[j], dram[j]).then_inc(loaded[j], 16)
    with sp.Fori(1, n // 2) as i:
        for j in range(2):
            sp.wait_ge(finished, 2 * i + j - 1)
            sp.dma_start(ring[j], dram[2 * i + j]).then_inc(loaded[j], 16)


def project(nc, ps, bank, w, x, k_tiles, span, rows=P, row=0):
    last = None
    for h in range(span.banks):
        for k in range(k_tiles):
            last = nc.tensor.matmul(ps[row:row + rows, bank + h, 0:span.width], w[:, k * rows:(k + 1) * rows],
                                    x(k)[:, h * span.width:(h + 1) * span.width],
                                    start=(k == 0), stop=(k == k_tiles - 1))
    return last


def setup_stage(nc, m, d):
    with stage(nc, "setup", "loaded", "const") as (block, s):
        @block.sync
        def _(sp):
            sp.dma_start(m.x[:, :, :], d["x"]).then_inc(s["loaded"], 16)
            sp.dma_start(m.vec[:, :], d["vectors"]).then_inc(s["loaded"], 16)
            sp.wait_ge(s["loaded"], 32)

        @block.gpsimd
        def _(pool):
            nc.gpsimd.memset(m.ones[:, :], 1.0).then_inc(s["const"], 1)
            nc.gpsimd.memset(m.ident[:, :], 0.0).then_inc(s["const"], 1)
            nc.gpsimd.memset(m.causal[:, :], 0.0).then_inc(s["const"], 1)
            pool.wait_ge(s["const"], 3)
            nc.gpsimd.affine_select(out=m.causal[:, :], in_=m.causal[:, :], compare_op=ALU.is_ge, fill=NEG,
                                    base=0, pattern=[[-1, P]], channel_multiplier=1)
            nc.gpsimd.memset(m.eps[:, 0:1], LN_EPS)
            nc.gpsimd.memset(m.eps[:, 1:2], RMS_EPS)
            nc.gpsimd.memset(m.eps[:, 2:3], GN_EPS)
            pool.wait_ge(s["const"], 2)
            nc.gpsimd.affine_select(out=m.ident[:, :], in_=m.ident[:, :], compare_op=ALU.not_equal, fill=1.0,
                                    base=0, pattern=[[-1, P]], channel_multiplier=1).then_inc(s["const"], 1)
            pool.wait_ge(s["const"], 4)


def load_masks_stage(nc, m, d):
    with stage(nc, "load_masks", "loaded") as (block, s):
        @block.sync
        def _(sp):
            sp.dma_start(m.masks[:, :], d["masks"]).then_inc(s["loaded"], 16)
            sp.wait_ge(s["loaded"], 16)


def lru_stage(nc, m, d):
    R = LRU
    width = 2 * KT * R
    hid = m.big[:, 0:N_LRU * T1].rearrange("p (n t) -> p n t", t=T1)
    ring = [m.ring[:, j, 0:width] for j in range(2)]
    gate_ring = [m.ring[0:R, j, width:width + 2 * R] for j in range(2)]
    slots = [[m.work[0:R, k, 0:T1 + 3] for k in range(8)],
             [m.wide[0:R, k * (T1 + 3):(k + 1) * (T1 + 3)] for k in range(7)] + [m.y[0:R, 0, 0:T1]]]
    decay = m.stat[0:R, 0:N_LRU]
    flat = lambda ap: ap.rearrange("p a t -> p (a t)")
    with stage(nc, "lru", "loaded0", "loaded1", "loaded2", "loaded3", "projected", "gates_psum", "padded", "gelu",
               "convolved", "rr_ready", "gated", "tanh_ready", "q_ready", "root_ready", "h_ready", "vec_own",
               "act_own", "lam_ready") as (block, s):

        def rounds(eng, head, tail):
            head(0, 0)
            with eng.Fori(0, N_LRU // 2 - 1) as i:
                for j in range(2):
                    head(*((i, 1) if j == 0 else (i + 1, 0)))
                    tail(i, j)
            head(N_LRU // 2 - 1, 1)
            tail(N_LRU // 2 - 1, 0)
            tail(N_LRU // 2 - 1, 1)

        @block.sync
        def _(sp):
            for j in range(2):
                sp.dma_start(ring[j], d["lru_w"][j][:, 0:width]).then_inc(s[f"loaded{j}"], 16)
                sp.dma_start(gate_ring[j], d["lru_w"][j][0:R, width:width + 2 * R]).then_inc(s[f"loaded{2 + j}"], 16)
            with sp.Fori(1, N_LRU // 2) as i:
                for j in range(2):
                    sp.wait_ge(s["projected"], 2 * i + j - 1)
                    sp.dma_start(ring[j], d["lru_w"][2 * i + j][:, 0:width]).then_inc(s[f"loaded{j}"], 16)
                    sp.wait_ge(s["gates_psum"], 2 * i + j - 1)
                    sp.dma_start(gate_ring[j], d["lru_w"][2 * i + j][0:R, width:width + 2 * R]).then_inc(
                        s[f"loaded{2 + j}"], 16)

        @block.tensor
        def _(pe):
            def head(i, j):
                t = 2 * i + j
                pe.wait_ge(s[f"loaded{j}"], 16 * i + 16)
                pe.wait_ge(s["gelu"], t + 1)
                project(nc, m.ps, 0, ring[j], lambda k: m.x[:, k, :], KT, S1, rows=R)
                pe.wait_ge(s["padded"], t + 1)
                project(nc, m.ps, 2, ring[j][:, KT * R:2 * KT * R], lambda k: m.x[:, k, :], KT, S1,
                        rows=R).then_inc(s["projected"], 1)

            def tail(i, j):
                t = 2 * i + j
                pe.wait_ge(s[f"loaded{2 + j}"], 16 * i + 16)
                pe.wait_ge(s["convolved"], t + 1)
                pe.wait_ge(s["gated"], t + 1)
                for g in range(2):
                    last = project(nc, m.ps, 4 + 2 * g, gate_ring[j][:, g * R:(g + 1) * R],
                                   lambda k: slots[j][2][:, 0:T1], 1, S1, rows=R)
                last.then_inc(s["gates_psum"], 1)

            rounds(pe, head, tail)

        @block.scalar
        def _(act):
            nc.scalar.activation(m.stat[0:R, 16:32], m.vec[0:R, COLS["a_lambda"][0]:COLS["a_lambda"][0] + N_LRU],
                                 ACT.Abs).then_inc(s["act_own"], 1)
            act.wait_ge(s["act_own"], 1)
            nc.scalar.activation(m.stat[0:R, 16:32], m.stat[0:R, 16:32], ACT.Exp, scale=-1.0).then_inc(s["act_own"], 1)
            act.wait_ge(s["act_own"], 2)
            nc.scalar.activation(m.stat[0:R, 16:32], m.stat[0:R, 16:32], ACT.Ln, bias=1.0).then_inc(s["lam_ready"], 1)
            act.sem_inc(s["padded"], 1)
            act.sem_inc(s["gelu"], 1)
            act.sem_inc(s["gated"], 1)
            act.wait_ge(s["lam_ready"], 2)

            def head(i, j):
                t = 2 * i + j
                gate, pad = slots[j][0:2]
                act.wait_ge(s["projected"], t + 1)
                act.wait_ge(s["h_ready"], t + 1)
                nc.scalar.copy(S1.sbuf(pad[:, 3:3 + T1]), S1.psum(m.ps, 2, rows=R)).then_inc(s["padded"], 1)
                nc.scalar.activation(S1.sbuf(gate[:, 0:T1]), S1.psum(m.ps, 0, rows=R),
                                     ACT.Gelu_apprx_tanh).then_inc(s["gelu"], 1)

            def tail(i, j):
                t = 2 * i + j
                rr, ii, th = slots[j][3:6]
                act.wait_ge(s["gates_psum"], t + 1)
                nc.scalar.activation(S1.sbuf(rr[:, 0:T1]), S1.psum(m.ps, 4, rows=R), ACT.Sigmoid,
                                     bias=m.col("a_b_r", t, R)).then_inc(s["rr_ready"], 1)
                nc.scalar.activation(S1.sbuf(ii[:, 0:T1]), S1.psum(m.ps, 6, rows=R), ACT.Sigmoid,
                                     bias=m.col("a_b_i", t, R)).then_inc(s["gated"], 1)
                act.wait_ge(s["rr_ready"], t + 1)
                nc.scalar.activation(th[:, 0:T1], rr[:, 0:T1], ACT.Tanh,
                                     scale=m.stat[0:R, bass.ds(t, 1)]).then_inc(s["tanh_ready"], 1)
                act.wait_ge(s["tanh_ready"], t + 1)
                nc.scalar.activation(rr[:, 0:T1], th[:, 0:T1], ACT.Sqrt, scale=-4.0).then_inc(s["root_ready"], 1)

            rounds(act, head, tail)

        @block.vector
        def _(dve):
            nc.vector.tensor_scalar(decay, m.vec[0:R, COLS["a_lambda"][0]:COLS["a_lambda"][0] + N_LRU], -1.0, 0.0,
                                    ALU.mult, ALU.max).then_inc(s["vec_own"], 1)
            for j in range(2):
                nc.vector.memset(slots[j][1][:, 0:3], 0.0).then_inc(s["vec_own"], 1)
            dve.wait_ge(s["vec_own"], 3)
            dve.wait_ge(s["lam_ready"], 1)
            nc.vector.tensor_tensor(decay, decay, m.stat[0:R, 16:32][:, 0:N_LRU], ALU.add).then_inc(s["vec_own"], 1)
            dve.wait_ge(s["vec_own"], 4)
            nc.vector.tensor_scalar(decay, decay, -4.0, None, ALU.mult).then_inc(s["lam_ready"], 1)
            dve.sem_inc(s["h_ready"], 2)
            HEAD, TAIL = 3, 6

            def head(i, j, first=False):
                t = 2 * i + j
                pad, conv = slots[j][1:3]
                own = Own(dve, s["vec_own"], 4 if first else 4 + HEAD * t + TAIL * (t - 1))
                dve.wait_ge(s["padded"], t + 2)
                own.then(nc.vector.tensor_scalar(conv[:, 0:T1], pad[:, 0:T1], m.col("a_conv_w0", t, R),
                                                 m.col("a_conv_b", t, R), ALU.mult, ALU.add))
                for k in (1, 2):
                    own.wait()
                    own.then(nc.vector.scalar_tensor_tensor(conv[:, 0:T1], pad[:, k:k + T1],
                                                            m.col(f"a_conv_w{k}", t, R), conv[:, 0:T1],
                                                            ALU.mult, ALU.add))
                own.wait()
                nc.vector.scalar_tensor_tensor(conv[:, 0:T1], pad[:, 3:3 + T1], m.col("a_conv_w3", t, R),
                                               conv[:, 0:T1], ALU.mult, ALU.add).then_inc(s["convolved"], 1)
                assert own.n == HEAD

            def tail(i, j, last=False):
                t = 2 * i + j
                gate, pad, conv, rr, ii, th, q, u = slots[j]
                own = Own(dve, s["vec_own"], 4 + (HEAD + TAIL) * t + (HEAD if last else 2 * HEAD))
                dve.wait_ge(s["tanh_ready"], t + 1)
                own.then(nc.vector.tensor_scalar(q[:, 0:T1], th[:, 0:T1], -1.0, 1.0, ALU.mult, ALU.add))
                dve.wait_ge(s["gated"], t + 2)
                dve.wait_ge(s["convolved"], t + 1)
                own.then(nc.vector.tensor_tensor(ii[:, 0:T1], ii[:, 0:T1], conv[:, 0:T1], ALU.mult))
                own.wait()
                own.then(nc.vector.reciprocal(q[:, 0:T1], q[:, 0:T1]))
                own.wait()
                own.then(nc.vector.tensor_tensor(u[:, 0:T1], ii[:, 0:T1], q[:, 0:T1], ALU.mult))
                own.wait()
                dve.wait_ge(s["root_ready"], t + 1)
                nc.vector.scalar_tensor_tensor(q[:, 0:T1], th[:, 0:T1], 1.0, q[:, 0:T1], ALU.add,
                                               ALU.mult).then_inc(s["q_ready"], 1)
                own.then(nc.vector.tensor_tensor(u[:, 0:T1], u[:, 0:T1], rr[:, 0:T1], ALU.mult))
                own.wait()
                dve.wait_ge(s["q_ready"], t + 1)
                own.then(nc.vector.tensor_tensor_scan(conv[:, 0:T1], q[:, 0:T1], u[:, 0:T1], 0.0, ALU.mult,
                                                      ALU.add))
                own.wait()
                dve.wait_ge(s["gelu"], t + 2)
                nc.vector.tensor_tensor(flat(hid[0:R, bass.ds(t, 1), :]), conv[:, 0:T1],
                                        gate[:, 0:T1], ALU.mult).then_inc(s["h_ready"], 1)
                assert own.n == TAIL

            head(0, 0, first=True)
            with dve.Fori(0, N_LRU // 2 - 1) as i:
                for j in range(2):
                    head(*((i, 1) if j == 0 else (i + 1, 0)))
                    tail(i, j)
            head(N_LRU // 2 - 1, 1)
            tail(N_LRU // 2 - 1, 0)
            tail(N_LRU // 2 - 1, 1, last=True)


def out_stage(nc, m, name, weights, k_tiles, rows, hidden, span, skip, y_scale, x_scale, dst=None, ring=None):
    preloaded = ring is not None
    ring = ring or [m.ring[0:rows, j, 0:k_tiles * P] for j in range(2)]
    tok = span.tokens
    dst = m.y if dst is None else dst
    with stage(nc, name, "loaded0", "loaded1", "projected", "emptied") as (block, s):
        @block.sync
        def _(sp):
            load_tiles(sp, nc, ring, weights, KT, (s["loaded0"], s["loaded1"]), s["projected"], preloaded)

        @block.tensor
        def _(pe):
            with pe.Fori(0, KT // 2) as i:
                for j in range(2):
                    pe.wait_ge((s["loaded0"], s["loaded1"])[j], 16 * i + 16)
                    pe.wait_ge(s["emptied"], 2 * i + j + 1)
                    project(nc, m.ps, 4 * j, ring[j], hidden, k_tiles, span).then_inc(s["projected"], 1)

        @block.vector
        def _(dve):
            dve.sem_inc(s["emptied"], 2)
            with dve.Fori(0, KT // 2) as i:
                for j in range(2):
                    t = 2 * i + j
                    xt = skip[:, bass.ds(t, 1), :].rearrange("p a t -> p (a t)")
                    dve.wait_ge(s["projected"], t + 1)
                    if y_scale != 1.0:
                        assert x_scale == 1.0
                        nc.vector.scalar_tensor_tensor(span.sbuf(dst[:, bass.ds(t, 1), 0:tok].rearrange("p a t -> p (a t)")),
                                                       span.psum(m.ps, 4 * j), y_scale, span.sbuf(xt), ALU.mult,
                                                       ALU.add).then_inc(s["emptied"], 1)
                    else:
                        nc.vector.scalar_tensor_tensor(span.sbuf(dst[:, bass.ds(t, 1), 0:tok].rearrange("p a t -> p (a t)")),
                                                       span.sbuf(xt), x_scale, span.psum(m.ps, 4 * j), ALU.mult,
                                                       ALU.add).then_inc(s["emptied"], 1)


def norm_stage(nc, m, name, src, dst, gain, bias, eps, span, centre, split=None, first=()):
    tok = span.tokens
    acc, mean, rstd = [m.work[:, k, 0:tok] for k in range(3)]
    sq = [m.work[:, 3 + k, 0:tok] for k in range(2)]
    inv = 1.0 / D
    with stage(nc, name, "summed", "mean_psum", "mean_ready", "centred", "squared", "sq_used", "sq_summed", "var_psum",
               "std_ready", "own", "scaled", "done", "hi_ready", "lo_ready", "preloaded") as (block, s):
        @block.sync
        def _(sp):
            for slot, source in enumerate(first):
                sp.dma_start(m.raw[:, slot, 0:source.shape[1]], source).then_inc(s["preloaded"], 16)
            if first:
                sp.wait_ge(s["preloaded"], 16 * len(first))

        @block.vector
        def _(dve):
            own = Own(dve, s["own"])
            if centre:
                own.then(nc.vector.tensor_tensor(acc, src(0), src(1), ALU.add))
                for k in range(2, KT):
                    own.wait()
                    ins = nc.vector.tensor_tensor(acc, acc, src(k), ALU.add)
                    if k < KT - 1:
                        own.then(ins)
                ins.then_inc(s["summed"], 1)
                dve.wait_ge(s["mean_psum"], 1)
                own.then(nc.vector.tensor_scalar(span.sbuf(mean), span.psum(m.ps, 0), inv, None, ALU.mult))
                own.wait()
                for k in range(KT):
                    nc.vector.tensor_tensor(src(k), src(k), mean, ALU.subtract).then_inc(s["centred"], 1)
            for k in range(KT):
                dve.wait_ge(s["squared"], k + 1)
                if k == 0:
                    nc.vector.tensor_copy(acc, sq[0]).then_inc(s["sq_used"], 1)
                else:
                    dve.wait_ge(s["sq_used"], k)
                    nc.vector.tensor_tensor(acc, acc, sq[k % 2], ALU.add).then_inc(s["sq_used"], 1)
            dve.wait_ge(s["std_ready"], 1)
            own.then(nc.vector.reciprocal(rstd, rstd))
            own.wait()

            def scale(k):
                if split and k >= 2:
                    dve.wait_ge(s["lo_ready"], k - 1)
                nc.vector.tensor_tensor(dst(k), src(k), rstd, ALU.mult).then_inc(s["scaled"], 1)

            scale(0)
            for k in range(KT):
                if k + 1 < KT:
                    scale(k + 1)
                if split:
                    dve.wait_ge(s["hi_ready"], k + 1)
                    nc.vector.tensor_tensor(split.lo[:, k, :], dst(k), split.hi[:, k, :].bitcast(FP32),
                                            ALU.subtract).then_inc(s["lo_ready"], 1)

        @block.tensor
        def _(pe):
            if centre:
                pe.wait_ge(s["summed"], 1)
                project(nc, m.ps, 0, m.ones, lambda k: acc, 1, span).then_inc(s["mean_psum"], 1)
            pe.wait_ge(s["sq_used"], KT)
            project(nc, m.ps, 2, m.ones, lambda k: acc, 1, span).then_inc(s["var_psum"], 1)

        @block.scalar
        def _(act):
            for k in range(KT):
                if centre:
                    act.wait_ge(s["centred"], k + 1)
                if k >= 2:
                    act.wait_ge(s["sq_used"], k - 1)
                nc.scalar.activation(sq[k % 2], src(k), ACT.Square).then_inc(s["squared"], 1)
            act.wait_ge(s["var_psum"], 1)
            nc.scalar.activation(span.sbuf(rstd), span.psum(m.ps, 2), ACT.Sqrt, scale=inv,
                                 bias=m.eps[:, 0:1] if eps == LN_EPS else m.eps[:, 1:2]).then_inc(s["std_ready"], 1)
            for k in range(KT):
                act.wait_ge(s["scaled"], k + 1)
                if bias is None:
                    nc.scalar.activation(dst(k), dst(k), ACT.Copy, scale=m.col(gain, k)).then_inc(s["done"], 1)
                else:
                    nc.scalar.activation(dst(k), dst(k), ACT.Identity, scale=m.col(gain, k),
                                         bias=m.col(bias, k)).then_inc(s["done"], 1)
                if split:
                    act.wait_ge(s["done"], k + 1)
                    nc.scalar.copy(split.hi[:, k, :], dst(k)).then_inc(s["hi_ready"], 1)


class Split:

    def __init__(self, nc, ctx, name, shape):
        self.hi = ctx.enter_context(nc.sbuf_tensor(f"{name}_hi", shape, FP32R))
        self.lo = ctx.enter_context(nc.sbuf_tensor(f"{name}_lo", shape, FP32R))


def ffn_memory(nc, ctx, m, name, span):
    tok = span.tokens
    m.xs = Split(nc, ctx, f"{name}_x", [P, KT, tok])
    m.hs = Split(nc, ctx, f"{name}_h", [P, FT, tok])
    m.ws = Split(nc, ctx, f"{name}_w", [P, 2, 11 * P])
    m.raw = ctx.enter_context(nc.sbuf_tensor(f"{name}_raw", [P, 4, 11 * P], FP32))
    m.work = ctx.enter_context(nc.sbuf_tensor(f"{name}_work", [P, 8 if tok > SEQ else 5, tok + 4], FP32))


def first_units(weights, k_tiles):
    return [weights[j][:, g * k_tiles * P:(g + 1) * k_tiles * P] for j in range(2) for g in range(2)]


class Units:

    def __init__(self, nc, m, s, weights, n, k_tiles):
        self.nc, self.m, self.s, self.weights, self.n = nc, m, s, weights, n
        self.k_tiles, self.cols = k_tiles, k_tiles * P

    SIGNALS = ("loaded0", "loaded1", "loaded2", "loaded3", "hi_ready", "lo_ready", "unit_done", "preloaded")

    def source(self, t, g):
        return self.weights[t][:, g * self.cols:(g + 1) * self.cols]

    def load_all(self, sp, following=()):
        for slot in range(4):
            sp.sem_inc(self.s[f"loaded{slot}"], 16)
        with sp.Fori(1, self.n // 2) as i:
            for j in range(2):
                for g in range(2):
                    sp.wait_ge(self.s["lo_ready"], 4 * i + 2 * j + g - 3)
                    sp.dma_start(self.m.raw[:, 2 * j + g, 0:self.cols], self.source(2 * i + j, g)).then_inc(
                        self.s[f"loaded{2 * j + g}"], 16)
        for slot, source in enumerate(following):
            sp.wait_ge(self.s["lo_ready"], 2 * self.n + slot - 3)
            sp.dma_start(self.m.raw[:, slot, 0:source.shape[1]], source).then_inc(self.s["preloaded"], 16)
        if following:
            sp.wait_ge(self.s["preloaded"], 16 * len(following))

    def split_hi(self, act, i, j, g):
        u = 4 * i + 2 * j + g
        act.wait_ge(self.s[f"loaded{2 * j + g}"], 16 * i + 16)
        act.wait_ge(self.s["unit_done"], u + 1)
        self.nc.scalar.copy(self.m.ws.hi[:, g, 0:self.cols], self.m.raw[:, 2 * j + g, 0:self.cols]).then_inc(
            self.s["hi_ready"], 1)

    def split_lo(self, dve, i, j, g):
        dve.wait_ge(self.s["hi_ready"], 4 * i + 2 * j + g + 1)
        self.nc.vector.tensor_tensor(self.m.ws.lo[:, g, 0:self.cols], self.m.raw[:, 2 * j + g, 0:self.cols],
                                     self.m.ws.hi[:, g, 0:self.cols].bitcast(FP32), ALU.subtract).then_inc(
            self.s["lo_ready"], 1)

    def multiply(self, pe, i, j, g, bank, x, k0, span, start, stop):
        pe.wait_ge(self.s["lo_ready"], 4 * i + 2 * j + g + 1)
        hi, lo, last = self.m.ws.hi, self.m.ws.lo, None
        for h in range(span.banks):
            cols = slice(h * span.width, (h + 1) * span.width)
            for k in range(self.k_tiles):
                w = slice(k * P, (k + 1) * P)
                for n, (a, b) in enumerate(((hi, x.hi), (hi, x.lo), (lo, x.hi))):
                    last = self.nc.tensor.matmul(self.m.ps[:, bank + h, 0:span.width], a[:, g, w], b[:, k0 + k, cols],
                                                 start=(start and k == 0 and n == 0),
                                                 stop=(stop and k == self.k_tiles - 1 and n == 2))
        last.then_inc(self.s["unit_done"], 1)

    def rounds(self, eng, body):
        with eng.Fori(0, self.n // 2 - 1) as i:
            for j in range(2):
                body(i, j, True)
        for j in range(2):
            body(self.n // 2 - 1, j, j == 0)

    def ahead(self, i, j):
        return (i, 1) if j == 0 else (i + 1, 0)


def conv_ffn_stage(nc, m, layer, weights, following):
    pads = [[m.work[:, 4 * j + g, 0:T1 + 2] for g in range(2)] for j in range(2)]
    convs = [[m.work[:, 4 * j + 2 + g, 0:T1] for g in range(2)] for j in range(2)]
    flat = lambda ap: ap.rearrange("p a t -> p (a t)")
    with stage(nc, f"ffn_in{layer}", *Units.SIGNALS, "emptied", "evacuated", "convolved", "gelu",
               "pads_free", "own", "product", "hidden_hi", "hidden_lo") as (block, s):
        un = Units(nc, m, s, weights, FT, KT)

        @block.sync
        def _(sp):
            un.load_all(sp, following)

        @block.tensor
        def _(pe):
            pe.sem_inc(s["unit_done"], 2)
            with pe.Fori(0, FT // 2) as i:
                for j in range(2):
                    pe.wait_ge(s["emptied"], 2 * i + j + 1)
                    for g in range(2):
                        un.multiply(pe, i, j, g, 4 * j + 2 * g, m.xs, 0, S1, True, True)

        @block.scalar
        def _(act):
            act.sem_inc(s["emptied"], 2)
            un.split_hi(act, 0, 0, 0)
            un.split_hi(act, 0, 0, 1)

            def body(i, j, more):
                t = 2 * i + j
                if more:
                    for g in range(2):
                        un.split_hi(act, *un.ahead(i, j), g)
                act.wait_ge(s["unit_done"], 2 * t + 4)
                act.wait_ge(s["pads_free"], t + 1)
                act.wait_ge(s["hidden_lo"], t + 1)
                nc.scalar.copy(S1.sbuf(pads[j][0][:, 2:2 + T1]), S1.psum(m.ps, 4 * j)).then_inc(s["evacuated"], 1)
                nc.scalar.copy(S1.sbuf(pads[j][1][:, 2:2 + T1]), S1.psum(m.ps, 4 * j + 2)).then_inc(s["emptied"], 1)
                act.wait_ge(s["convolved"], t + 1)
                nc.scalar.activation(convs[j][0], convs[j][0], ACT.Gelu_apprx_tanh).then_inc(s["gelu"], 1)
                act.wait_ge(s["product"], t + 1)
                nc.scalar.copy(flat(m.hs.hi[:, bass.ds(t, 1), :]), convs[j][1]).then_inc(s["hidden_hi"], 1)

            un.rounds(act, body)

        @block.vector
        def _(dve):
            for j in range(2):
                for g in range(2):
                    nc.vector.memset(pads[j][g][:, 0:2], 0.0).then_inc(s["own"], 1)
            dve.wait_ge(s["own"], 4)
            dve.sem_inc(s["pads_free"], 2)
            dve.sem_inc(s["hidden_lo"], 2)
            un.split_lo(dve, 0, 0, 0)
            un.split_lo(dve, 0, 0, 1)

            def body(i, j, more):
                t = 2 * i + j
                own = Own(dve, s["own"], 4 * t + 4)
                if more:
                    for g in range(2):
                        un.split_lo(dve, *un.ahead(i, j), g)
                for g in range(2):
                    if g == 0:
                        dve.wait_ge(s["evacuated"], t + 1)
                    else:
                        dve.wait_ge(s["emptied"], t + 3)
                    c, x = convs[j][g], pads[j][g]
                    own.then(nc.vector.tensor_scalar(c, x[:, 0:T1], m.col(f"f_conv_w{layer}_0", t + g * FT),
                                                     m.col(f"f_conv_b{layer}", t + g * FT), ALU.mult, ALU.add))
                    own.wait()
                    own.then(nc.vector.scalar_tensor_tensor(c, x[:, 1:1 + T1], m.col(f"f_conv_w{layer}_1", t + g * FT),
                                                            c, ALU.mult, ALU.add))
                    own.wait()
                    nc.vector.scalar_tensor_tensor(c, x[:, 2:2 + T1], m.col(f"f_conv_w{layer}_2", t + g * FT),
                                                   c, ALU.mult, ALU.add).then_inc((s["convolved"], s["pads_free"])[g], 1)
                dve.wait_ge(s["gelu"], t + 1)
                dve.wait_ge(s["pads_free"], t + 3)
                nc.vector.tensor_tensor(convs[j][1], convs[j][0], convs[j][1], ALU.mult).then_inc(s["product"], 1)
                dve.wait_ge(s["hidden_hi"], t + 1)
                nc.vector.tensor_tensor(flat(m.hs.lo[:, bass.ds(t, 1), :]), convs[j][1],
                                        flat(m.hs.hi[:, bass.ds(t, 1), :]).bitcast(FP32), ALU.subtract).then_inc(
                    s["hidden_lo"], 1)
                assert own.n == 4

            un.rounds(dve, body)


def swiglu_stage(nc, m, name, weights, following):
    silu = [m.work[:, j, 0:SEQ] for j in range(2)]
    prod = [m.work[:, 2 + j, 0:SEQ] for j in range(2)]
    flat = lambda ap: ap.rearrange("p a t -> p (a t)")
    with stage(nc, name, *Units.SIGNALS, "silu_ready", "product", "hidden_hi", "hidden_lo") as (block, s):
        un = Units(nc, m, s, weights, FT2, KT)

        @block.sync
        def _(sp):
            un.load_all(sp, following)

        @block.tensor
        def _(pe):
            pe.sem_inc(s["unit_done"], 2)
            with pe.Fori(0, FT2 // 2) as i:
                for j in range(2):
                    pe.wait_ge(s["product"], 2 * i + j + 1)
                    for g in range(2):
                        un.multiply(pe, i, j, g, 2 * j + g, m.xs, 0, S2, True, True)

        @block.scalar
        def _(act):
            un.split_hi(act, 0, 0, 0)
            un.split_hi(act, 0, 0, 1)

            def body(i, j, more):
                t = 2 * i + j
                if more:
                    for g in range(2):
                        un.split_hi(act, *un.ahead(i, j), g)
                act.wait_ge(s["unit_done"], 2 * t + 4)
                nc.scalar.activation(silu[j], m.ps[:, 2 * j, :], ACT.Silu).then_inc(s["silu_ready"], 1)
                act.wait_ge(s["product"], t + 3)
                nc.scalar.copy(flat(m.hs.hi[:, bass.ds(t, 1), :]), prod[j]).then_inc(s["hidden_hi"], 1)

            un.rounds(act, body)

        @block.vector
        def _(dve):
            dve.sem_inc(s["product"], 2)
            un.split_lo(dve, 0, 0, 0)
            un.split_lo(dve, 0, 0, 1)

            def body(i, j, more):
                t = 2 * i + j
                if more:
                    for g in range(2):
                        un.split_lo(dve, *un.ahead(i, j), g)
                dve.wait_ge(s["silu_ready"], t + 1)
                nc.vector.tensor_tensor(prod[j], silu[j], m.ps[:, 2 * j + 1, :], ALU.mult).then_inc(s["product"], 1)
                dve.wait_ge(s["hidden_hi"], t + 1)
                nc.vector.tensor_tensor(flat(m.hs.lo[:, bass.ds(t, 1), :]), prod[j],
                                        flat(m.hs.hi[:, bass.ds(t, 1), :]).bitcast(FP32), ALU.subtract).then_inc(
                    s["hidden_lo"], 1)

            un.rounds(dve, body)


def split_out_stage(nc, m, name, weights, k_tiles, hidden, span, x, y_scale, x_scale):
    half = k_tiles // 2
    with stage(nc, name, *Units.SIGNALS, "emptied") as (block, s):
        un = Units(nc, m, s, weights, KT, half)

        @block.sync
        def _(sp):
            un.load_all(sp)

        @block.tensor
        def _(pe):
            pe.sem_inc(s["unit_done"], 2)
            with pe.Fori(0, KT // 2) as i:
                for j in range(2):
                    pe.wait_ge(s["emptied"], 2 * i + j + 1)
                    for g in range(2):
                        un.multiply(pe, i, j, g, 4 * j, hidden, g * half, span, g == 0, g == 1)

        @block.scalar
        def _(act):
            un.split_hi(act, 0, 0, 0)
            un.split_hi(act, 0, 0, 1)

            def body(i, j, more):
                if more:
                    for g in range(2):
                        un.split_hi(act, *un.ahead(i, j), g)

            un.rounds(act, body)

        @block.vector
        def _(dve):
            dve.sem_inc(s["emptied"], 2)
            un.split_lo(dve, 0, 0, 0)
            un.split_lo(dve, 0, 0, 1)

            def body(i, j, more):
                t = 2 * i + j
                if more:
                    for g in range(2):
                        un.split_lo(dve, *un.ahead(i, j), g)
                xt = span.sbuf(x[:, bass.ds(t, 1), :].rearrange("p a t -> p (a t)"))
                dve.wait_ge(s["unit_done"], 2 * t + 4)
                if y_scale != 1.0:
                    assert x_scale == 1.0
                    nc.vector.scalar_tensor_tensor(xt, span.psum(m.ps, 4 * j), y_scale, xt, ALU.mult, ALU.add).then_inc(
                        s["emptied"], 1)
                else:
                    nc.vector.scalar_tensor_tensor(xt, xt, x_scale, span.psum(m.ps, 4 * j), ALU.mult, ALU.add).then_inc(
                        s["emptied"], 1)

            un.rounds(dve, body)


def forget_stage(nc, m, d):
    w = m.ring[:, 0, 0:KT * HEADS1]
    soft, low, c = [m.work[0:HEADS1, k, 0:T1] for k in range(3)]
    logits = S1.psum(m.ps, 0, rows=HEADS1)
    bias = m.col("kv_f_b", 0, HEADS1)
    with stage(nc, "forget", "loaded", "projected", "soft_own", "soft_ready", "own", "c_ready", "stored") as (block, s):
        @block.sync
        def _(sp):
            sp.dma_start(w, d["forget_w"]).then_inc(s["loaded"], 16)
            sp.wait_ge(s["c_ready"], 1)
            sp.dma_start(m.c_dram, c).then_inc(s["stored"], 16)
            sp.wait_ge(s["stored"], 16)

        @block.tensor
        def _(pe):
            pe.wait_ge(s["loaded"], 16)
            project(nc, m.ps, 0, w, lambda k: m.x[:, k, :], KT, S1, rows=HEADS1).then_inc(s["projected"], 1)

        @block.scalar
        def _(act):
            own = Own(act, s["soft_own"])
            act.wait_ge(s["projected"], 1)
            own.then(nc.scalar.activation(S1.sbuf(soft), logits, ACT.Abs, bias=bias))
            own.wait()
            own.then(nc.scalar.activation(soft, soft, ACT.Exp, scale=-1.0))
            own.wait()
            nc.scalar.activation(soft, soft, ACT.Ln, bias=1.0).then_inc(s["soft_ready"], 1)

        @block.vector
        def _(dve):
            own = Own(dve, s["own"])
            dve.wait_ge(s["soft_own"], 1)
            own.then(nc.vector.tensor_scalar(S1.sbuf(low), logits, bias, 0.0, ALU.add, ALU.min))
            own.wait()
            dve.wait_ge(s["soft_ready"], 1)
            own.then(nc.vector.tensor_tensor(low, low, soft, ALU.subtract))
            own.wait()
            own.then(nc.vector.tensor_scalar(low, low, -1.0 / SCALE, None, ALU.mult))
            own.then(nc.vector.memset(soft, 1.0))
            own.wait()
            nc.vector.tensor_tensor_scan(c, soft, low, 0.0, ALU.mult, ALU.add).then_inc(s["c_ready"], 1)


def attention_stage(nc, m, d):
    PAIRS = HEADS1 // 2
    NQ = -(-T1 // QB)
    rows_of = lambda i: min(QB, T1 - i * QB)
    units = [(hh, i) for hh in range(2) for i in range(NQ)]
    NU = len(units)
    HALF, NC = S1.width, 8
    ring = [m.ring[:, j, :] for j in range(2)]
    q_off, k_off, v_off, g_off = [g * KT * P for g in range(4)]
    qT, kT, gate = [[m.work[:, 3 * b + k, 0:T1] for b in range(2)] for k in range(3)]
    v = [m.wide[:, at:at + NQ * P].rearrange("p (n f) -> p n f", f=P) for at in (0, 2976)]
    prob = [m.wide[:, 640 + 528 * b:640 + 528 * b + T1] for b in range(2)]
    probT = [m.wide[:, 1696 + 640 * b:1696 + 640 * (b + 1)] for b in range(2)]
    crow = [m.crow[0:1, 2 * T1 * b:2 * T1 * (b + 1)].rearrange("p (h t) -> p h t", t=T1) for b in range(2)]
    out = m.big[:, 0:KT * T1].rearrange("p (n t) -> p n t", t=T1)
    peak = [m.stat[:, b:b + 1] for b in range(2)]
    shift = [m.stat[:, 2 + b:3 + b] for b in range(2)]
    total = [m.stat[:, 4 + b:5 + b] for b in range(2)]
    scores = [m.ps[:, 2 + 2 * b:4 + 2 * b, :].rearrange("p b t -> p (b t)") for b in range(2)]
    with stage(nc, "attend", "loaded0", "loaded1", "bias0", "bias1", "chunk_psum", "chunk_out", "gate_ready", "scored",
               "shift_ready", "exp_done", "prob_ready", "probT_psum", "probT_ready", "out_psum", "out_done",
               "own") as (block, s):

        def pairs(eng, body):
            with eng.Fori(0, PAIRS // 2 - 1) as it:
                for j in range(2):
                    body(2 * it + j, j, True)
            for j in range(2):
                body(PAIRS - 2 + j, j, j == 0)

        @block.sync
        def _(sp):
            def load(t, j, heads):
                sp.dma_start(ring[j], d["attn_w"][t]).then_inc(s[f"loaded{j}"], 16)
                sp.dma_start(crow[j], heads).then_inc(s[f"bias{j}"], 16)

            by_pair = m.c_dram.rearrange("(n h) t -> n h t", h=2)
            for j in range(2):
                load(j, j, by_pair[j:j + 1])
            with sp.Fori(1, PAIRS // 2) as i:
                for j in range(2):
                    sp.wait_ge(s["out_done"], NU * (2 * i + j - 1) + 2)
                    load(2 * i + j, j, by_pair[bass.ds(2 * i + j, 1)])

        @block.tensor
        def _(pe):
            def score(j, u):
                hh, i = units[u]
                n, nk = rows_of(i), min((i + 1) * QB, T1)
                lo = 64 * hh
                for a, b in ((0, min(nk, 512)), (512, nk)):
                    if b <= a:
                        continue
                    dst = scores[u % 2][0:n, a:b]
                    diag = b > i * QB >= a
                    nc.tensor.matmul(dst, qT[j][lo:lo + HD, i * QB:i * QB + n], kT[j][lo:lo + HD, a:b], start=True,
                                     stop=False)
                    last = nc.tensor.matmul(dst, m.ones[0:1, 0:n], crow[j][0:1, hh, a:b], start=False, stop=not diag)
                    if diag:
                        last = nc.tensor.matmul(scores[u % 2][0:n, i * QB:nk], m.ident[0:n, 0:n],
                                                m.causal[0:n, 0:n], start=False, stop=True)
                last.then_inc(s["scored"], 1)

            def chunk(j, c):
                if c < 6:
                    at, h = (q_off, k_off, g_off)[c // 2], c % 2
                    return [(m.ps[:, 1, 0:HALF], ring[j][:, at + k * P:at + (k + 1) * P],
                             m.x[:, k, h * HALF:(h + 1) * HALF], k) for k in range(KT)]
                return [(m.ps[0:rows_of(n), 1, n % 4 * P:(n % 4 + 1) * P], m.x[:, k, n * QB:n * QB + rows_of(n)],
                         ring[j][:, v_off + k * P:v_off + (k + 1) * P], k)
                        for n in (range(4) if c == 6 else (4,)) for k in range(KT)]

            def run(t, j, c):
                if c == 0:
                    pe.wait_ge(s[f"loaded{j}"], 8 * t - 8 * j + 16)
                pe.wait_ge(s["chunk_out"], NC * t + c + 1)
                for dst, a, b, k in chunk(j, c):
                    last = nc.tensor.matmul(dst, a, b, start=(k == 0), stop=(k == KT - 1))
                last.then_inc(s["chunk_psum"], 1)

            def attend(t, j, u):
                hh, i = units[u]
                n = rows_of(i)
                pe.wait_ge(s["probT_ready"], NU * t + u + 1)
                pe.wait_ge(s["out_done"], NU * t + u + 1)
                for b in range(i + 1):
                    r = rows_of(b)
                    last = nc.tensor.matmul(m.ps[64 * hh:64 * hh + HD, 6 + u % 2, 0:n],
                                            v[j][0:r, b, 64 * hh:64 * hh + HD], probT[u % 2][0:r, b * n:(b + 1) * n],
                                            start=(b == 0), stop=(b == i))
                last.then_inc(s["out_psum"], 1)

            def pair(t, j, more):
                pe.wait_ge(s["chunk_out"], NC * t + NC + 1)
                pe.wait_ge(s[f"bias{j}"], 8 * t - 8 * j + 16)
                score(j, 0)
                for u, (hh, i) in enumerate(units):
                    n = rows_of(i)
                    if u + 1 < NU:
                        score(j, u + 1)
                    filler = more and u < NC
                    if filler:
                        run(t + 1, 1 - j, u)
                    pe.wait_ge(s["prob_ready"], NU * t + u + 1)
                    if u:
                        pe.wait_ge(s["probT_ready"], NU * t + u)
                    for b in range(i + 1):
                        r = rows_of(b)
                        dst, src, one = (m.ps[0:r, 0, b * n:(b + 1) * n],
                                         prob[u % 2][0:n, b * QB:b * QB + r], m.ident[0:n, 0:n])
                        last = nc.tensor.transpose(dst, src, one) if n == QB else nc.tensor.matmul(
                            dst, src, one, start=True, stop=True)
                    last.then_inc(s["probT_psum"], 1)
                    if u:
                        attend(t, j, u - 1)
                attend(t, j, NU - 1)

            for c in range(NC):
                run(0, 0, c)
            pairs(pe, pair)

        @block.scalar
        def _(act):
            def exponentiate(t, u):
                hh, i = units[u]
                n, nk = rows_of(i), min((i + 1) * QB, T1)
                act.wait_ge(s["shift_ready"], NU * t + u + 1)
                nc.scalar.activation(prob[u % 2][0:n, 0:nk], scores[u % 2][0:n, 0:nk], ACT.Exp, scale=SCALE,
                                     bias=shift[u % 2][0:n], accum_out=total[u % 2][0:n]).then_inc(s["exp_done"], 1)

            def empty(t, j, c, first=False):
                act.wait_ge(s["chunk_psum"], NC * t + c + 1)
                if c == 4 and not first:
                    act.wait_ge(s["out_done"], NU * (t - 1) + 2)
                if c < 6:
                    dst, src = (qT, kT, gate)[c // 2][j][:, c % 2 * HALF:(c % 2 + 1) * HALF], m.ps[:, 1, 0:HALF]
                elif c == 6:
                    dst, src = v[j][:, 0:4, :], m.ps[:, 1, :].rearrange("p (n f) -> p n f", f=P)
                else:
                    dst, src = v[j][0:rows_of(4), 4, :], m.ps[0:rows_of(4), 1, 0:P]
                nc.scalar.copy(dst, src).then_inc(s["chunk_out"], 1)

            def open_gate(t, j):
                act.wait_ge(s["chunk_out"], NC * t + NC + 1)
                nc.scalar.activation(gate[j], gate[j], ACT.Sigmoid).then_inc(s["gate_ready"], 1)

            def pair(t, j, more):
                exponentiate(t, 0)
                for u, (hh, i) in enumerate(units):
                    if u + 1 < NU:
                        exponentiate(t, u + 1)
                    n = rows_of(i)
                    act.wait_ge(s["probT_psum"], NU * t + u + 1)
                    full = n * (i + 1) if n == QB else n * i
                    ins = nc.scalar.copy(probT[u % 2][:, 0:full], m.ps[:, 0, 0:full])
                    if n < QB:
                        ins = nc.scalar.copy(probT[u % 2][0:n, full:full + n], m.ps[0:n, 0, full:full + n])
                    ins.then_inc(s["probT_ready"], 1)
                    if more and u < NC:
                        empty(t + 1, 1 - j, u)
                if more:
                    open_gate(t + 1, 1 - j)

            act.sem_inc(s["chunk_out"], 1)
            for c in range(NC):
                empty(0, 0, c, first=True)
            open_gate(0, 0)
            pairs(act, pair)

        @block.vector
        def _(dve):
            OWN = 2 * NU

            def stabilise(t, u):
                hh, i = units[u]
                n, nk = rows_of(i), min((i + 1) * QB, T1)
                dve.wait_ge(s["scored"], NU * t + u + 1)
                nc.vector.reduce_max(peak[u % 2][0:n], scores[u % 2][0:n, 0:nk], AX.X).then_inc(s["own"], 1)

            def negate(u):
                n = rows_of(units[u][1])
                nc.vector.tensor_scalar(shift[u % 2][0:n], peak[u % 2][0:n], -SCALE, None, ALU.mult).then_inc(
                    s["shift_ready"], 1)

            def finish(t, j, u):
                hh, i = units[u]
                rows, cols = slice(64 * hh, 64 * hh + HD), slice(i * QB, i * QB + rows_of(i))
                dve.wait_ge(s["out_psum"], NU * t + u + 1)
                dve.wait_ge(s["gate_ready"], t + 1)
                dst = out[rows, t, cols] if isinstance(t, int) else out[rows, bass.ds(t, 1), cols].rearrange(
                    "p a t -> p (a t)")
                nc.vector.tensor_tensor(dst, m.ps[rows, 6 + u % 2, 0:rows_of(i)], gate[j][rows, cols],
                                        ALU.mult).then_inc(s["out_done"], 1)

            def pair(t, j, more):
                stabilise(t, 0)
                dve.wait_ge(s["own"], OWN * t + 1)
                negate(0)
                for u, (hh, i) in enumerate(units):
                    n, nk = rows_of(i), min((i + 1) * QB, T1)
                    if u + 1 < NU:
                        stabilise(t, u + 1)
                    dve.wait_ge(s["exp_done"], NU * t + u + 1)
                    nc.vector.reciprocal(total[u % 2][0:n], total[u % 2][0:n]).then_inc(s["own"], 1)
                    dve.wait_ge(s["own"], OWN * t + min(2 * u + 3, 2 * NU))
                    if u + 1 < NU:
                        negate(u + 1)
                    nc.vector.tensor_scalar(prob[u % 2][0:n, 0:nk], prob[u % 2][0:n, 0:nk], total[u % 2][0:n], None,
                                            ALU.mult).then_inc(s["prob_ready"], 1)
                    if u >= 2:
                        finish(t, j, u - 2)
                finish(t, j, NU - 2)
                finish(t, j, NU - 1)

            dve.sem_inc(s["out_done"], 2)
            pairs(dve, pair)


def part_one(nc, m, d):
    x_tile = lambda k: m.x[:, k, :]
    y_tile = lambda k: m.y[:, k, :]
    for l in range(2):
        with ExitStack() as ctx:
            mixer_memory(nc, ctx, m, f"m{l}")
            h_lru = m.big[0:LRU, 0:N_LRU * T1].rearrange("p (n t) -> p n t", t=T1)
            h_att = m.big[:, 0:KT * T1].rearrange("p (n t) -> p n t", t=T1)
            if l == 0:
                lru_stage(nc, m, d)
                out_stage(nc, m, "lru_out", d["lru_out"], N_LRU, LRU, lambda k: h_lru[:, k, :], S1, m.x, 1.0, ALPHA, m.x)
            else:
                forget_stage(nc, m, d)
                attention_stage(nc, m, d)
                out_stage(nc, m, "attn_out", d["attn_out"], KT, P, lambda k: h_att[:, k, :], S1, m.x, 1.0, ALPHA, m.x)
        with ExitStack() as ctx:
            ffn_memory(nc, ctx, m, f"f{l}", S1)
            norm_stage(nc, m, f"ln1_{l}", x_tile, x_tile, f"ln1_g{l}", f"ln1_b{l}", LN_EPS, S1, True, m.xs,
                       first_units(d["ffn_in"][l], KT))
            conv_ffn_stage(nc, m, l, d["ffn_in"][l], first_units(d["ffn_out"][l], FT // 2))
            split_out_stage(nc, m, f"ffn_out{l}", d["ffn_out"][l], FT, m.hs, S1, m.x, 1.0, ALPHA)
            norm_stage(nc, m, f"ln2_{l}", x_tile, x_tile, f"ln2_g{l}", f"ln2_b{l}", LN_EPS, S1, True)


class Signals:

    def __init__(self, sem, names):
        self.sem, self.names, self.given = sem, names, 0

    def start(self, eng):
        eng.sem_inc(self.sem, 1)

    def give(self, ins, name):
        assert self.names[self.given % len(self.names)] == name, (name, self.names[self.given % len(self.names)])
        self.given += 1
        ins.then_inc(self.sem, 1)

    def wait(self, eng, rnd, name):
        eng.wait_ge(self.sem, len(self.names) * rnd + self.names.index(name) + 2)

    def wait_round(self, eng, rnd):
        eng.wait_ge(self.sem, len(self.names) * rnd + 1)


def mix_in_stage(nc, m, layer, d):
    NO, NV, NR = 16, 2, 10
    PARTS = (NO + NV + NR) // 2
    rwkv = m.low.rearrange("p (n t) -> p n t", t=SEQ)
    pads = [m.work[:, j, 0:SEQ + 1] for j in range(4)]
    diff = [m.work[:, 4 + j, 0:SEQ] for j in range(4)]
    flat = lambda ap: ap.rearrange("p a t -> p (a t)")
    with stage(nc, f"mix_in{layer}", *Units.SIGNALS, "emptied", "shifted", "own", "v_psum", "v_ready") as (block, s):
        un = Units(nc, m, s, d["mix_in"][layer], PARTS, KT)

        @block.sync
        def _(sp):
            un.load_all(sp)

        @block.tensor
        def _(pe):
            pe.sem_inc(s["unit_done"], 2)
            with pe.Fori(0, PARTS // 2) as i:
                for j in range(2):
                    for g in range(2):
                        pe.wait_ge(s["emptied"], 4 * i + 2 * j + g + 1)
                        un.multiply(pe, i, j, g, 2 * j + g, m.xs, 0, S2, True, True)
            pe.wait_ge(s["emptied"], 4 + NO + NV)
            for n in range(SEQ // P):
                for f in range(NV):
                    last = nc.tensor.transpose(m.ps[:, 4 + n, f * P:(f + 1) * P], m.values[f][:, n * P:(n + 1) * P],
                                               m.ident[:, :])
            last.then_inc(s["v_psum"], 1)

        @block.scalar
        def _(act):
            act.sem_inc(s["emptied"], 4)
            un.split_hi(act, 0, 0, 0)
            un.split_hi(act, 0, 0, 1)

            def body(i, j, more):
                if more:
                    for g in range(2):
                        un.split_hi(act, *un.ahead(i, j), g)
                for g in range(2):
                    u = 4 * i + 2 * j + g
                    act.wait_ge(s["unit_done"], u + 3)
                    if not isinstance(i, int):
                        dst = flat(m.other[:, bass.ds(u, 1), :])
                    elif u < NO + NV:
                        dst = m.values[u - NO]
                    else:
                        r = u - NO - NV
                        if r >= 4:
                            act.wait_ge(s["shifted"], r - 3)
                        dst = pads[r % 4][:, 1:1 + SEQ]
                    nc.scalar.copy(dst, m.ps[:, 2 * j + g, :]).then_inc(s["emptied"], 1)

            with act.Fori(0, NO // 4) as i:
                for j in range(2):
                    body(i, j, True)
            for i in range(NO // 4, PARTS // 2):
                for j in range(2):
                    body(i, j, 2 * i + j + 1 < PARTS)

        @block.vector
        def _(dve):
            for j in range(4):
                nc.vector.memset(pads[j][:, 0:1], 0.0).then_inc(s["own"], 1)
            dve.wait_ge(s["own"], 4)
            un.split_lo(dve, 0, 0, 0)
            un.split_lo(dve, 0, 0, 1)
            with dve.Fori(0, NO // 4) as i:
                for j in range(2):
                    for g in range(2):
                        un.split_lo(dve, *un.ahead(i, j), g)
            own = Own(dve, s["own"], 4)
            for i in range(NO // 4, PARTS // 2):
                for j in range(2):
                    if 2 * i + j + 1 < PARTS:
                        for g in range(2):
                            un.split_lo(dve, *un.ahead(i, j), g)
                    for g in range(2):
                        u = 4 * i + 2 * j + g
                        r = u - NO - NV
                        if r < 0:
                            continue
                        dve.wait_ge(s["emptied"], u + 5)
                        x = pads[r % 4]
                        own.then(nc.vector.tensor_tensor(diff[r % 4], x[:, 0:SEQ], x[:, 1:1 + SEQ], ALU.subtract))
                        own.wait()
                        nc.vector.scalar_tensor_tensor(rwkv[:, r, :], diff[r % 4], m.col(f"rwkv_mu{layer}", r),
                                                       x[:, 1:1 + SEQ], ALU.mult, ALU.add).then_inc(s["shifted"], 1)
            dve.wait_ge(s["v_psum"], 1)
            nc.vector.tensor_copy(m.ret_v[:, :, :], m.ps[:, 4:8, 0:256]).then_inc(s["v_ready"], 1)


class Rwkv:

    def __init__(self, m):
        three = lambda ap: ap.rearrange("p (n t) -> p n t", t=SEQ)
        low, high, ring, wide, work = m.low, m.high, m.ring[:, :, :].rearrange("p a b -> p (a b)"), m.wide, m.work[:, :, :].rearrange("p a b -> p (a b)")
        N = 3 * SEQ
        at = lambda t, i: three(t[:, i:i + N])
        self.r, self.k, self.v = at(low, 0), at(low, N), at(low, 2 * N)
        self.lo = low[:, 3 * N:3 * N + SEQ]
        self.el = at(high, 0)
        self.logw, self.cum, self.prev = at(high, N), at(high, 2 * N), at(high, 3 * N)
        self.a, self.g, self.kk, self.neg = at(ring, 0), at(ring, N), at(ring, 2 * N), at(ring, 3 * N)
        self.square = [ring[:, 4 * N + j * SEQ:4 * N + (j + 1) * SEQ] for j in range(2)]
        self.prod = [ring[:, 4 * N + (2 + j) * SEQ:4 * N + (3 + j) * SEQ] for j in range(2)]
        self.bonus = at(wide, 0)
        self.lo_w = wide[:, N:N + 768]
        self.mv = wide[:, N + 768:N + 768 + SEQ]
        self.mv_pad = wide[:, N + 768 + SEQ:N + 768 + 2 * SEQ]
        S = 3 * P
        sl = lambda t, i: t[:, i:i + S].rearrange("p (n t) -> p n t", t=P)
        spare = m.y[:, :, :].rearrange("p a b -> p (a b)")[:, 3 * T1:8 * T1]
        self.st_a, self.st_b, self.st_k, self.st_r, self.st_v = [sl(spare, i * S) for i in range(5)]
        self.tok_b, self.tok_v, self.x = [work[:, i * S:(i + 1) * S] for i in range(3)]
        self.tok_k = [work[:, (3 + i) * S:(4 + i) * S] for i in range(2)]
        self.u = [work[:, (5 + i) * S:(6 + i) * S] for i in range(2)]
        self.state = sl(work, 7 * S)
        self.end = [sl(work, (8 + i) * S) for i in range(2)]
        M = 6 * P
        free = [high[:, N + i * M:N + (i + 1) * M] for i in range(7)]
        free += [ring[:, 3 * N + i * M:3 * N + (i + 1) * M] for i in range(4)]
        free += [wide[:, N:N + M]]
        (self.E1, self.E2, self.GA, self.GB, self.HA, self.HB, self.ZA, self.ZB, self.Z, self.MAK, self.MRB,
         self.MRK) = free
        assert N + 7 * M <= 14 * SEQ + 384 and 3 * N + 4 * M <= 8192 and 10 * S <= 8 * 532


def rwkv_prepare_stage(nc, m, layer, d):
    w = Rwkv(m)
    C, LW = 3, layer == 1
    col = lambda n, c: m.col(f"rwkv_{n}{layer}", c)
    with stage(nc, f"rwkv_prep{layer}", "loaded", "lo_ready", "mv_ready", "z_psum", "z_out", "cum_ready", "exp_out", "sq_ready",
               "ss_psum", "ss_ready", "root_ready", "prod_ready", "bonus_psum", "bonus_out", "v_saved", "own",
               "scaled") as (block, s):
        @block.sync
        def _(sp):
            sp.dma_start(w.lo_w, d["rwkv_lo"][layer]).then_inc(s["loaded"], 16)
            sp.wait_ge(s["loaded"], 16)

        @block.tensor
        def _(pe):
            pe.wait_ge(s["loaded"], 16)
            pe.wait_ge(s["lo_ready"], 2)
            if LW:
                pe.wait_ge(s["mv_ready"], 1)
            for c in range(C):
                b = 4 * (c % 2)
                if c == 2:
                    pe.wait_ge(s["z_out"], 1)
                for q, (lo, n) in enumerate(((0, 32), (32, 32), (64, 64))):
                    last = nc.tensor.matmul(m.ps[:, b + q, :], w.lo_w[lo:lo + n, c * P:(c + 1) * P], w.lo[lo:lo + n, :],
                                            start=True, stop=True)
                if LW:
                    last = nc.tensor.matmul(m.ps[:, b + 3, :], w.lo_w[32:48, 384 + c * P:384 + (c + 1) * P],
                                            w.mv[32:48, :], start=True, stop=True)
                last.then_inc(s["z_psum"], 1)
            pe.wait_ge(s["z_out"], C)
            for c in range(C):
                pe.wait_ge(s["sq_ready"], c + 1)
                nc.tensor.matmul(m.ps[:, c, :], m.head_ones, w.square[c % 2], start=True, stop=True).then_inc(s["ss_psum"], 1)
                pe.wait_ge(s["prod_ready"], c + 1)
                nc.tensor.matmul(m.ps[:, 4 + c, :], m.head_ones, w.prod[c % 2], start=True, stop=True).then_inc(s["bonus_psum"], 1)

        @block.scalar
        def _(act):
            nc.scalar.activation(w.lo[0:32, :], w.lo[0:32, :], ACT.Tanh).then_inc(s["lo_ready"], 1)
            nc.scalar.activation(w.lo[64:128, :], w.lo[64:128, :], ACT.Sigmoid).then_inc(s["lo_ready"], 1)
            for c in range(C):
                b = 4 * (c % 2)
                act.wait_ge(s["z_psum"], c + 1)
                nc.scalar.activation(w.logw[:, c, :], m.ps[:, b, :], ACT.Sigmoid, bias=col("w0", c))
                nc.scalar.activation(w.a[:, c, :], m.ps[:, b + 1, :], ACT.Sigmoid, bias=col("a0", c))
                if LW:
                    nc.scalar.activation(w.neg[:, c, :], m.ps[:, b + 3, :], ACT.Sigmoid, bias=m.col("rwkv_v0", c))
                nc.scalar.copy(w.g[:, c, :], m.ps[:, b + 2, :]).then_inc(s["z_out"], 1)
            for c in range(C):
                act.wait_ge(s["cum_ready"], c + 1)
                nc.scalar.activation(w.prev[:, c, :], w.prev[:, c, :], ACT.Exp)
                nc.scalar.activation(w.el[:, c, :], w.cum[:, c, :], ACT.Exp)
                nc.scalar.activation(w.neg[:, c, :], w.cum[:, c, :], ACT.Exp, scale=-1.0).then_inc(s["exp_out"], 1)
            for c in range(C):
                act.wait_ge(s["ss_ready"], c + 1)
                nc.scalar.activation(w.logw[:, c, :], w.logw[:, c, :], ACT.Sqrt).then_inc(s["root_ready"], 1)

        @block.gpsimd
        def _(pool):
            if not LW:
                nc.gpsimd.tensor_copy(m.v_first[:, :, :], w.v).then_inc(s["v_saved"], 1)
                pool.wait_ge(s["v_saved"], 1)

        @block.vector
        def _(dve):
            own = Own(dve, s["own"])
            if LW:
                src = m.other[32:48, 15, :]
                own.then(nc.vector.memset(w.mv_pad[32:48, 0:1], 0.0))
                own.then(nc.vector.tensor_copy(w.mv_pad[32:48, 1:SEQ], src[:, 0:SEQ - 1]))
                own.wait()
                own.then(nc.vector.tensor_tensor(w.mv[32:48, :], w.mv_pad[32:48, 0:SEQ], src, ALU.subtract))
                own.wait()
                nc.vector.scalar_tensor_tensor(w.mv[32:48, :], w.mv[32:48, :],
                                               m.vec[32:48, COLS["rwkv_vres_mu"][0]:COLS["rwkv_vres_mu"][0] + 1], src,
                                               ALU.mult, ALU.add).then_inc(s["mv_ready"], 1)
            own.then(nc.vector.memset(m.reset, 1.0))
            own.wait()
            own.then(nc.vector.memset(m.reset.rearrange("p (n c) -> p n c", c=HD)[:, :, 0:1], 0.0))
            for c in range(C):
                dve.wait_ge(s["z_out"], c + 1)
                L, cum, k, v, r, a = (x[:, c, :] for x in (w.logw, w.cum, w.k, w.v, w.r, w.a))
                own.then(nc.vector.tensor_scalar(L, L, -math.exp(-0.5), None, ALU.mult))
                own.wait()
                own.then(nc.vector.tensor_tensor_scan(cum, m.reset, L, 0.0, ALU.mult, ALU.add))
                if LW:
                    sv = w.neg[:, c, :]
                    own.then(nc.vector.tensor_tensor(w.prev[:, c, :], m.v_first[:, c, :], v, ALU.subtract))
                    own.wait()
                    own.then(nc.vector.tensor_tensor(w.prev[:, c, :], w.prev[:, c, :], sv, ALU.mult))
                    own.wait()
                    own.then(nc.vector.tensor_tensor(v, v, w.prev[:, c, :], ALU.add))
                own.wait()
                nc.vector.tensor_tensor(w.prev[:, c, :], cum, L, ALU.subtract).then_inc(s["cum_ready"], 1)
                own.then(nc.vector.tensor_scalar(w.kk[:, c, :], k, col("k_k", c), None, ALU.mult))
                own.wait()
                if c >= 2:
                    dve.wait_ge(s["ss_psum"], c - 1)
                nc.vector.tensor_tensor(w.square[c % 2], w.kk[:, c, :], w.kk[:, c, :], ALU.mult).then_inc(s["sq_ready"], 1)
                if c >= 2:
                    dve.wait_ge(s["bonus_psum"], c - 1)
                own.then(nc.vector.tensor_scalar(w.prod[c % 2], a, -1.0, col("k_a", c), ALU.add, ALU.mult))
                own.wait()
                own.then(nc.vector.scalar_tensor_tensor(k, w.prod[c % 2], 1.0, k, ALU.add, ALU.mult))
                own.wait()
                nc.vector.scalar_tensor_tensor(w.prod[c % 2], r, col("r_k", c), k, ALU.mult, ALU.mult).then_inc(
                    s["prod_ready"], 1)
            for c in range(C):
                dve.wait_ge(s["ss_psum"], c + 1)
                nc.vector.tensor_scalar(w.logw[:, c, :], m.ps[:, c, :], 1e-24, None, ALU.max).then_inc(s["ss_ready"], 1)
                dve.wait_ge(s["bonus_psum"], c + 1)
                own.then(nc.vector.tensor_tensor(w.bonus[:, c, :], m.ps[:, 4 + c, :], w.v[:, c, :], ALU.mult))
            for c in range(C):
                kk, a, k, r, neg, n = (x[:, c, :] for x in (w.kk, w.a, w.k, w.r, w.neg, w.logw))
                dve.wait_ge(s["root_ready"], c + 1)
                own.then(nc.vector.reciprocal(n, n))
                own.wait()
                own.then(nc.vector.tensor_tensor(kk, kk, n, ALU.mult))
                own.wait()
                own.then(nc.vector.tensor_tensor(a, kk, a, ALU.mult))
                own.wait()
                dve.wait_ge(s["exp_out"], c + 1)
                nc.vector.tensor_tensor(a, a, neg, ALU.mult).then_inc(s["scaled"], 1)
                nc.vector.scalar_tensor_tensor(kk, kk, -1.0, w.prev[:, c, :], ALU.mult, ALU.mult).then_inc(s["scaled"], 1)
                nc.vector.tensor_tensor(k, k, neg, ALU.mult).then_inc(s["scaled"], 1)
                nc.vector.tensor_tensor(r, r, w.el[:, c, :], ALU.mult).then_inc(s["scaled"], 1)


def rwkv_recurrence_stage(nc, m, layer):
    w = Rwkv(m)
    H = 6
    half = lambda h: slice(64 * (h % 2), 64 * (h % 2) + 64)
    pair = lambda q: m.ps[:, 2 * q:2 * q + 2, 0:3 * P]
    set_psum = lambda q, h: m.ps[:, 2 * q + h % 2, (h // 2) * P:(h // 2 + 1) * P]
    block_of = lambda M, h: M[:, (h % 2 * 3 + h // 2) * P:(h % 2 * 3 + h // 2 + 1) * P]
    shaped = lambda M: M.rearrange("p (a b) -> p a b", a=2)
    four = lambda M: M.rearrange("p (a b c) -> p a b c", a=2, b=3)
    spread = lambda mask: mask.unsqueeze(1).unsqueeze(1).broadcast_to([P, 2, 3, P])
    with stage(nc, f"rwkv_rec{layer}", "made", "vec_out", "act_out", "staged", "ones_added") as (block, s):
        HALVES = ("g1", "h1", "z1", "g2", "h2", "z2", "g3", "z3", "t3", "q3", "z4", "t4", "q4", "z5")
        spell = lambda names: [x for n in names for x in ((f"{n}_even", f"{n}_odd") if n in HALVES else (n,))]
        made = Signals(s["made"], spell(
            ["tok", "ab", "ba", "ak", "g1", "h1", "z1", "rb", "g2", "h2", "z2", "rk", "g3", "z3", "t3", "q3", "z4", "t4",
             "q4", "z5", "x0", "u0", "y0", "s0", "x1", "u1", "y1", "s1"]))
        vec = Signals(s["vec_out"], spell(
            ["st_r", "tok_v", "GA", "E1", "E2", "HA", "MAK", "z1", "MRB", "z2", "MRK", "z3", "z4", "z5", "u0", "s0", "u1",
             "s1"]))
        act_ = Signals(s["act_out"], spell(
            ["st_a", "tok_bk", "g1", "h1", "g2", "h2", "g3", "t3", "q3", "t4", "q4", "x0", "y0", "x1", "y1"]))

        @block.gpsimd
        def _(pool):
            nc.gpsimd.memset(w.state, 0.0)
            nc.gpsimd.memset(w.x, 0.0)
            for c in range(2):
                nc.gpsimd.memset(w.u[c], 0.0)
                nc.gpsimd.memset(w.tok_k[c], 0.0)
            nc.gpsimd.memset(m.ident[0:1, 0:1], 1.0).then_inc(s["staged"], 1)

            def slices(t):
                for dst, src in ((w.st_b, w.a), (w.st_k, w.k), (w.st_v, w.v)):
                    nc.gpsimd.tensor_copy(dst, src[:, :, bass.ds(t * P, P)]).then_inc(s["staged"], 1)

            def around(t, more):
                vec.wait_round(pool, t)
                for c in range(2):
                    at_end = w.el.rearrange("p n (c s) -> p n c s", s=HD)[:, :, bass.ds(2 * t + c, 1), HD - 1]
                    nc.gpsimd.tensor_tensor(w.end[c], at_end.broadcast_to([P, 3, P]),
                                            m.head_ones.unsqueeze(1).broadcast_to([P, 3, P]), ALU.mult).then_inc(
                        s["staged"], 1)
                vec.wait(pool, t, "HA")
                nc.gpsimd.tensor_tensor(four(w.ZA), four(w.HA), spread(m.ident[:, :]), ALU.add).then_inc(s["ones_added"], 1)
                if more:
                    made.wait(pool, t, "rk")
                    slices(t + 1)

            slices(0)
            with pool.Fori(0, 3) as t:
                around(t, True)
            around(3, False)

        @block.tensor
        def _(pe):
            def batch(name, q, left, right):
                for h in range(H):
                    last = nc.tensor.matmul(set_psum(q, h), left(h), right(h), start=True, stop=True)
                made.give(last, name)

            def halves(name, q, left, right, *needs):
                for odd, which in enumerate(("even", "odd")):
                    for signals, needed in needs:
                        signals.wait(pe, t, f"{needed}_{which}")
                    for h in range(odd, H, 2):
                        if right is None:
                            last = nc.tensor.transpose(set_psum(q, h), left(h), m.ident[:, :])
                        else:
                            last = nc.tensor.matmul(set_psum(q, h), left(h), right(h), start=True, stop=True)
                    made.give(last, f"{name}_{which}")

            feat = lambda x: (lambda h: x[half(h), h // 2, :])
            mat = lambda M: (lambda h: block_of(M, h))

            made.start(pe)
            with pe.Fori(0, 4) as t:
                pe.wait_ge(s["staged"], 5 * t + 4)
                act_.wait(pe, t, "st_a")
                vec.wait(pe, t, "st_r")
                for b, src in enumerate((w.st_b, w.st_k, w.st_v)):
                    for c in range(3):
                        last = nc.tensor.transpose(m.ps[:, b, c * P:(c + 1) * P], src[:, c, :], m.ident[:, :])
                made.give(last, "tok")
                batch("ab", 2, feat(w.st_a), feat(w.st_b))
                batch("ba", 3, feat(w.st_b), feat(w.st_a))
                act_.wait(pe, t, "tok_bk")
                batch("ak", 0, feat(w.st_k), feat(w.st_a))
                vec.wait(pe, t, "tok_v")
                vec.wait(pe, t, "HA")
                halves("g1", 1, mat(w.HA), mat(w.GA))
                halves("h1", 2, mat(w.GA), mat(w.HA))
                pe.wait_ge(s["ones_added"], t + 1)
                halves("z1", 3, mat(w.GB), mat(w.ZA), (act_, "g1"))
                vec.wait(pe, t, "MAK")
                batch("rb", 0, feat(w.st_b), feat(w.st_r))
                halves("g2", 1, mat(w.HB), mat(w.GB), (act_, "h1"))
                halves("h2", 2, mat(w.GB), mat(w.HB))
                halves("z2", 3, mat(w.GA), mat(w.ZB), (act_, "g2"), (vec, "z1"))
                vec.wait(pe, t, "MRB")
                batch("rk", 0, feat(w.st_k), feat(w.st_r))
                halves("g3", 1, mat(w.HA), mat(w.GA), (act_, "h2"))
                halves("z3", 3, mat(w.GB), mat(w.ZA), (act_, "g3"), (vec, "z2"))
                halves("t3", 1, mat(w.ZB), None, (vec, "z3"))
                halves("q3", 2, mat(w.E1), mat(w.ZB))
                halves("z4", 3, mat(w.HA), mat(w.HB), (act_, "q3"))
                halves("t4", 1, mat(w.ZA), None, (vec, "z4"))
                halves("q4", 2, mat(w.E2), mat(w.ZA))
                halves("z5", 3, mat(w.HA), mat(w.HB), (act_, "q4"))
                vec.wait(pe, t, "z5_odd")
                for c in range(2):
                    rows = slice(64 * c, 64 * c + 64)
                    if c == 1:
                        vec.wait(pe, t, "s0")
                    for n in range(3):
                        dst = m.ps[rows, 0, n * P:(n + 1) * P]
                        nc.tensor.matmul(dst, w.st_a[:, n, rows], w.state[:, n, :], start=True, stop=False)
                        for h in (2 * n, 2 * n + 1):
                            last = nc.tensor.matmul(m.ps[rows, 0, h * HD:(h + 1) * HD], block_of(w.MAK, h)[:, rows],
                                                    w.tok_v[:, h * HD:(h + 1) * HD], start=False, stop=(h % 2 == 1))
                    made.give(last, f"x{c}")
                    act_.wait(pe, t, f"x{c}")
                    for h in range(H):
                        last = nc.tensor.matmul(m.ps[rows, 1, h * HD:(h + 1) * HD], block_of(w.Z, h)[:, rows],
                                                w.x[:, h * HD:(h + 1) * HD], start=True, stop=True)
                    made.give(last, f"u{c}")
                    vec.wait(pe, t, f"u{c}")
                    if c == 1:
                        act_.wait(pe, t, "y0")
                    for n in range(3):
                        dst = m.ps[:, 2, n * HD:(n + 1) * HD]
                        nc.tensor.matmul(dst, w.state[:, n, :], w.st_r[:, n, rows], start=True, stop=False)
                        for h in (2 * n, 2 * n + 1):
                            dst, cols = m.ps[half(h), 2, n * HD:(n + 1) * HD], slice(h * HD, (h + 1) * HD)
                            nc.tensor.matmul(dst, w.u[c][:, cols], block_of(w.MRB, h)[:, rows], start=False, stop=False)
                            last = nc.tensor.matmul(dst, w.tok_v[:, cols], block_of(w.MRK, h)[:, rows], start=False, stop=True)
                    made.give(last, f"y{c}")
                    for n in range(3):
                        dst, cols = m.ps[:, 3, n * P:(n + 1) * P], slice(n * P, (n + 1) * P)
                        nc.tensor.matmul(dst, m.ident[:, :], w.state[:, n, :], start=True, stop=False)
                        nc.tensor.matmul(dst, w.tok_b[:, cols], w.u[c][:, cols], start=False, stop=False)
                        last = nc.tensor.matmul(dst, w.tok_k[c][:, cols], w.tok_v[:, cols], start=False, stop=True)
                    made.give(last, f"s{c}")

        @block.scalar
        def _(act):
            def take(t, name, src, dst):
                made.wait(act, t, name)
                act_.give(nc.scalar.copy(dst, src), name)

            def take_halves(t, name, q, dst):
                for odd, which in enumerate(("even", "odd")):
                    take(t, f"{name}_{which}", pair(q)[:, odd, :], shaped(dst)[:, odd, :])

            act_.start(act)
            with act.Fori(0, 4) as t:
                made.wait_round(act, t)
                act_.give(nc.scalar.copy(w.st_a, w.kk[:, :, bass.ds(t * P, P)]), "st_a")
                made.wait(act, t, "tok")
                nc.scalar.copy(w.tok_b, m.ps[:, 0, 0:3 * P])
                nc.scalar.copy(w.tok_k[0][0:64, :], m.ps[0:64, 1, 0:3 * P])
                act_.give(nc.scalar.copy(w.tok_k[1][64:128, :], m.ps[64:128, 1, 0:3 * P]), "tok_bk")
                take_halves(t, "g1", 1, w.GB)
                take_halves(t, "h1", 2, w.HB)
                take_halves(t, "g2", 1, w.GA)
                act.wait_ge(s["ones_added"], t + 1)
                take_halves(t, "h2", 2, w.HA)
                take_halves(t, "g3", 1, w.GB)
                take_halves(t, "t3", 1, w.HA)
                take_halves(t, "q3", 2, w.HB)
                take_halves(t, "t4", 1, w.HA)
                take_halves(t, "q4", 2, w.HB)
                for c in range(2):
                    rows = slice(64 * c, 64 * c + 64)
                    take(t, f"x{c}", m.ps[rows, 0, 0:3 * P], w.x[rows, :])
                    take(t, f"y{c}", m.ps[:, 2, 0:192].rearrange("p (n t) -> p n t", t=HD),
                         w.v[:, :, bass.ds(t * P + 64 * c, HD)])

        @block.vector
        def _(dve):
            def masked(t, name, q, mask, dst, given):
                made.wait(dve, t, name)
                vec.give(nc.vector.tensor_tensor(four(dst), m.ps[:, 2 * q:2 * q + 2, 0:3 * P].rearrange(
                    "p a (b c) -> p a b c", c=P), spread(mask), ALU.mult), given)

            def added(t, name, old, dst, before=None):
                for odd, which in enumerate(("even", "odd")):
                    if before:
                        vec.wait(dve, t, f"{before}_{which}")
                    made.wait(dve, t, f"{name}_{which}")
                    vec.give(nc.vector.tensor_tensor(shaped(dst)[:, odd, :], pair(3)[:, odd, :], shaped(old)[:, odd, :],
                                                     ALU.add), f"{name}_{which}")

            vec.start(dve)
            with dve.Fori(0, 4) as t:
                made.wait_round(dve, t)
                vec.give(nc.vector.tensor_copy(w.st_r, w.r[:, :, bass.ds(t * P, P)]), "st_r")
                made.wait(dve, t, "tok")
                vec.give(nc.vector.tensor_copy(w.tok_v, m.ps[:, 2, 0:3 * P]), "tok_v")
                masked(t, "ab", 2, m.low16, w.GA, "GA")
                masked(t, "ab", 2, m.edge16, w.E1, "E1")
                masked(t, "ab", 2, m.edge32, w.E2, "E2")
                masked(t, "ba", 3, m.up16, w.HA, "HA")
                masked(t, "ak", 0, m.strict64, w.MAK, "MAK")
                dve.wait_ge(s["ones_added"], t + 1)
                added(t, "z1", w.ZA, w.ZB)
                masked(t, "rb", 0, m.upto64, w.MRB, "MRB")
                added(t, "z2", w.ZB, w.ZA, "z1")
                masked(t, "rk", 0, m.upto64, w.MRK, "MRK")
                added(t, "z3", w.ZA, w.ZB, "z2")
                added(t, "z4", w.ZB, w.ZA, "z3")
                added(t, "z5", w.ZA, w.Z, "z4")
                for c in range(2):
                    rows = slice(64 * c, 64 * c + 64)
                    made.wait(dve, t, f"u{c}")
                    vec.give(nc.vector.tensor_copy(w.u[c][rows, :], m.ps[rows, 1, 0:3 * P]), f"u{c}")
                    made.wait(dve, t, f"s{c}")
                    dve.wait_ge(s["staged"], 5 * t + 6)
                    vec.give(nc.vector.tensor_tensor(w.state, m.ps[:, 3, 0:3 * P].rearrange("p (n t) -> p n t", t=P),
                                                     w.end[c], ALU.mult), f"s{c}")


def rwkv_finish_stage(nc, m, layer):
    w = Rwkv(m)
    C, col = 3, lambda n, c: m.col(f"rwkv_{n}{layer}", c)
    with stage(nc, f"rwkv_fin{layer}", "mean_psum", "centred", "squared", "var_psum", "root_ready", "own", "done") as (block, s):
        @block.tensor
        def _(pe):
            for c in range(C):
                nc.tensor.matmul(m.ps[:, c, :], m.head_ones, w.v[:, c, :], start=True, stop=True).then_inc(s["mean_psum"], 1)
            for c in range(C):
                pe.wait_ge(s["squared"], c + 1)
                nc.tensor.matmul(m.ps[:, 4 + c, :], m.head_ones, w.cum[:, c, :], start=True, stop=True).then_inc(s["var_psum"], 1)

        @block.scalar
        def _(act):
            for c in range(C):
                act.wait_ge(s["centred"], c + 1)
                nc.scalar.activation(w.cum[:, c, :], w.logw[:, c, :], ACT.Square).then_inc(s["squared"], 1)
            for c in range(C):
                act.wait_ge(s["var_psum"], c + 1)
                nc.scalar.activation(w.prev[:, c, :], m.ps[:, 4 + c, :], ACT.Sqrt, scale=1.0 / HD,
                                     bias=m.eps[:, 2:3]).then_inc(s["root_ready"], 1)

        @block.vector
        def _(dve):
            own = Own(dve, s["own"])
            for c in range(C):
                dve.wait_ge(s["mean_psum"], c + 1)
                nc.vector.scalar_tensor_tensor(w.logw[:, c, :], m.ps[:, c, :], -1.0 / HD, w.v[:, c, :], ALU.mult,
                                               ALU.add).then_inc(s["centred"], 1)
            for c in range(C):
                y, r = w.logw[:, c, :], w.prev[:, c, :]
                dve.wait_ge(s["root_ready"], c + 1)
                own.then(nc.vector.reciprocal(r, r))
                own.wait()
                own.then(nc.vector.tensor_tensor(y, y, r, ALU.mult))
                own.wait()
                own.then(nc.vector.tensor_scalar(y, y, col("ln_w", c), col("ln_b", c), ALU.mult, ALU.add))
                own.wait()
                own.then(nc.vector.tensor_tensor(y, y, w.bonus[:, c, :], ALU.add))
                own.wait()
                nc.vector.tensor_tensor(m.y[:, c, 0:SEQ], y, w.g[:, c, :], ALU.mult).then_inc(s["done"], 1)


TOPK = 128
RET_COLS = 2 * SEQ + P + 4 * SEQ


def mix_out_ring(m):
    return [m.ring[:, 1, j * KT * P:(j + 1) * KT * P] for j in range(2)]


HIDDEN = -3.0e38
TAKEN = -3.4e38


class Dsa:

    def __init__(self, m):
        low, high, wide = m.low, m.high, m.wide
        slot = lambda t, i: t[:, i * SEQ:(i + 1) * SEQ]
        self.qlat = low[:, 0:6 * SEQ].rearrange("p (n t) -> p n t", t=SEQ)
        self.olat = high[:, 0:6 * SEQ].rearrange("p (n t) -> p n t", t=SEQ)
        self.mask = [m.causal[:, :]] + [slot(high, 6 + b)[:, 0:(b + 2) * QB] for b in range(3)]
        self.logits = [slot(high, 9), slot(high, 10), slot(low, 6), slot(low, 7)]
        self.probT = [slot(high, 11 + j) for j in range(2)]
        self.relu = [slot(low, 6 + j) for j in range(4)]
        self.root, self.square = wide[:, 0:SEQ], wide[:, SEQ:2 * SEQ]
        self.c_tok = wide[:, 2 * SEQ:3 * SEQ].rearrange("p (n f) -> p n f", f=P)
        self.score = wide[:, 3 * SEQ:4 * SEQ]
        self.both = wide[:, 4 * SEQ:4 * SEQ + 768]
        self.up = wide[:, 4 * SEQ:4 * SEQ + 384]
        self.down = wide[:, 4 * SEQ + 384:4 * SEQ + 768]
        self.iw = wide[:, 6 * SEQ:6 * SEQ + 32]
        self.top = wide[:, 6 * SEQ + 32:6 * SEQ + 40]


def dsa_stage(nc, m, layer, d):
    w = Dsa(m)
    half = lambda h: slice(64 * (h % 2), 64 * (h % 2) + 64)
    c = m.other[:, 3, :]
    NB, IH, H = SEQ // QB, 8, 6
    with stage(nc, f"dsa_in{layer}", "loaded", "squared", "ss_psum", "root_ready", "own", "c_scaled", "c_ready", "iw_psum", "c_psum",
               "q_psum", "q_out", "tok_ready") as (block, s):
        @block.sync
        def _(sp):
            sp.dma_start(w.both, d["dsa_w"][layer]).then_inc(s["loaded"], 16)
            sp.wait_ge(s["loaded"], 16)

        @block.tensor
        def _(pe):
            for n in range(NB):
                last = nc.tensor.transpose(m.ps[:, 7, n * 8:(n + 1) * 8], m.other[0:8, 15, n * P:(n + 1) * P],
                                           m.ident[0:8, 0:8])
            last.then_inc(s["iw_psum"], 1)
            pe.wait_ge(s["squared"], 1)
            nc.tensor.matmul(m.ps[:, 6, :], m.ones[:, :], w.square, start=True, stop=True).then_inc(s["ss_psum"], 1)
            pe.wait_ge(s["loaded"], 16)
            for h in range(H):
                nc.tensor.matmul(m.ps[:, h, :], w.up[half(h), (h // 2) * P:(h // 2 + 1) * P], m.other[half(h), h // 2, :],
                                 start=True, stop=True).then_inc(s["q_psum"], 1)
            pe.wait_ge(s["c_ready"], 1)
            for n in range(NB):
                last = nc.tensor.transpose(m.ps[:, 6, n * P:(n + 1) * P], c[:, n * P:(n + 1) * P], m.ident[:, :])
            last.then_inc(s["c_psum"], 1)

        @block.scalar
        def _(act):
            nc.scalar.activation(w.square, c, ACT.Square).then_inc(s["squared"], 1)
            act.wait_ge(s["ss_psum"], 1)
            nc.scalar.activation(w.root, m.ps[:, 6, :], ACT.Sqrt, scale=1.0 / P, bias=m.eps[:, 1:2]).then_inc(s["root_ready"], 1)
            for h in range(H):
                if h == 3:
                    act.wait_ge(s["c_scaled"], 1)
                    nc.scalar.activation(c, c, ACT.Copy, scale=m.col(f"dsa_kv_norm{layer}")).then_inc(s["c_ready"], 1)
                act.wait_ge(s["q_psum"], h + 1)
                nc.scalar.mul(w.qlat[:, h, :], m.ps[:, h, :], SCALE).then_inc(s["q_out"], 1)

        @block.vector
        def _(dve):
            own = Own(dve, s["own"])
            dve.wait_ge(s["iw_psum"], 1)
            own.then(nc.vector.tensor_scalar(w.iw, m.ps[:, 7, 0:32], SCALE * IH ** -0.5, None, ALU.mult))
            dve.wait_ge(s["root_ready"], 1)
            own.then(nc.vector.reciprocal(w.root, w.root))
            own.wait()
            nc.vector.tensor_tensor(c, c, w.root, ALU.mult).then_inc(s["c_scaled"], 1)
            dve.wait_ge(s["c_psum"], 1)
            nc.vector.tensor_copy(w.c_tok, m.ps[:, 6, :].rearrange("p (n f) -> p n f", f=P)).then_inc(s["tok_ready"], 1)

    with stage(nc, f"dsa_index{layer}", "rel_psum", "relu_ready", "relu_used", "scored", "hidden", "own", "mask_ready") as (block, s):
        blocks = (3, 2, 1)

        @block.tensor
        def _(pe):
            for i, b in enumerate(blocks):
                for h in range(IH):
                    if i:
                        pe.wait_ge(s["relu_ready"], IH * (i - 1) + h + 1)
                    nc.tensor.matmul(m.ps[:, h, 0:(b + 1) * QB], m.other[half(h), 4 + h // 2, b * QB:(b + 1) * QB],
                                     m.other[half(h), 8, 0:(b + 1) * QB], start=True, stop=True).then_inc(s["rel_psum"], 1)

        @block.scalar
        def _(act):
            for i, b in enumerate(blocks):
                for h in range(IH):
                    u = IH * i + h
                    act.wait_ge(s["rel_psum"], u + 1)
                    if u >= 4:
                        act.wait_ge(s["relu_used"], u - 3)
                    nc.scalar.activation(w.relu[h % 4][:, 0:(b + 1) * QB], m.ps[:, h, 0:(b + 1) * QB],
                                         ACT.Relu).then_inc(s["relu_ready"], 1)

        @block.gpsimd
        def _(pool):
            for i, b in enumerate(blocks):
                pool.wait_ge(s["relu_used"], IH * (i + 1))
                diag = w.score[:, b * QB:(b + 1) * QB]
                nc.gpsimd.affine_select(out=diag, in_=diag, compare_op=ALU.is_ge, fill=HIDDEN, base=0,
                                        pattern=[[-1, QB]], channel_multiplier=1).then_inc(s["hidden"], 1)

        @block.vector
        def _(dve):
            own = Own(dve, s["own"])
            for i, b in enumerate(blocks):
                n = (b + 1) * QB
                score = w.score[:, 0:n]
                for h in range(IH):
                    u = IH * i + h
                    dve.wait_ge(s["relu_ready"], u + 1)
                    iw = w.iw[:, b * IH + h:b * IH + h + 1]
                    if h == 0:
                        if i:
                            dve.wait_ge(s["mask_ready"], i)
                        nc.vector.tensor_scalar(score, w.relu[0][:, 0:n], iw, None, ALU.mult).then_inc(s["relu_used"], 1)
                    else:
                        dve.wait_ge(s["relu_used"], u)
                        nc.vector.scalar_tensor_tensor(score, w.relu[h % 4][:, 0:n], iw, score, ALU.mult,
                                                       ALU.add).then_inc(s["relu_used"], 1)
                dve.wait_ge(s["hidden"], i + 1)
                for _ in range(TOPK // 8):
                    own.then(nc.vector.max(w.top, score))
                    own.wait()
                    own.then(nc.vector.match_replace(score, w.top, score, TAKEN))
                    own.wait()
                nc.vector.tensor_scalar(w.mask[b], score, 0.5 * (HIDDEN + TAKEN), NEG, ALU.is_gt, ALU.mult).then_inc(
                    s["mask_ready"], 1)

    units = [(b, h) for b in range(NB) for h in range(H)]
    NU = len(units)
    LB, SB = len(w.logits), 3
    peak, shift, total = ([m.stat[:, LB * i + j:LB * i + j + 1] for j in range(LB)] for i in range(3))
    score_bank = (0, 1, 6)
    with stage(nc, f"dsa_att{layer}", "scored", "masked", "shift_ready", "exp_done", "own", "prob_ready", "probT_psum",
               "probT_ready", "out_psum", "out_ready", "final_psum", "final_ready", "preloaded") as (block, s):
        @block.sync
        def _(sp):
            sp.dma_start(m.ring[:, 0, 0:RET_COLS], d["ret_const"]).then_inc(s["preloaded"], 16)
            for j in range(2):
                sp.dma_start(mix_out_ring(m)[j], d["mix_out"][layer][j]).then_inc(s["preloaded"], 16)
            sp.wait_ge(s["preloaded"], 48)

        @block.tensor
        def _(pe):
            def score(u):
                b, h = units[u]
                if u >= SB:
                    pe.wait_ge(s["masked"], u - SB + 1)
                nc.tensor.matmul(m.ps[:, score_bank[u % SB], 0:(b + 1) * QB], w.qlat[:, h, b * QB:(b + 1) * QB],
                                 c[:, 0:(b + 1) * QB], start=True, stop=True).then_inc(s["scored"], 1)

            def transpose(u):
                b, h = units[u]
                pe.wait_ge(s["prob_ready"], u + 1)
                if u >= 2:
                    pe.wait_ge(s["probT_ready"], u - 1)
                for k in range(b + 1):
                    last = nc.tensor.transpose(m.ps[:, 2 + u % 2, k * QB:(k + 1) * QB],
                                               w.logits[u % LB][:, k * QB:(k + 1) * QB], m.ident[:, :])
                last.then_inc(s["probT_psum"], 1)

            def attend(u):
                b, h = units[u]
                pe.wait_ge(s["probT_ready"], u + 1)
                if u >= 2:
                    pe.wait_ge(s["out_ready"], u - 1)
                for k in range(b + 1):
                    last = nc.tensor.matmul(m.ps[:, 4 + u % 2, 0:QB], w.c_tok[:, k, :],
                                            w.probT[u % 2][:, k * QB:(k + 1) * QB], start=(k == 0), stop=(k == b))
                last.then_inc(s["out_psum"], 1)

            for u in range(SB):
                score(u)
            for u in range(NU):
                if u and u + SB - 1 < NU:
                    score(u + SB - 1)
                transpose(u)
                if u:
                    attend(u - 1)
            attend(NU - 1)
            pe.wait_ge(s["out_ready"], NU)
            for h in range(H):
                last = nc.tensor.matmul(m.ps[half(h), h // 2, :], w.down[:, h * HD:(h + 1) * HD], w.olat[:, h, :],
                                        start=True, stop=True)
                if h % 2:
                    last.then_inc(s["final_psum"], 1)

        @block.scalar
        def _(act):
            def exponentiate(u):
                b, h = units[u]
                act.wait_ge(s["shift_ready"], u + 1)
                x = w.logits[u % LB][:, 0:(b + 1) * QB]
                nc.scalar.activation(x, x, ACT.Exp, bias=shift[u % LB], accum_out=total[u % LB]).then_inc(
                    s["exp_done"], 1)

            exponentiate(0)
            for u, (b, h) in enumerate(units):
                if u + 1 < NU:
                    exponentiate(u + 1)
                act.wait_ge(s["probT_psum"], u + 1)
                if u >= 2:
                    act.wait_ge(s["out_psum"], u - 1)
                nc.scalar.copy(w.probT[u % 2][:, 0:(b + 1) * QB], m.ps[:, 2 + u % 2, 0:(b + 1) * QB]).then_inc(s["probT_ready"], 1)

        @block.vector
        def _(dve):
            own = Own(dve, s["own"])

            def stabilise(u):
                b, h = units[u]
                n = (b + 1) * QB
                dve.wait_ge(s["scored"], u + 1)
                if u >= LB:
                    dve.wait_ge(s["probT_psum"], u - LB + 1)
                nc.vector.tensor_tensor_reduce(out=w.logits[u % LB][:, 0:n], in0=m.ps[:, score_bank[u % SB], 0:n],
                                               in1=w.mask[b], scale=1.0, scalar=4.0 * NEG, op0=ALU.add, op1=ALU.max,
                                               accum_out=peak[u % LB]).then_inc(s["masked"], 1)

            def negate(u):
                dve.wait_ge(s["masked"], u + 1)
                nc.vector.tensor_scalar(shift[u % LB], peak[u % LB], -1.0, None, ALU.mult).then_inc(s["shift_ready"], 1)

            def keep(u):
                b, h = units[u]
                dve.wait_ge(s["out_psum"], u + 1)
                nc.vector.tensor_copy(w.olat[:, h, b * QB:(b + 1) * QB], m.ps[:, 4 + u % 2, 0:QB]).then_inc(s["out_ready"], 1)

            stabilise(0)
            negate(0)
            for u, (b, h) in enumerate(units):
                if u + 1 < NU:
                    stabilise(u + 1)
                dve.wait_ge(s["exp_done"], u + 1)
                own.then(nc.vector.reciprocal(total[u % LB], total[u % LB]))
                if u + 1 < NU:
                    negate(u + 1)
                own.wait()
                x = w.logits[u % LB][:, 0:(b + 1) * QB]
                nc.vector.tensor_scalar(x, x, total[u % LB], None, ALU.mult).then_inc(s["prob_ready"], 1)
                if u >= 2:
                    keep(u - 2)
            keep(NU - 2)
            keep(NU - 1)
            for n in range(H // 2):
                dve.wait_ge(s["final_psum"], n + 1)
                nc.vector.tensor_copy(m.y[:, 3 + n, 0:SEQ], m.ps[:, n, :]).then_inc(s["final_ready"], 1)


def retention_stage(nc, m, layer, d):
    ring = m.ring[:, :, :].rearrange("p a b -> p (a b)")
    cos, sin, turn = ring[:, 0:SEQ], ring[:, SEQ:2 * SEQ], ring[:, 2 * SEQ:2 * SEQ + P]
    decay = [ring[:, 2 * SEQ + P + h * SEQ:2 * SEQ + P + (h + 1) * SEQ] for h in range(4)]
    z = [m.other[:, 9 + i, :] for i in range(4)]
    q, k = z[0:2], z[2:4]
    g = [m.other[:, 13 + i, :] for i in range(2)]
    half = lambda h: slice(64 * (h % 2), 64 * (h % 2) + 64)
    st = [m.wide[:, i * SEQ:(i + 1) * SEQ] for i in range(4)]
    tmp = [m.wide[:, (4 + i) * SEQ:(5 + i) * SEQ] for i in range(4)]
    yf, sq, root, sg = ([m.work[:, 2 * j + i, 0:SEQ] for i in range(2)] for j in range(4))
    NK = SEQ // P
    units = [(h, j) for h in range(4) for j in range(NK)]
    with stage(nc, f"retain{layer}", "turned_psum", "cosine", "own", "rotated", "scored", "decayed", "y_psum",
               "y_ready", "squared", "ss_psum", "root_ready", "gate_ready", "done") as (block, s):
        @block.gpsimd
        def _(pool):
            pool.wait_ge(s["turned_psum"], 4)
            for i in range(4):
                nc.gpsimd.tensor_tensor(z[i], z[i], cos, ALU.mult).then_inc(s["cosine"], 1)

        @block.tensor
        def _(pe):
            for i in range(4):
                nc.tensor.matmul(m.ps[:, i, :], turn, z[i], start=True, stop=True).then_inc(s["turned_psum"], 1)
            pe.wait_ge(s["rotated"], 4)

            def score(u):
                h, j = units[u]
                if u >= 4:
                    pe.wait_ge(s["decayed"], u - 3)
                n = SEQ - j * P
                nc.tensor.matmul(m.ps[:, u % 4, 0:n], k[h // 2][half(h), j * P:(j + 1) * P], q[h // 2][half(h), j * P:SEQ],
                                 start=True, stop=True).then_inc(s["scored"], 1)

            for u in range(3):
                score(u)
            for u, (h, j) in enumerate(units):
                if u + 3 < len(units):
                    score(u + 3)
                pe.wait_ge(s["decayed"], u + 1)
                n = SEQ - j * P
                last = nc.tensor.matmul(m.ps[half(h), 4 + h // 2, j * P:SEQ], m.ret_v[:, j, h * HD:(h + 1) * HD],
                                        st[u % 4][:, 0:n], start=(j == 0), stop=(j == NK - 1))
                if j == NK - 1 and h % 2:
                    last.then_inc(s["y_psum"], 1)
                else:
                    last.then_inc(s["own"], 1)
            for i in range(2):
                pe.wait_ge(s["squared"], i + 1)
                nc.tensor.matmul(m.ps[:, 6 + i, :], m.head_ones, sq[i], start=True, stop=True).then_inc(s["ss_psum"], 1)

        @block.scalar
        def _(act):
            for i in range(2):
                nc.scalar.activation(sg[i], g[i], ACT.Silu).then_inc(s["gate_ready"], 1)
            for i in range(2):
                act.wait_ge(s["y_psum"], i + 1)
                nc.scalar.copy(yf[i], m.ps[:, 4 + i, :]).then_inc(s["y_ready"], 1)
                act.wait_ge(s["y_ready"], i + 1)
                nc.scalar.activation(sq[i], yf[i], ACT.Square).then_inc(s["squared"], 1)
            for i in range(2):
                act.wait_ge(s["ss_psum"], i + 1)
                nc.scalar.activation(root[i], m.ps[:, 6 + i, :], ACT.Sqrt, scale=1.0 / HD,
                                     bias=m.eps[:, 1:2]).then_inc(s["root_ready"], 1)

        @block.vector
        def _(dve):
            for i in range(4):
                dve.wait_ge(s["turned_psum"], i + 1)
                nc.vector.tensor_tensor(tmp[i], m.ps[:, i, :], sin, ALU.mult).then_inc(s["done"], 1)
                dve.wait_ge(s["cosine"], i + 1)
                dve.wait_ge(s["done"], i + 1)
                nc.vector.tensor_tensor(z[i], z[i], tmp[i], ALU.add).then_inc(s["rotated"], 1)
            for u, (h, j) in enumerate(units):
                n = SEQ - j * P
                dve.wait_ge(s["scored"], u + 1)
                if u >= 4:
                    before = sum(1 for hh, jj in units[:u - 3] if jj == NK - 1 and hh % 2)
                    dve.wait_ge(s["own"], u - 3 - before)
                    if before:
                        dve.wait_ge(s["y_psum"], before)
                nc.vector.tensor_tensor(st[u % 4][:, 0:n], m.ps[:, u % 4, 0:n], decay[h][:, 0:n], ALU.mult).then_inc(
                    s["decayed"], 1)
            n_done = 4
            for i in range(2):
                dve.wait_ge(s["root_ready"], i + 1)
                nc.vector.reciprocal(root[i], root[i]).then_inc(s["done"], 1)
                n_done += 1
                dve.wait_ge(s["done"], n_done)
                nc.vector.tensor_tensor(yf[i], yf[i], root[i], ALU.mult).then_inc(s["done"], 1)
                n_done += 1
                dve.wait_ge(s["done"], n_done)
                dve.wait_ge(s["gate_ready"], i + 1)
                nc.vector.tensor_tensor(m.y[:, 6 + i, 0:SEQ], yf[i], sg[i], ALU.mult).then_inc(s["done"], 1)
                n_done += 1


def part_two(nc, m, d):
    x2 = m.x[:, :, META:T1]
    x_tile = lambda k: m.x[:, k, META:T1]
    y_tile = lambda k: m.y[:, k, 0:SEQ]

    def feed_forward(l, f, w_in, w_out):
        with ExitStack() as ctx:
            ffn_memory(nc, ctx, m, f"s{f}_{l}", S2)
            norm_stage(nc, m, f"norm{f}_{l}", x_tile, lambda k: m.work[:, 3 + k % 2, 0:SEQ], f"ffn{f}_norm{l}", None,
                       RMS_EPS, S2, False, m.xs, first_units(w_in, KT))
            swiglu_stage(nc, m, f"swiglu{f}_{l}", w_in, first_units(w_out, FT2 // 2))
            split_out_stage(nc, m, f"swi_out{f}_{l}", w_out, FT2, m.hs, S2, x2, 0.5, 1.0)

    for l in range(2):
        feed_forward(l, 1, d["swi1_in"][l], d["swi1_out"][l])
        with ExitStack() as ctx:
            projected_memory(nc, ctx, m, f"mix{l}")
            with ExitStack() as inner:
                split_memory(nc, inner, m, f"mix{l}")
                norm_stage(nc, m, f"mix_norm_{l}", x_tile, lambda k: m.work[:, 3 + k % 2, 0:SEQ], f"mix_norm{l}", None,
                           RMS_EPS, S2, False, m.xs, first_units(d["mix_in"][l], KT))
                mix_in_stage(nc, m, l, d)
            mixed_memory(nc, ctx, m, f"mix{l}")
            rwkv_prepare_stage(nc, m, l, d)
            rwkv_recurrence_stage(nc, m, l)
            rwkv_finish_stage(nc, m, l)
            dsa_stage(nc, m, l, d)
            retention_stage(nc, m, l, d)
            out_stage(nc, m, f"mix_out{l}", d["mix_out"][l], KT, P, y_tile, S2, x2, 1.0, 1.0, x2,
                      mix_out_ring(m))
        feed_forward(l, 2, d["swi2_in"][l], d["swi2_out"][l])
    with ExitStack() as ctx:
        ffn_memory(nc, ctx, m, "last", S2)
        norm_stage(nc, m, "final", x_tile, x_tile, "final_norm", None, RMS_EPS, S2, False)


def build(nc, d):
    with ExitStack() as ctx:
        m = Mem(nc, ctx)
        setup_stage(nc, m, d)
        part_one(nc, m, d)
        m.add_part_two(nc, ctx)
        load_masks_stage(nc, m, d)
        part_two(nc, m, d)
        with stage(nc, "store", "stored") as (block, s):
            @block.sync
            def _(sp):
                sp.dma_start(d["out"], m.x[:, :, META:T1]).then_inc(s["stored"], 16)
                sp.wait_ge(s["stored"], 16)


def weight_tiles(w, cols, rows=P):
    k, n = w.shape
    return np.ascontiguousarray(w.reshape(k // rows, rows, n // cols, cols).transpose(2, 1, 0, 3)).reshape(
        n // cols, rows, (k // rows) * cols)


def columns(v, size=P):
    v = np.asarray(v).reshape(-1, size).T
    out = np.zeros((P, v.shape[1]), v.dtype)
    out[:size] = v
    return out


def masks():
    p, f = np.meshgrid(np.arange(P), np.arange(P), indexing="ij")
    same = lambda n: p // n == f // n
    out = [same(64), same(16) & (f < p), same(32) & (p % 32 >= 16) & (f % 32 < 16), same(64) & (p % 64 >= 32) & (f % 64 < 32),
           same(16) & (p < f), same(64) & (p < f), same(64) & (p <= f)]
    return np.concatenate([x.astype(np.float32) for x in out], axis=1)


def retention_constants():
    f32 = np.float32
    theta = f32(10000.0) ** -np.linspace(0.0, 1.0, HD // 2, dtype=f32)
    ang = (np.arange(SEQ, dtype=f32)[None, :] * theta[:, None]).astype(f32)
    ang = np.tile(ang, (4, 1)).astype(np.float64)
    turn = np.zeros((P, P), f32)
    for r in range(P):
        turn[(r + 32 if r % 64 < 32 else r - 32), r] = -1.0 if r % 64 < 32 else 1.0
    key, query = np.meshgrid(np.arange(P), np.arange(SEQ), indexing="ij")
    decay = [np.where(query >= key, np.exp((query - key) * np.log(1.0 - 2.0 ** (-5.0 - h))), 0.0) * SCALE for h in range(4)]
    return np.concatenate([np.cos(ang), np.sin(ang), turn] + decay, axis=1).astype(f32)


def layout(a):
    A = {}
    x = np.concatenate([a["meta"], a["x"][0]], axis=0).T
    A["x"] = np.ascontiguousarray(x.reshape(KT, P, T1).transpose(1, 0, 2))
    vec = np.zeros((P, NCOLS), np.float32)

    def put(name, v, size=P):
        at, n = COLS[name]
        c = columns(v, size)
        assert c.shape[1] == n, name
        vec[:, at:at + n] = c

    for k in range(4):
        put(f"a_conv_w{k}", a["a_conv_w"][0, k], LRU)
    for n in ("a_conv_b", "a_b_r", "a_b_i", "a_lambda"):
        put(n, a[n][0], LRU)
    for l in range(2):
        for k in range(3):
            put(f"f_conv_w{l}_{k}", a["f_conv_w"][l, k])
        put(f"f_conv_b{l}", a["f_conv_b"][l])
        for n in ("ln1_g", "ln1_b", "ln2_g", "ln2_b"):
            put(f"{n}{l}", a[n][l])
    put("kv_f_b", a["kv_f_b"], HEADS1)
    for l in range(2):
        for n in ("ffn1_norm", "mix_norm", "ffn2_norm"):
            put(f"{n}{l}", a[f"{n}_2"][l])
        put(f"rwkv_mu{l}", a["rwkv_mu_2"][l])
        for n in ("w0", "a0", "k_k", "k_a", "r_k", "ln_w", "ln_b"):
            put(f"rwkv_{n}{l}", a[f"rwkv_{n}_2"][l].reshape(-1))
        put(f"dsa_kv_norm{l}", a["dsa_kv_norm_2"][l])
    put("rwkv_v0", a["rwkv_v0_2"][0])
    vec[32:48, COLS["rwkv_vres_mu"][0]] = a["rwkv_vres_mu_2"][0]
    put("final_norm", a["final_norm_2"])
    A["vectors"] = vec
    A["masks"] = masks()
    A["ret_const"] = retention_constants()
    for l in range(2):
        for f in (1, 2):
            pad = lambda w: np.concatenate([w, np.zeros((w.shape[0], FT2 * P - w.shape[1]), w.dtype)], axis=1)
            g, u = a[f"ffn{f}_w_gate_2"][l], a[f"ffn{f}_w_up_2"][l]
            A[f"swi{f}_in{l}"] = np.concatenate([weight_tiles(pad(g), P), weight_tiles(pad(u), P)], axis=2)
            A[f"swi{f}_out{l}"] = weight_tiles(pad(a[f"ffn{f}_w_down_2"][l].T).T, P)
        w = a["w_in_2"][l]
        q, c, iq, ik, iw = np.split(w[:, 1280:2376], np.cumsum([384, 128, 512, 64]), axis=1)
        rq, rk, rv, rg = np.split(w[:, 2376:], 4, axis=1)
        last = np.zeros((D, P), w.dtype)
        last[:, 0:8] = iw
        if l == 1:
            last[:, 32:48] = a["rwkv_vres_w_in_2"][0]
        tiles = weight_tiles(np.concatenate([q, c, iq, ik, ik, rq, rk, rg, last, rv, w[:, :1280]], axis=1), P)
        A[f"mix_in{l}"] = np.concatenate([tiles[0::2], tiles[1::2]], axis=2)
        lo = np.zeros((P, 768), w.dtype)
        lo[0:32, 0:384], lo[32:64, 0:384], lo[64:128, 0:384] = a["rwkv_w2_2"][l], a["rwkv_a2_2"][l], a["rwkv_g2_2"][l]
        lo[32:48, 384:768] = a["rwkv_v2_2"][0]
        A[f"rwkv_lo{l}"] = lo
        A[f"dsa_w{l}"] = np.concatenate([a["dsa_w_uk_2"][l].reshape(3, P, P).transpose(1, 0, 2).reshape(P, 384),
                                         a["dsa_w_uv_2"][l].transpose(1, 0, 2).reshape(P, 384)], axis=1)
        A[f"mix_out{l}"] = weight_tiles(a["w_out_2"][l], P)
    win = a["a_w_in"][0]
    g, r = weight_tiles(win[:, :D_RNN], LRU), weight_tiles(win[:, D_RNN:], LRU)
    small = np.zeros((N_LRU, P, 2 * LRU), np.float32)
    small[:, :LRU, :LRU] = a["a_w_r"][0]
    small[:, :LRU, LRU:] = a["a_w_i"][0]
    kv, qg = a["kv_w"], a["b_w_in"][0]
    A["attn_w"] = np.concatenate([weight_tiles(qg[:, :D], P), weight_tiles(kv[:, :D], P),
                                  weight_tiles(kv[:, D:2 * D], P), weight_tiles(qg[:, D:], P)], axis=2)
    A["forget_w"] = weight_tiles(kv[:, 2 * D:], HEADS1)[0]
    A["attn_out"] = weight_tiles(a["b_w_out"][0], P)
    A["lru_w"] = np.concatenate([g, r, small], axis=2)
    A["lru_out"] = weight_tiles(a["a_w_out"][0], P, LRU)
    for l in range(2):
        w = a["f_w_in"][l]
        A[f"ffn_in{l}"] = np.concatenate([weight_tiles(w[:, :D_FF], P), weight_tiles(w[:, D_FF:], P)], axis=2)
        A[f"ffn_out{l}"] = weight_tiles(a["f_w_out"][l], P)
    return A


def program(nc, shapes):
    aps, groups = {}, {}
    for name, shape in shapes.items():
        ap = nc.dram_tensor(f"in_{name}", shape, FP32, kind="ExternalInput").ap()
        if name[-1] in "01":
            groups.setdefault(name[:-1], {})[int(name[-1])] = ap
        else:
            aps[name] = ap
    out = nc.dram_tensor("out_tokens", (P, KT, SEQ), FP32, kind="ExternalOutput").ap()
    d = {"out": out, **aps, **groups}
    build(nc, d)


def kernel(**inputs):
    import concourse.bacc as bacc
    from concourse.bass_utils import run_bass_kernel_spmd

    a = {k: np.asarray(v) for k, v in inputs.items()}
    arrays = layout(a)
    nc = bacc.Bacc("TRN2", target_bir_lowering=False, num_devices=1)
    program(nc, {k: v.shape for k, v in arrays.items()})
    r = run_bass_kernel_spmd(nc, [{f"in_{k}": v for k, v in arrays.items()}], core_ids=[0])
    out = r.results[0]["out_tokens"]
    return np.ascontiguousarray(out.transpose(2, 1, 0)).reshape(1, SEQ, D)
```
